# Optimizing a Trainium2 kernel written in Bass

```python
import math
import jax, jax.numpy as jnp
from jax import lax
import numpy as np

D_MODEL = 2048
BATCH = 1
SEQ = 256
DEPTH = 1

MEM_LEN = 256
NORM_EPS = 1e-6

DA_HEADS = 8
DA_QK_DIM = 64
DA_V_DIM = 2 * DA_QK_DIM
DA_WIDTH = DA_HEADS * DA_V_DIM
Q_BLOCK = 128

HG_HEADS = 8
HG_DK = 128
HG_DV = 128
HG_WIDTH = HG_HEADS * HG_DV
HG_CHUNK = 64

MIX_WIDTH = DA_WIDTH + HG_WIDTH

DA_Q_COLS = DA_HEADS * 2 * DA_QK_DIM
DA_K_COLS = DA_HEADS * 2 * DA_QK_DIM
DA_V_COLS = DA_WIDTH
HG_KEY_COLS = HG_HEADS * HG_DK
HG_VAL_COLS = HG_HEADS * HG_DV
IN_SIZES = (DA_Q_COLS, DA_K_COLS, DA_V_COLS, HG_KEY_COLS, HG_KEY_COLS, HG_VAL_COLS, HG_VAL_COLS)
IN_COLS = sum(IN_SIZES)
IN_SPLITS = tuple(int(v) for v in np.cumsum(IN_SIZES)[:-1])

REL_BUCKETS = 32
REL_MAX_DIST = 128

CX_HEADS = 4
CX_HEAD_DIM = 128
CX_WIDTH = CX_HEADS * CX_HEAD_DIM

FFN_HIDDEN = ((8 * D_MODEL // 3 + 255) // 256) * 256


def rms_norm(x, g):
    xf = x.astype(jnp.float32)
    y = xf * lax.rsqrt(jnp.mean(xf * xf, axis=-1, keepdims=True) + NORM_EPS)
    return (y * g.astype(jnp.float32)).astype(x.dtype)

def t5_causal_bucket(dist):
    n = jnp.maximum(dist, 0)
    max_exact = REL_BUCKETS // 2
    nf = jnp.maximum(n, 1).astype(jnp.float32)
    large = max_exact + (jnp.log(nf / max_exact) / math.log(REL_MAX_DIST / max_exact)
                         * (REL_BUCKETS - max_exact)).astype(jnp.int32)
    large = jnp.minimum(large, REL_BUCKETS - 1)
    return jnp.where(n < max_exact, n, large)

def differential_attention(q, k, v, lam, lam_init, subln_g, rel_bias):
    B, S = q.shape[0], q.shape[1]
    n_blk = S // Q_BLOCK
    scale = DA_QK_DIM ** -0.5
    kt = jnp.transpose(k, (0, 2, 3, 1, 4))
    vt = jnp.transpose(v, (0, 2, 1, 3))
    qb = q.reshape(B, n_blk, Q_BLOCK, DA_HEADS, 2, DA_QK_DIM).transpose(1, 0, 3, 4, 2, 5)
    k_pos = jnp.arange(S)

    def block(args):
        q_blk, blk = args
        q_pos = blk * Q_BLOCK + jnp.arange(Q_BLOCK)
        dist = q_pos[:, None] - k_pos[None, :]
        bias = jnp.transpose(rel_bias[t5_causal_bucket(dist)], (2, 0, 1)).astype(jnp.float32)
        s = jnp.einsum('bhmqd,bhmkd->bhmqk', q_blk, kt).astype(jnp.float32) * scale + bias[None, :, None]
        s = jnp.where(dist >= 0, s, -jnp.inf)
        p = jax.nn.softmax(s, axis=-1)
        a = p[:, :, 0] - lam * p[:, :, 1]
        return jnp.einsum('bhqk,bhkd->bhqd', a.astype(vt.dtype), vt)

    o = lax.map(block, (qb, jnp.arange(n_blk)))
    o = rms_norm(o, subln_g) * (1.0 - lam_init)
    return o.transpose(1, 0, 3, 2, 4).reshape(B, S, DA_WIDTH)

def hgrn2(f_logit, q, i, g, lb, onorm_g):
    B, S = q.shape[0], q.shape[1]
    n_chunk = S // HG_CHUNK
    f = lb.astype(jnp.float32) + (1.0 - lb.astype(jnp.float32)) * jax.nn.sigmoid(f_logit.astype(jnp.float32))
    log_f = jnp.log(f)
    k = 1.0 - f

    def to_chunks(t, d):
        return t.astype(jnp.float32).reshape(B, n_chunk, HG_CHUNK, HG_HEADS, d).transpose(1, 0, 3, 2, 4)

    qc, kc, vc, gc = to_chunks(q, HG_DK), to_chunks(k, HG_DK), to_chunks(i, HG_DV), to_chunks(log_f, HG_DK)
    causal = jnp.tril(jnp.ones((HG_CHUNK, HG_CHUNK), dtype=bool))

    def step(state, inp):
        qt, kt, vt, gt = inp
        b = jnp.cumsum(gt, axis=2)
        diff = b[:, :, :, None, :] - b[:, :, None, :, :]
        decay = jnp.exp(jnp.where(causal[:, :, None], diff, -jnp.inf))
        attn = jnp.einsum('bhtc,bhsc,bhtsc->bhts', qt, kt, decay)
        o = (jnp.einsum('bhts,bhsv->bhtv', attn, vt)
             + jnp.einsum('bhtc,bhcv->bhtv', qt * jnp.exp(b), state))
        b_last = b[:, :, -1:, :]
        state = (jnp.exp(b_last[:, :, 0, :])[..., None] * state
                 + jnp.einsum('bhsc,bhsv->bhcv', kt * jnp.exp(b_last - b), vt))
        return state, o

    state0 = jnp.zeros((B, HG_HEADS, HG_DK, HG_DV), jnp.float32)
    _, outs = lax.scan(step, state0, (qc, kc, vc, gc))
    o = outs.transpose(1, 0, 3, 2, 4).reshape(B, S, HG_HEADS, HG_DV).astype(q.dtype)
    o = rms_norm(o, onorm_g) * jax.nn.silu(g.reshape(B, S, HG_HEADS, HG_DV))
    return o.reshape(B, S, HG_WIDTH)

def first_inputs(seed: int = 0) -> dict:
    key = jax.random.key(seed)
    ks = jax.random.split(key, 24)

    def w(k, shape, fan_in):
        return jax.random.normal(k, shape, jnp.float32) * fan_in ** -0.5

    def gain(k, shape):
        return 1.0 + 0.02 * jax.random.normal(k, shape, jnp.float32)

    return {
        "x": jax.random.normal(ks[0], (BATCH, SEQ, D_MODEL), jnp.float32),
        "mem": jax.random.normal(ks[1], (BATCH, MEM_LEN, D_MODEL), jnp.float32),
        "w_in": w(ks[2], (DEPTH, D_MODEL, IN_COLS), D_MODEL),
        "w_out": w(ks[3], (DEPTH, MIX_WIDTH, D_MODEL), MIX_WIDTH),
        "w_cq": w(ks[4], (DEPTH, D_MODEL, CX_WIDTH), D_MODEL),
        "w_ckv": w(ks[5], (DEPTH, D_MODEL, 2 * CX_WIDTH), D_MODEL),
        "w_co": w(ks[6], (DEPTH, CX_WIDTH, D_MODEL), CX_WIDTH),
        "w_ffn_in": w(ks[7], (DEPTH, D_MODEL, 2 * FFN_HIDDEN), D_MODEL),
        "w_ffn_out": w(ks[8], (DEPTH, FFN_HIDDEN, D_MODEL), FFN_HIDDEN),
        "mix_pre_g": gain(ks[9], (DEPTH, D_MODEL)),
        "mix_post_g": gain(ks[10], (DEPTH, D_MODEL)),
        "cross_pre_g": gain(ks[11], (DEPTH, D_MODEL)),
        "cross_post_g": gain(ks[12], (DEPTH, D_MODEL)),
        "mem_norm_g": gain(ks[13], (DEPTH, D_MODEL)),
        "ffn_pre_g": gain(ks[14], (DEPTH, D_MODEL)),
        "ffn_post_g": gain(ks[15], (DEPTH, D_MODEL)),
        "da_subln_g": gain(ks[16], (DEPTH, DA_V_DIM)),
        "hg_onorm_g": gain(ks[17], (DEPTH, HG_DV)),
        "lambda_q1": 0.1 * jax.random.normal(ks[18], (DEPTH, DA_QK_DIM), jnp.float32),
        "lambda_k1": 0.1 * jax.random.normal(ks[19], (DEPTH, DA_QK_DIM), jnp.float32),
        "lambda_q2": 0.1 * jax.random.normal(ks[20], (DEPTH, DA_QK_DIM), jnp.float32),
        "lambda_k2": 0.1 * jax.random.normal(ks[21], (DEPTH, DA_QK_DIM), jnp.float32),
        "hg_lb_logits": 0.5 * jax.random.normal(ks[22], (DEPTH, HG_KEY_COLS), jnp.float32),
        "rel_bias": 0.1 * jax.random.normal(ks[23], (REL_BUCKETS, DA_HEADS), jnp.float32),
    }

def first_block(x, mem, w_in, w_out, w_cq, w_ckv, w_co, w_ffn_in, w_ffn_out,
              mix_pre_g, mix_post_g, cross_pre_g, cross_post_g, mem_norm_g,
              ffn_pre_g, ffn_post_g, da_subln_g, hg_onorm_g,
              lambda_q1, lambda_k1, lambda_q2, lambda_k2, hg_lb_logits, rel_bias):
    B, S = x.shape[0], x.shape[1]
    M = mem.shape[1]
    lb_p = jax.nn.softmax(hg_lb_logits.astype(jnp.float32), axis=0)
    lower_bounds = jnp.cumsum(lb_p, axis=0) - lb_p[0:1]

    for l in range(DEPTH):
        h = rms_norm(x, mix_pre_g[l])
        proj = h @ w_in[l]
        q_da, k_da, v_da, f_hg, q_hg, i_hg, g_hg = jnp.split(proj, IN_SPLITS, axis=-1)

        lam_init = 0.8 - 0.6 * math.exp(-0.3 * l)
        lam = (jnp.exp(jnp.sum(lambda_q1[l].astype(jnp.float32) * lambda_k1[l].astype(jnp.float32)))
               - jnp.exp(jnp.sum(lambda_q2[l].astype(jnp.float32) * lambda_k2[l].astype(jnp.float32)))
               + lam_init)
        o_da = differential_attention(
            q_da.reshape(B, S, DA_HEADS, 2, DA_QK_DIM),
            k_da.reshape(B, S, DA_HEADS, 2, DA_QK_DIM),
            v_da.reshape(B, S, DA_HEADS, DA_V_DIM),
            lam, lam_init, da_subln_g[l], rel_bias)
        o_hg = hgrn2(f_hg, q_hg, i_hg, g_hg, lower_bounds[l], hg_onorm_g[l])
        mixed = jnp.concatenate([o_da, o_hg], axis=-1) @ w_out[l]
        x = x + rms_norm(mixed, mix_post_g[l])

        h = rms_norm(x, cross_pre_g[l])
        m = rms_norm(mem, mem_norm_g[l])
        qx = (h @ w_cq[l]).reshape(B, S, CX_HEADS, CX_HEAD_DIM)
        kv = (m @ w_ckv[l]).reshape(B, M, 2, CX_HEADS, CX_HEAD_DIM)
        s = jnp.einsum('bqhd,bkhd->bhqk', qx, kv[:, :, 0]).astype(jnp.float32) * CX_HEAD_DIM ** -0.5
        p = jax.nn.softmax(s, axis=-1)
        o = jnp.einsum('bhqk,bkhd->bqhd', p.astype(x.dtype), kv[:, :, 1]).reshape(B, S, CX_WIDTH)
        x = x + rms_norm(o @ w_co[l], cross_post_g[l])

        h = rms_norm(x, ffn_pre_g[l])
        gate, up = jnp.split(h @ w_ffn_in[l], 2, axis=-1)
        x = x + rms_norm((jax.nn.silu(gate) * up) @ w_ffn_out[l], ffn_post_g[l])

    return x


POOL_WINDOWS = (2, 4, 8, 16)
POOL_GROUPS = 4
POOL_WIDTH = D_MODEL // 2
POOL_GROUP_DIM = POOL_WIDTH // POOL_GROUPS
GLA_HEADS = 4
GLA_KEY_DIM = D_MODEL // 2
GLA_VALUE_DIM = D_MODEL
GLA_HEAD_K = GLA_KEY_DIM // GLA_HEADS
GLA_HEAD_V = GLA_VALUE_DIM // GLA_HEADS
GLA_GATE_RANK = 16
GLA_GATE_TAU = 16.0
GLA_CHUNK = 64
D_FF = -(-8 * D_MODEL // (3 * 256)) * 256
N_BRANCHES = 2
EPS = 1e-6
IN_SIZES_2 = (POOL_WIDTH, GLA_KEY_DIM, GLA_KEY_DIM, GLA_VALUE_DIM, GLA_GATE_RANK, GLA_VALUE_DIM, N_BRANCHES * D_MODEL)
D_IN = sum(IN_SIZES_2)


def rms_norm_2(x, g):
    xf = x.astype(jnp.float32)
    y = xf * lax.rsqrt(jnp.mean(xf * xf, axis=-1, keepdims=True) + EPS)
    return (y * g.astype(jnp.float32)).astype(x.dtype)

def split_combined(z):
    idx = [int(i) for i in np.cumsum(IN_SIZES_2)[:-1]]
    return jnp.split(z, idx, axis=-1)

def pool_mixer(p, w_pool, pool_scale):
    B, T, _ = p.shape
    pg = p.reshape(B, T, POOL_GROUPS, POOL_GROUP_DIM).astype(jnp.float32)
    cs = jnp.concatenate([jnp.zeros((B, 1, POOL_GROUPS, POOL_GROUP_DIM), jnp.float32),
                          jnp.cumsum(pg, axis=1)], axis=1)
    pos = jnp.arange(T)
    outs = []
    for g, w in enumerate(POOL_WINDOWS):
        c = cs[:, :, g]
        lo = jnp.maximum(pos + 1 - w, 0)
        win_sum = c[:, 1:] - jnp.take(c, lo, axis=1)
        count = (pos + 1 - lo).astype(jnp.float32)
        outs.append(win_sum / count[None, :, None] - pg[:, :, g])
    d = jnp.stack(outs, axis=2).astype(p.dtype)
    y = jnp.einsum('btgc,gcd->btgd', d, w_pool).reshape(B, T, POOL_WIDTH)
    return y * pool_scale

def gla_chunked(q, k, v, log_a):
    B, T, H, dk = q.shape
    dv = v.shape[-1]
    nC = T // GLA_CHUNK
    C = GLA_CHUNK

    def chunks(t):
        return t.astype(jnp.float32).reshape(B, nC, C, H, t.shape[-1]).transpose(1, 0, 3, 2, 4)

    qc = chunks(q) * (dk ** -0.5)
    kc, vc = chunks(k), chunks(v)
    Gc = jnp.cumsum(chunks(log_a), axis=3)
    mask = jnp.tril(jnp.ones((C, C), dtype=bool))

    def step(S, inp):
        qi, ki, vi, Gi = inp
        o_inter = jnp.einsum('bhik,bhkv->bhiv', qi * jnp.exp(Gi), S)
        diff = Gi[:, :, :, None, :] - Gi[:, :, None, :, :]
        decay = jnp.exp(jnp.where(mask[:, :, None], diff, -jnp.inf))
        A = jnp.einsum('bhik,bhjk,bhijk->bhij', qi, ki, decay)
        o_intra = jnp.einsum('bhij,bhjv->bhiv', A, vi)
        G_last = Gi[:, :, -1]
        k_dec = ki * jnp.exp(G_last[:, :, None] - Gi)
        S_new = jnp.exp(G_last)[..., None] * S + jnp.einsum('bhjk,bhjv->bhkv', k_dec, vi)
        return S_new, o_inter + o_intra

    S0 = jnp.zeros((B, H, dk, dv), jnp.float32)
    _, o = lax.scan(step, S0, (qc, kc, vc, Gc))
    return o.transpose(1, 0, 3, 2, 4).reshape(B, T, H, dv).astype(v.dtype)

def second_inputs(seed: int = 0) -> dict:
    key = jax.random.key(seed)
    ks = jax.random.split(key, 20)
    f32 = jnp.float32
    L = DEPTH

    def nrm(k, shape, fan_in):
        return jax.random.normal(k, shape, f32) * (fan_in ** -0.5)

    def gain(k, shape):
        return 1.0 + 0.05 * jax.random.normal(k, shape, f32)

    return {
        "x": jax.random.normal(ks[0], (BATCH, SEQ, D_MODEL), f32),
        "norm_mix_pre": gain(ks[1], (L, D_MODEL)),
        "w_in": nrm(ks[2], (L, D_MODEL, D_IN), D_MODEL),
        "w_gate_up": nrm(ks[3], (L, GLA_GATE_RANK, GLA_KEY_DIM), GLA_GATE_RANK),
        "b_gate": 0.1 * jax.random.normal(ks[4], (L, GLA_KEY_DIM), f32),
        "w_pool": nrm(ks[5], (L, POOL_GROUPS, POOL_GROUP_DIM, POOL_GROUP_DIM), POOL_GROUP_DIM),
        "pool_scale": gain(ks[6], (L, POOL_WIDTH)),
        "gla_norm": gain(ks[7], (L, GLA_HEAD_V)),
        "w_branch_a": nrm(ks[8], (L, POOL_WIDTH, D_MODEL), POOL_WIDTH),
        "w_branch_b": nrm(ks[9], (L, GLA_VALUE_DIM, D_MODEL), GLA_VALUE_DIM),
        "b_branch_gates": 0.01 * jax.random.normal(ks[10], (L, N_BRANCHES, D_MODEL), f32),
        "w_out": nrm(ks[11], (L, D_MODEL, D_MODEL), D_MODEL),
        "norm_mix_post": gain(ks[12], (L, D_MODEL)),
        "norm_ffn_pre": gain(ks[13], (L, D_MODEL)),
        "w_ffn_gate": nrm(ks[14], (L, D_MODEL, D_FF), D_MODEL),
        "w_ffn_up": nrm(ks[15], (L, D_MODEL, D_FF), D_MODEL),
        "w_ffn_down": nrm(ks[16], (L, D_FF, D_MODEL), D_FF),
        "norm_ffn_post": gain(ks[17], (L, D_MODEL)),
    }

def second_block(x, norm_mix_pre, w_in, w_gate_up, b_gate, w_pool, pool_scale, gla_norm,
              w_branch_a, w_branch_b, b_branch_gates, w_out, norm_mix_post,
              norm_ffn_pre, w_ffn_gate, w_ffn_up, w_ffn_down, norm_ffn_post):
    B, T, _ = x.shape
    for l in range(DEPTH):
        h = rms_norm_2(x, norm_mix_pre[l])
        z = h @ w_in[l]
        p, q, k, v, g_lr, r, gate_logits = split_combined(z)
        y_a = pool_mixer(p, w_pool[l], pool_scale[l]) @ w_branch_a[l]
        log_a = jax.nn.log_sigmoid((g_lr @ w_gate_up[l] + b_gate[l]).astype(jnp.float32)) / GLA_GATE_TAU
        o = gla_chunked(q.reshape(B, T, GLA_HEADS, GLA_HEAD_K),
                        k.reshape(B, T, GLA_HEADS, GLA_HEAD_K),
                        v.reshape(B, T, GLA_HEADS, GLA_HEAD_V),
                        log_a.reshape(B, T, GLA_HEADS, GLA_HEAD_K))
        o = rms_norm_2(o, gla_norm[l]).reshape(B, T, GLA_VALUE_DIM) * jax.nn.silu(r)
        y_b = o @ w_branch_b[l]
        gates = jax.nn.sigmoid(gate_logits.reshape(B, T, N_BRANCHES, D_MODEL) + b_branch_gates[l])
        mixed = (gates[:, :, 0] * y_a + gates[:, :, 1] * y_b) @ w_out[l]
        x = x + rms_norm_2(mixed, norm_mix_post[l])
        h = rms_norm_2(x, norm_ffn_pre[l])
        f = (jax.nn.silu(h @ w_ffn_gate[l]) * (h @ w_ffn_up[l])) @ w_ffn_down[l]
        x = x + rms_norm_2(f, norm_ffn_post[l])
    return x


def setup_inputs(seed=0):
    out = dict(first_inputs(seed))
    for name, value in second_inputs(seed + 1).items():
        if name != "x":
            out[name + "_2"] = value
    return out


def reference(
    x, mem, w_in, w_out, w_cq, w_ckv, w_co, w_ffn_in, w_ffn_out, mix_pre_g, mix_post_g,
    cross_pre_g, cross_post_g, mem_norm_g, ffn_pre_g, ffn_post_g, da_subln_g, hg_onorm_g,
    lambda_q1, lambda_k1, lambda_q2, lambda_k2, hg_lb_logits, rel_bias, norm_mix_pre_2, w_in_2,
    w_gate_up_2, b_gate_2, w_pool_2, pool_scale_2, gla_norm_2, w_branch_a_2, w_branch_b_2,
    b_branch_gates_2, w_out_2, norm_mix_post_2, norm_ffn_pre_2, w_ffn_gate_2, w_ffn_up_2,
    w_ffn_down_2, norm_ffn_post_2,
):
    x = first_block(
        x, mem, w_in, w_out, w_cq, w_ckv, w_co, w_ffn_in, w_ffn_out, mix_pre_g, mix_post_g,
        cross_pre_g, cross_post_g, mem_norm_g, ffn_pre_g, ffn_post_g, da_subln_g, hg_onorm_g,
        lambda_q1, lambda_k1, lambda_q2, lambda_k2, hg_lb_logits, rel_bias,
    )
    return second_block(
        x, norm_mix_pre_2, w_in_2, w_gate_up_2, b_gate_2, w_pool_2, pool_scale_2, gla_norm_2,
        w_branch_a_2, w_branch_b_2, b_branch_gates_2, w_out_2, norm_mix_post_2, norm_ffn_pre_2,
        w_ffn_gate_2, w_ffn_up_2, w_ffn_down_2, norm_ffn_post_2,
    )


_drawn_inputs = setup_inputs


def setup_inputs(seed=0):
    import zlib

    import numpy as np

    out = dict(_drawn_inputs(seed))
    spreads = {}
    factors = {'mix_post_g': 2.951,
     'cross_pre_g': 3.73,
     'cross_post_g': 10.401,
     'ffn_pre_g': 3.147,
     'ffn_post_g': 44.586,
     'da_subln_g': 3.522,
     'hg_onorm_g': 5.03,
     'b_gate_2': 11.634,
     'pool_scale_2': 125.068,
     'gla_norm_2': 154.625,
     'b_branch_gates_2': 64.0,
     'norm_ffn_post_2': 25.089,
     'norm_mix_pre_2': 4.238,
     'w_gate_up_2': 3.65,
     'norm_mix_post_2': 21.239}
    for name, (base, spread) in spreads.items():
        noise = np.random.default_rng([zlib.crc32(name.encode()), seed]).standard_normal(out[name].shape)
        drawn = base * np.exp(spread * noise) if base else spread * noise
        out[name] = __import__('jax').numpy.asarray(drawn.astype(out[name].dtype))
    for name, factor in factors.items():
        out[name] = (out[name] * factor).astype(out[name].dtype)
    return out
```

```python
from contextlib import ExitStack

import numpy as np

import concourse.bass as bass
from concourse import mybir

F32 = mybir.dt.float32
F32R = mybir.dt.float32r
U8 = mybir.dt.uint8
ACT = mybir.ActivationFunctionType
ALU = mybir.AluOpType
AXX = mybir.AxisListType.X
P = 128
D = 2048
T = 256
FF = 5632
EPS = 1e-6

GAINS = ["mix_pre_g", "cross_pre_g", "mem_norm_g", "ffn_pre_g", "norm_mix_pre_2", "norm_ffn_pre_2",
         "b_gate_2", "pool_scale_2", "b_branch_gates_2", "hg_lb_logits", "da_subln_g", "hg_onorm_g", "gla_norm_2"]
GCOLS = [16, 16, 16, 16, 16, 16, 8, 8, 32, 8, 1, 1, 4]
GOFF = {n: sum(GCOLS[:i]) for i, n in enumerate(GAINS)}
NGC = sum(GCOLS)
LEVELS = [1, 2, 4, 8, 16, 32, 64]


def shape_constants():
    i = np.arange(P)
    ident = np.eye(P, dtype=np.float32)
    flip = np.ascontiguousarray(ident[::-1])
    m = np.arange(384)
    dist = np.maximum(255 - m, 0)
    nf = np.maximum(dist, 1).astype(np.float32)
    large = 16 + (np.log(nf / np.float32(16)) / np.float32(np.log(8.0)) * np.float32(16)).astype(np.int32)
    bucket = np.where(dist < 16, dist, np.minimum(large, 31))
    onehot = ((bucket[None, :] == np.arange(32)[:, None]) & (m[None, :] <= 255)).astype(np.float32)
    dead = np.broadcast_to(np.where(m > 255, -1e30, 0.0).astype(np.float32), (8, 384))
    masks = [i[:, None] == i[None, :]]
    for L in LEVELS:
        s, t = i[:, None], i[None, :]
        masks.append((s // (2 * L) == t // (2 * L)) & (s % (2 * L) < L) & (t % (2 * L) >= L))
    masks = np.stack(masks, 1).astype(np.float32)
    counts = np.stack([1.0 / np.minimum(np.arange(16) + 1, w) for w in (2, 4, 8, 16)])
    counts = np.broadcast_to(counts.astype(np.float32).reshape(1, 64), (P, 64))
    return {"c_eye": np.concatenate([ident, flip, counts], 1).astype(np.float32),
            "c_hot": np.ascontiguousarray(onehot), "c_dead": np.ascontiguousarray(dead),
            "c_mask": np.ascontiguousarray(masks.reshape(P, 8 * P))}


class Queues:

    def __init__(self, nc, ctx):
        self.nc, self.ctx = nc, ctx
        self.q = {e: [] for e in ("pe", "act", "dve", "pool", "sp")}
        self.sem = {e: ctx.enter_context(nc.semaphore("s_" + e)) for e in ("pe", "act", "dve", "pool")}
        self.n = {e: 0 for e in self.sem}
        self.told = {e: {} for e in self.q}

    def wait(self, e, after):
        need = {}
        for t in after:
            if isinstance(t, list):
                for u in t:
                    need[u[0]] = max(need.get(u[0], 0), u[1])
            elif t is not None:
                need[t[0]] = max(need.get(t[0], 0), t[1])
        for k, v in need.items():
            if self.told[e].get(k, 0) < v:
                self.told[e][k] = v
                self.q[e].append(("wait", k, v))

    def op(self, e, fn, after=(), inc=True):
        self.wait(e, after)
        if inc:
            self.n[e] += 1
        self.q[e].append(("op", fn, inc))
        return (e, self.n[e]) if inc else None

    def dma(self, e, name, out, in_, after=()):
        if name not in self.sem:
            self.sem[name] = self.ctx.enter_context(self.nc.semaphore("d_" + name))
            self.n[name] = 0
        self.wait(e, after)
        self.n[name] += 16
        self.q[e].append(("dma", lambda g: g.dma_start(out, in_), name))
        return (name, self.n[name])

    def play(self, e, g):
        for it in self.q[e]:
            if it[0] == "wait":
                g.wait_ge(self.sem[it[1]], it[2])
            elif it[0] == "dma":
                it[1](g).then_inc(self.sem[it[2]], 16)
            else:
                i = it[1](g)
                if it[2]:
                    i.then_inc(self.sem[e], 1)


def build(nc, A, out, scratch):
    ctx = ExitStack()
    with ctx:
        Q = Queues(nc, ctx)

        def sb(name, shape, dt=F32):
            return ctx.enter_context(nc.sbuf_tensor(name, shape, dt))

        NR, NH = 3, 4
        LA = NH - 1
        RAW = sb("RAW", [P, NR, 1024])
        RH = sb("RH", [P, NH, 1024], F32R)
        RL = sb("RL", [P, NH, 1024], F32R)
        AH, AL = sb("AH", [P, 16, T], F32R), sb("AL", [P, 16, T], F32R)
        BH, BL = sb("BH", [P, 16, T], F32R), sb("BL", [P, 16, T], F32R)
        X = sb("X", [P, 2, D])
        AR = sb("AR", [P, 9 * 2048])
        SP4 = sb("SP4", [P, 1024])
        EYE = sb("EYE", [P, 320])
        MASK = sb("MASK", [P, 8, P], U8)
        GC = sb("GC", [P, NGC])
        ST = sb("ST", [P, 448])
        SM = sb("SM", [P, 512])
        GL = sb("GL", [P, 32 + T])
        PS = ctx.enter_context(nc.psum_tensor("PS", [P, 8, 512], F32))
        ident, flip = EYE[:, 0:P], EYE[:, P:2 * P]

        def U(k, n=1):
            return AR[:, k * 2048:(k + n) * 2048]

        def gcol(name, c=0):
            return GC[:, GOFF[name] + c:GOFF[name] + c + 1]

        used = [0]

        def stat(n):
            used[0] += n
            assert used[0] <= 448
            return ST[:, used[0] - n:used[0]]

        def act(o, i, f=ACT.Copy, scale=1.0, bias=0.0, accum=None, after=()):
            return Q.op("act", lambda g: g.activation(o, i, f, bias=bias, scale=scale, accum_out=accum), after)

        def tt(o, a, b, f, after=(), e="dve"):
            return Q.op(e, lambda g: g.tensor_tensor(o, a, b, f), after)

        def ts(o, a, s1, s2, f0, f1=None, after=(), e="dve"):
            if f1 is None:
                return Q.op(e, lambda g: g.tensor_scalar(o, a, s1, None, f0), after)
            return Q.op(e, lambda g: g.tensor_scalar(o, a, s1, s2, f0, f1), after)

        def stt(o, a, s, b, f0, f1, after=()):
            return Q.op("dve", lambda g: g.scalar_tensor_tensor(o, a, s, b, f0, f1), after)

        def red(o, i, f, after=(), negate=False):
            return Q.op("dve", lambda g: g.tensor_reduce(o, i, AXX, f, negate=negate), after)

        def cp(o, i, after=(), e="dve"):
            return Q.op(e, lambda g: g.tensor_copy(o, i), after)

        def mm(o, l, r, start, stop, after=(), inc=False):
            return Q.op("pe", lambda g: g.matmul(o, l, r, start=start, stop=stop, skip_group_check=True), after, inc)

        def tr(o, i, after=(), inc=False):
            return Q.op("pe", lambda g: g.transpose(o, i, ident), after, inc)

        def split(src, h, l, scale=None, after=()):
            if scale is None:
                t = act(h, src, after=after)
                return tt(l, src, h.bitcast(F32), ALU.subtract, [t])
            t = act(h, src, scale=scale, after=after)
            return stt(l, src, scale, h.bitcast(F32), ALU.mult, ALU.subtract, [t])

        def splits(parts, after=()):
            for src, h, l, scale in parts:
                t = act(h, src, scale=scale, after=after)
            for src, h, l, scale in parts:
                u = stt(l, src, scale, h.bitcast(F32), ALU.mult, ALU.subtract, [t])
            return u

        def rsqrt(ss, n, k, after):
            a, b = stat(k), stat(k)
            t = ts(a, ss, 1.0 / n, EPS, ALU.mult, ALU.add, after)
            return b, tt(b, a, NEG[:, 0:k], ALU.pow, [t], "pool")

        free = {b: [] for b in range(8)}

        slots, groups = [], {}

        def group(name, w, k0, nk, c0, nc_=512):
            per = min(nk, 1024 // nc_)
            ids = []
            for k in range(k0, k0 + nk, per):
                src = w[k * P:(k + per) * P, c0:c0 + nc_].rearrange("(k p) n -> p k n", p=P)
                ids.append(len(slots))
                slots.append((src, per, nc_))
            groups[name] = ids

        w_in, w_in2 = A["w_in"][0], A["w_in_2"][0]
        for n, c in (("q", 0), ("k", 1024), ("v", 2048), ("f", 3072), ("qh", 4096), ("i", 5120), ("g", 6144)):
            for j in range(2):
                group(f"{n}{j}", w_in, 0, 16, c + 512 * j)
        for j in range(2):
            group(f"ckv{j}", A["w_ckv"][0], 0, 16, 512 * j)
        for j in range(4):
            group(f"wo{j}", A["w_out"][0], 0, 16, 512 * j)
        group("cq", A["w_cq"][0], 0, 16, 0)
        for j in range(4):
            group(f"co{j}", A["w_co"][0], 0, 4, 512 * j)
        PARTS = [(0, 4), (4, 8), (8, 11)]

        def ffn_groups(tag, wg, wu, wo):
            for p, (a, b) in enumerate(PARTS):
                for j in range(a, b):
                    group(f"{tag}g{j}", wg, 0, 16, 512 * j)
                    group(f"{tag}u{j}", wu, 0, 16, 512 * j)
                for c in range(4):
                    group(f"{tag}o{p}_{c}", wo, 4 * a, 4 * (b - a), 512 * c)

        ffn_groups("F", A["w_ffn_in"][0][:, 0:FF], A["w_ffn_in"][0][:, FF:2 * FF], A["w_ffn_out"][0])
        for n, c, k in (("K", 2048, 2), ("Q", 1024, 2)):
            for j in range(k):
                group(f"{n}{j}", w_in2, 0, 16, c + 512 * j)
        group("LR", w_in2, 0, 16, 5120, 16)
        for j in range(2):
            group(f"P{j}", w_in2, 0, 16, 512 * j)
        for j in range(4):
            group(f"G0{j}", w_in2, 0, 16, 7184 + 512 * j)
        for j in range(4):
            group(f"ya{j}", A["w_branch_a_2"][0], 0, 8, 512 * j)
        for j in range(4):
            group(f"V{j}", w_in2, 0, 16, 3072 + 512 * j)
        for j in range(4):
            group(f"R{j}", w_in2, 0, 16, 5136 + 512 * j)
        for j in range(4):
            group(f"G1{j}", w_in2, 0, 16, 9232 + 512 * j)
        for j in range(4):
            group(f"yb{j}", A["w_branch_b_2"][0], 0, 16, 512 * j)
        for j in range(4):
            group(f"W{j}", A["w_out_2"][0], 0, 16, 512 * j)
        ffn_groups("H", A["w_ffn_gate_2"][0], A["w_ffn_up_2"][0], A["w_ffn_down_2"][0])

        raw_read, lo_done, pe_done = [], [], []

        def ensure(n):
            while len(lo_done) <= min(n, len(slots) - 1):
                i = len(lo_done)
                src, per, w = slots[i]
                r, h = i % NR, i % NH
                m = per * w
                t = Q.dma("sp", f"w{r}", RAW[:, r, 0:m].rearrange("p (k n) -> p k n", k=per), src,
                          [raw_read[i - NR]] if i >= NR else [])
                th = act(RH[:, h, 0:m], RAW[:, r, 0:m], after=[t] + ([pe_done[i - NH]] if i >= NH else []))
                tl = tt(RL[:, h, 0:m], RAW[:, r, 0:m], RH[:, h, 0:m].bitcast(F32), ALU.subtract, [th])
                raw_read.append(tl)
                lo_done.append(tl)

        sides = []

        def pump():
            for s in list(sides):
                if next(s, "end") == "end":
                    sides.remove(s)

        def side(s):
            sides.append(s)

        def drain(s=None):
            while (s in sides) if s is not None else sides:
                pump()

        def run(name, H, L, feature, banks, after=()):
            ids = groups[name]
            last = None
            first = list(after) + [free[b] for b in banks]
            k = 0
            for si in ids:
                ensure(si + LA)
                _, per, w = slots[si]
                h = si % NH
                hi = RH[:, h, 0:per * w].rearrange("p (k n) -> p k n", k=per)
                lo = RL[:, h, 0:per * w].rearrange("p (k n) -> p k n", k=per)
                need = first + [lo_done[si]]
                first = []
                for j in range(per):
                    s0 = k == 0
                    fin = si == ids[-1] and j == per - 1
                    if feature:
                        for c in range(4):
                            o = PS[:, banks[c // 2], (c % 2) * T:(c % 2) * T + T]
                            cs = slice(c * P, c * P + P)
                            mm(o, lo[:, j, cs], H[:, k, :], s0 and c % 2 == 0, False, need)
                            need = []
                            mm(o, hi[:, j, cs], H[:, k, :], False, False)
                            last = mm(o, hi[:, j, cs], L[:, k, :], False, fin, inc=j == per - 1 and c == 3)
                    else:
                        for b in range(2):
                            o = PS[:, banks[b], 0:w]
                            bs = slice(b * P, b * P + P)
                            mm(o, L[:, k, bs], hi[:, j, :], s0, False, need)
                            need = []
                            mm(o, H[:, k, bs], lo[:, j, :], False, False)
                            last = mm(o, H[:, k, bs], hi[:, j, :], False, fin, inc=j == per - 1 and b == 1)
                    k += 1
                pe_done.append(last)
                pump()
            return last

        turn = [0]

        def unit(n=2):
            b = 2 * (turn[0] % n)
            turn[0] += 1
            return [b, b + 1]

        def flat(banks):
            return PS[:, banks[0]:banks[1] + 1, :].rearrange("p b n -> p (b n)")

        d_x = Q.dma("act", "x", X[:, :, :], A["x"][0].rearrange("(b p) d -> p b d", p=P))
        d_eye = Q.dma("act", "eye", EYE[:, :], A["c_eye"])
        d_gc = Q.dma("act", "gc", GC[:, :], A["gains"])
        MEM = U(4, 2).rearrange("p (b d) -> p b d", b=2)
        d_mem = Q.dma("act", "mem", MEM, A["mem"][0].rearrange("(b p) d -> p b d", p=P))
        d_hot = Q.dma("act", "hot", U(2)[0:32, 0:384], A["c_hot"])
        d_dead = Q.dma("act", "dead", U(2)[0:8, 384:768], A["c_dead"])
        d_rel = Q.dma("act", "rel", U(2)[0:32, 768:776], A["rel_bias"])
        d_lam = Q.dma("act", "lam", U(2)[:, 776:1032], A["lambdas"].broadcast_to([P, 256]))
        d_mask = Q.dma("act", "mask", U(8)[:, 0:1024], A["c_mask"])
        d_mask = cp(MASK[:, :, :].rearrange("p a b -> p (a b)"), U(8)[:, 0:1024], [d_mask])

        NEG = sb("NEG", [P, 16])
        Q.op("pool", lambda g: g.memset(NEG[:, :], -0.5))
        t = Q.op("pool", lambda g: g.memset(SM[:, :], 1.0))
        t_sm = Q.op("pool", lambda g: g.memset(SM[:, :].rearrange("p (a b) -> p a b", b=64)[:, :, 0:1], 0.0), after=[t])

        def norm_t(src, xn, junk, H, L, gain, banks, after, dst_free=(), per_yield=0):
            ss = stat(2)
            t0 = act(junk[0], src[:, 0, :], ACT.Square, accum=ss[:, 0:1], after=after)
            t1 = Q.op("dve", lambda g: g.scalar_tensor_tensor(junk[1], src[:, 1, :], 1.0, src[:, 1, :],
                                                              ALU.mult, ALU.mult, accum_out=ss[:, 1:2]), after)
            if per_yield:
                yield
            r, t = rsqrt(ss, D, 2, [t0, t1])
            t0 = act(xn[:, 0, :], src[:, 0, :], scale=r[:, 0:1], after=[t, t0])
            t1 = ts(xn[:, 1, :], src[:, 1, :], r[:, 1:2], None, ALU.mult, after=[t, t1])
            if per_yield:
                yield
            done = [None] * 16
            for i in range(8):
                b = banks[i % len(banks)]
                for c in range(2):
                    for blk in range(2):
                        cc = 2 * i + c
                        t = tr(PS[:, b, c * T + blk * P:c * T + blk * P + P], xn[:, blk, cc * P:cc * P + P],
                               [t0, t1, d_eye, d_gc] + free[b], inc=c == 1 and blk == 1)
                if per_yield:
                    yield
                t = splits([(PS[:, b, c * T:c * T + T], H[:, 2 * i + c, :], L[:, 2 * i + c, :],
                             GC[:, gain + 2 * i + c:gain + 2 * i + c + 1]) for c in range(2)],
                           [t, d_gc] + list(dst_free))
                done[2 * i] = done[2 * i + 1] = t
                free[b] = [t]
            ready[0] = done

        ready = [None]

        def finish(gen):
            for _ in gen:
                pass
            return [x for x in ready[0]]

        def gain_rows(name, after):
            return Q.dma("pool", "gb", U(8), A[name].broadcast_to([P, D]), after)

        def post_norm(M, mtoks, ssq, d_gb, x_free):
            s = stat(2)
            t = red(s, ssq, ALU.add, mtoks)
            r, t = rsqrt(s, D, 2, [t])
            res = []
            for b in range(2):
                t1 = stt(M[:, b, :], M[:, b, :], r[:, b:b + 1], U(8), ALU.mult, ALU.mult, [t, d_gb] + mtoks)
                res.append(tt(X[:, b, :], X[:, b, :], M[:, b, :], ALU.add, [t1] + list(x_free)))
            return res

        def token_groups(names, H, L, M, after, m_free, d_sq):
            ssq = stat(8).rearrange("p (b c) -> p b c", b=2)
            toks = []
            for c, n in enumerate(names):
                bk = unit()
                t = run(n, H, L, False, bk, after if c == 0 else ())
                cs = slice(c * 512, c * 512 + 512)
                v = cp(M[:, :, cs], PS[:, bk[0]:bk[1] + 1, :], [t] + list(m_free))
                free[bk[0]] = free[bk[1]] = [v]
                for b in range(2):
                    toks.append(act(d_sq[b], M[:, b, cs], ACT.Square, accum=ssq[:, b, c:c + 1], after=[v] + list(m_free)))
            return ssq, toks

        XN67 = U(6, 2).rearrange("p (b d) -> p b d", b=2)
        XN45 = U(4, 2).rearrange("p (b d) -> p b d", b=2)
        xr = finish(norm_t(X, XN67, [U(0), U(1)], AH, AL, GOFF["mix_pre_g"], list(range(8)), [d_x, d_gc]))

        mem_ready = []

        def mem_side():
            yield from norm_t(MEM, MEM, [U(0), U(1)], BH, BL, GOFF["mem_norm_g"], [4, 5], [d_mem] + xr, (), 1)
            mem_ready.extend(ready[0])

        BIAS = U(8).rearrange("p (h n) -> p h n", h=8)
        bias_ready, lam_ready, lb_ready = [], [], []
        neglam, lb, oml = stat(1), stat(8), stat(8)

        def bias_side():
            x = stat(8), stat(8)
            t = mm(PS[0:8, 6, 0:384], U(2)[0:32, 768:776], U(2)[0:32, 0:384], True, True,
                   [d_hot, d_rel] + free[6], inc=True)
            l2 = stat(2)
            lv = U(2)[:, 776:1032].rearrange("p (a m n) -> p a m n", a=2, m=2)
            t1 = tt(lv[:, :, 0, :], lv[:, :, 0, :], lv[:, :, 1, :], ALU.mult, [d_lam])
            t1 = red(l2, lv[:, :, 0, :], ALU.add, [t1])
            lg = GC[:, GOFF["hg_lb_logits"]:GOFF["hg_lb_logits"] + 8]
            t2 = tt(x[0], lg, lg, ALU.subtract, [d_gc])
            yield
            t = tt(U(2)[0:8, 384:768], PS[0:8, 6, 0:384], U(2)[0:8, 384:768], ALU.add, [t, d_dead])
            free[6] = [t]
            d = Q.dma("pool", "scr", scratch, U(2)[0:8, 384:768], [t])
            e = stat(2)
            t1 = act(e, l2, ACT.Exp, after=[t1])
            t2 = act(x[0], x[0], ACT.Exp, after=[t2])
            yield
            t1 = tt(neglam, e[:, 1:2], e[:, 0:1], ALU.subtract, [t1])
            lam_ready.append(ts(neglam, neglam, LAM0, None, ALU.subtract, after=[t1]))
            t3 = Q.op("dve", lambda g: g.reciprocal(x[1], x[0]), [t2])
            t3 = tt(x[0], x[0], x[1], ALU.mult, [t3])
            t3 = tt(lb, x[0], x[0], ALU.subtract, [t3])
            lb_ready.append(ts(oml, lb, -1.0, 1.0, ALU.mult, ALU.add, [t3]))
            lb_ready.append(t3)
            yield
            hank = bass.AP(scratch.tensor, 0, [[1, P], [384, 8], [1, 256]])
            d = Q.dma("pool", "hank", U(3).rearrange("p (h n) -> p h n", h=8), hank, [d])
            for _ in range(5):
                yield
            ts_ = []
            for c in range(2):
                for b in (6, 7):
                    j = 2 * c + b - 6
                    t = mm(PS[:, b, :], flip, U(3)[:, 512 * j:512 * j + 512], True, True, [d, d_eye] + free[b], inc=True)
                    t = act(U(8)[:, 512 * j:512 * j + 512], PS[:, b, :], after=[t, d_mask])
                    free[b] = [t]
                    ts_.append(t)
                yield
            bias_ready.extend(ts_)

        LAM0 = 0.8 - 0.6 * float(np.exp(0.0))
        side(bias_side())
        side(mem_side())

        hv = lambda ap: ap.rearrange("p (h t) -> p h t", t=T)
        tq, tk, tv = [], [], []
        V = U(2).rearrange("p (b n) -> p b n", b=2)
        for j in range(2):
            bk = unit()
            t = run(f"q{j}", AH, AL, True, bk, xr if j == 0 else ())
            t = act(U(0)[:, 1024 * j:1024 * j + 1024], flat(bk), scale=0.125, after=[t] + mem_ready + xr)
            free[bk[0]] = free[bk[1]] = [t]
            tq.append(t)
        for j in range(2):
            bk = unit()
            t = run(f"k{j}", AH, AL, True, bk)
            t = act(U(1)[:, 1024 * j:1024 * j + 1024], flat(bk), after=[t] + mem_ready)
            free[bk[0]] = free[bk[1]] = [t]
            tk.append(t)
        for j in range(2):
            bk = unit()
            t = run(f"v{j}", AH, AL, False, bk)
            t = act(V[:, :, 512 * j:512 * j + 512], PS[:, bk[0]:bk[1] + 1, :], after=[t] + lam_ready + bias_ready)
            free[bk[0]] = free[bk[1]] = [t]
            tv.append(t)
        drain()

        ODA = U(3).rearrange("p (b h d) -> p b h d", b=2, h=8)
        s_free, a_free, oda = [[], []], [[], []], []

        def da_head(h):
            for _ in range(3 * h):
                yield
            S = U(7)[:, 1024 * (h % 2):1024 * (h % 2) + 768].rearrange("p (m n) -> p m n", m=2)
            aT = SP4[:, 512 * (h % 2):512 * (h % 2) + 384]
            qv, kv = hv(U(0)), hv(U(1))
            done = [None, None]
            for m in range(2):
                r = slice(64 * m, 64 * m + 64)
                mm(PS[:, 4 + m, 0:256], qv[r, h, P:T], kv[r, h, :], True, True, tq + tk + free[4 + m])
                done[m] = mm(PS[:, 4 + m, 256:384], qv[r, h, 0:P], kv[r, h, 0:P], False, True, inc=True)
            yield
            Bh = BIAS[:, h:h + 1, :]
            t0 = tt(S[:, :, 0:256], PS[:, 4:6, 0:256], Bh.broadcast_to([P, 2, 256]), ALU.add,
                    done + bias_ready + s_free[h % 2])
            t1 = tt(S[:, :, 256:384], PS[:, 4:6, 256:384], Bh[:, :, P:T].broadcast_to([P, 2, P]), ALU.add, done)
            free[4] = free[5] = [t0, t1]
            nm, l, rc = stat(4), stat(4), stat(4)
            t0 = red(nm[:, 0:2], S[:, :, 0:256], ALU.max, [t0], negate=True)
            t1 = red(nm[:, 2:4], S[:, :, 256:384], ALU.max, [t1], negate=True)
            e = []
            for m in range(2):
                for c, cs, t in ((m, slice(0, 256), t0), (2 + m, slice(256, 384), t1)):
                    e.append(act(S[:, m, cs], S[:, m, cs], ACT.Exp, bias=nm[:, c:c + 1], accum=l[:, c:c + 1], after=[t]))
            yield
            t = Q.op("dve", lambda g: g.reciprocal(rc, l), e)
            t = ts(rc.rearrange("p (a m) -> p a m", m=2)[:, :, 1], rc.rearrange("p (a m) -> p a m", m=2)[:, :, 1],
                   neglam, None, ALU.mult, after=[t] + lam_ready)
            a = []
            for c, cs in ((0, slice(0, 256)), (2, slice(256, 384))):
                t1 = ts(S[:, 1, cs], S[:, 1, cs], rc[:, c + 1:c + 2], None, ALU.mult, after=[t])
                a.append(stt(S[:, 0, cs], S[:, 0, cs], rc[:, c:c + 1], S[:, 1, cs], ALU.mult, ALU.add, [t1]))
            yield
            for c in range(3):
                t = tr(PS[:, 6, c * P:c * P + P], S[:, 0, c * P:c * P + P], a + free[6], inc=c == 2)
            s_free[h % 2] = [t]
            yield
            t = act(aT, PS[:, 6, 0:384], after=[t] + a_free[h % 2])
            free[6] = [t]
            yield
            vs = slice(h * P, h * P + P)
            mm(PS[:, 7, P:T], aT[:, 0:P], V[:, 0, vs], True, False, [t] + tv + free[7])
            mm(PS[:, 7, P:T], aT[:, P:T], V[:, 1, vs], False, True)
            t = mm(PS[:, 7, 0:P], aT[:, T:384], V[:, 0, vs], False, True, inc=True)
            a_free[h % 2] = [t]
            yield
            t = cp(ODA[:, :, h, :], PS[:, 7, 0:T].rearrange("p (b d) -> p b d", b=2), [t] + bias_ready)
            free[7] = [t]
            oda.append(t)

        heads = [da_head(h) for h in range(8)]
        for s in heads:
            side(s)

        def head_norm(O, n, d, junk, after, junk_free):
            Of = O.rearrange("p n d -> p (n d)")
            t = act(junk, Of, ACT.Square, after=list(after) + list(junk_free))
            yield
            ss = stat(n)
            t = red(ss, junk.rearrange("p (n d) -> p n d", n=n), ALU.add, [t])
            r, t = rsqrt(ss, d, n, [t])
            yield
            norm_done.append(tt(O, O, r.unsqueeze(2).broadcast_to([P, n, d]), ALU.mult, [t]))

        norm_done = []

        tf, tqh, ti, tg = [], [], [], []
        KK, BB, QH, EE = U(4), U(5), U(6), U(7)
        for j in range(2):
            bk = unit()
            t = run(f"f{j}", AH, AL, True, bk)
            cs = slice(1024 * j, 1024 * j + 1024)
            t = act(KK[:, cs], flat(bk), ACT.Sigmoid, after=[t] + mem_ready)
            free[bk[0]] = free[bk[1]] = [t]
            fs = []
            for h in range(4):
                hs = slice(1024 * j + T * h, 1024 * j + T * h + T)
                c = 4 * j + h
                fs.append(ts(KK[:, hs], KK[:, hs], oml[:, c:c + 1], lb[:, c:c + 1], ALU.mult, ALU.add, [t] + lb_ready))
            t = ts(BB[:, cs], KK[:, cs], 2.0 ** -62, None, ALU.max, after=fs)
            t = act(BB[:, cs], BB[:, cs], ACT.Ln, after=[t])
            t2 = ts(KK[:, cs], KK[:, cs], -1.0, 1.0, ALU.mult, ALU.add, fs)
            sc = []
            for h in range(2):
                hs = slice(1024 * j + 512 * h, 1024 * j + 512 * h + 512)
                sc.append(Q.op("dve", lambda g, hs=hs: g.tensor_tensor_scan(BB[:, hs], SM[:, :], BB[:, hs], 0.0,
                                                                            ALU.mult, ALU.add), [t, t_sm]))
            tf.append([t2] + sc)
        for j in range(2):
            bk = unit()
            t = run(f"qh{j}", AH, AL, True, bk)
            t = act(QH[:, 1024 * j:1024 * j + 1024], flat(bk), after=[t] + xr)
            free[bk[0]] = free[bk[1]] = [t]
            tqh.append(t)

        def levels(q, k, b, E, dst, cross, nu, kc, banks, escale, after, dst_free, e_free, cross_free, cdone):
            nres = 2 * nu
            nb = len(banks)
            blk = lambda ap, u, c, s: ap[:, (u * kc + c) * T + s * P:(u * kc + c) * T + s * P + P]
            wr = [Q.op("pool", lambda g: g.memset(dst, 0.0), dst_free)]
            e_busy = list(e_free)

            def products(lhs, rhs, need, mask):
                pos = 0
                toks = {}
                for u in range(nu):
                    for s in range(2):
                        bk, o = banks[pos // 4], (pos % 4) * P
                        for c in range(kc):
                            t = mm(PS[:, bk, o:o + P], blk(lhs, u, c, s), blk(rhs, u, c, s), pos % 4 == 0 and c == 0,
                                   c == kc - 1, need + free[bk], inc=pos % 4 == 3 and c == kc - 1)
                        if t:
                            toks[bk] = t
                        pos += 1
                return toks

            def pick(toks, mi):
                for n, bk in enumerate(banks):
                    d = dst[:, 512 * n:512 * n + 512].rearrange("p (r t) -> p r t", t=P)
                    m = MASK[:, mi:mi + 1, :].broadcast_to([P, 4, P])
                    src = PS[:, bk, :].rearrange("p (r t) -> p r t", t=P)
                    t = Q.op("dve", lambda g, d=d, m=m, src=src: g.copy_predicated(d, m, src),
                             [toks[bk], d_mask] + wr)
                    free[bk] = [t]
                    last.append(t)

            last = []
            toks = products(k, q, list(after), 0)
            yield
            pick(toks, 0)
            b_now = list(after)
            for li, L in enumerate(LEVELS):
                if L == 64:
                    v = b.rearrange("p (n t) -> p n t", t=P)
                    t = tt(v[:, :, 64:P], v[:, :, 64:P], v[:, :, 63:64].broadcast_to([P, v.shape[1], 64]), ALU.add, b_now)
                    b_now = [t]
                w = lambda ap: ap.rearrange("p (n t) -> p n t", t=2 * L)
                bv, ev, qv, kv = w(b), w(E), w(q), w(k)
                n = bv.shape[1]
                ref = bv[:, :, L - 1:L].broadcast_to([P, n, L])
                t0 = tt(ev[:, :, L:2 * L], bv[:, :, L:2 * L], ref, ALU.subtract, b_now + e_busy)
                t1 = tt(ev[:, :, 0:L], ref, bv[:, :, 0:L], ALU.subtract, b_now + e_busy)
                t = act(E, E, ACT.Exp, scale=escale, after=[t0, t1])
                yield
                t0 = tt(ev[:, :, L:2 * L], ev[:, :, L:2 * L], qv[:, :, L:2 * L], ALU.mult, [t])
                t1 = tt(ev[:, :, 0:L], ev[:, :, 0:L], kv[:, :, 0:L], ALU.mult, [t])
                yield
                toks = products(E, E, [t0, t1], li + 1)
                e_busy = list(toks.values())
                yield
                pick(toks, li + 1)
            w = lambda ap: ap.rearrange("p (n t) -> p n t", t=T)
            bv, ev, qv, kv = w(b), w(E), w(q), w(k)
            n = bv.shape[1]
            t1 = tt(ev[:, :, 0:P], bv[:, :, P - 1:P].broadcast_to([P, n, P]), bv[:, :, 0:P], ALU.subtract, b_now + e_busy)
            t0 = cp(ev[:, :, P:T], bv[:, :, P:T], b_now + e_busy)
            t = act(E, E, ACT.Exp, scale=escale, after=[t0, t1])
            yield
            t0 = tt(ev[:, :, P:T], ev[:, :, P:T], qv[:, :, P:T], ALU.mult, [t])
            t1 = tt(ev[:, :, 0:P], ev[:, :, 0:P], kv[:, :, 0:P], ALU.mult, [t])
            yield
            bk = banks[0]
            for u in range(nu):
                for c in range(kc):
                    t = mm(PS[:, bk, u * P:u * P + P], blk(E, u, c, 0), blk(E, u, c, 1), u == 0 and c == 0, c == kc - 1,
                           [t0, t1] + free[bk], inc=u == nu - 1 and c == kc - 1)
            yield
            t = cp(cross, PS[:, bk, 0:nu * P], [t] + list(cross_free))
            free[bk] = [t]
            cdone.extend([t] + last)

        att, att_x = U(0), SP4
        lev_done = []

        def hg_levels(j):
            while len(oda) < 8:
                yield
            cs = slice(1024 * j, 1024 * j + 1024)
            yield from levels(QH[:, cs], KK[:, cs], BB[:, cs], EE[:, cs], att[:, cs], att_x[:, 512 * j:512 * j + 512],
                              4, 1, [4 + 2 * j, 5 + 2 * j], 1.0, tqh + tf[j], [oda, s_free[0], s_free[1]],
                              [s_free[0], s_free[1]], [a_free[0], a_free[1]], lev_done)

        def da_norm():
            while len(oda) < 8:
                yield
            yield from head_norm(U(3).rearrange("p (n d) -> p n d", d=P), 16, P, U(8), oda, oda)

        lev = [hg_levels(0), hg_levels(1)]
        for s in lev:
            side(s)
        dn = da_norm()
        side(dn)

        VI = U(2).rearrange("p (b n) -> p b n", b=2)
        for j in range(2):
            bk = unit()
            t = run(f"i{j}", AH, AL, False, bk)
            for h in heads:
                drain(h)
            t = act(VI[:, :, 512 * j:512 * j + 512], PS[:, bk[0]:bk[1] + 1, :], after=[t] + oda)
            free[bk[0]] = free[bk[1]] = [t]
            ti.append(t)
        GT = U(1)
        for j in range(2):
            bk = unit()
            t = run(f"g{j}", AH, AL, True, bk)
            t = act(GT[:, 1024 * j:1024 * j + 1024], flat(bk), ACT.Silu, after=[t] + oda)
            free[bk[0]] = free[bk[1]] = [t]
            tg.append(t)
        a_free_tok = [pe_done[-1]]
        drain(dn)
        da_normed = [norm_done[-1]]
        subg = stat(1)
        t_sub = ts(subg, gcol("da_subln_g"), 1.0 - LAM0, None, ALU.mult, after=[d_gc])
        mix_ready = []

        def da_out():
            o = U(3).rearrange("p (b h d) -> p b h d", b=2, h=8)
            for i in range(4):
                b = 4 + i % 2
                for c in range(2):
                    for blk in range(2):
                        t = tr(PS[:, b, c * T + blk * P:c * T + blk * P + P], o[:, blk, 2 * i + c, :],
                               da_normed + free[b], inc=c == 1 and blk == 1)
                yield
                hl = slice(2 * i, 2 * i + 2)
                t = split(PS[:, b, :].rearrange("p (c t) -> p c t", c=2), AH[:, hl, :], AL[:, hl, :], subg,
                          [t, t_sub] + a_free_tok)
                free[b] = [t]
                mix_ready.append(t)

        OHG = U(4).rearrange("p (b h d) -> p b h d", b=2, h=8)
        hg_end = []

        def hg_out():
            while lev[0] in sides or lev[1] in sides:
                yield
            av = att.rearrange("p (h b t) -> p h b t", h=8, b=2)
            o_t = []
            for half in range(2):
                for blk in range(2):
                    b = 6 + blk
                    for hh in range(4):
                        h = 4 * half + hh
                        o = PS[:, b, hh * P:hh * P + P]
                        vs = slice(h * P, h * P + P)
                        t = mm(o, av[:, h, blk, :], VI[:, blk, vs], hh == 0, blk == 0, lev_done + ti + free[b],
                               inc=hh == 3 and blk == 0)
                        if blk:
                            t = mm(o, att_x[:, h * P:h * P + P], VI[:, 0, vs], False, True, inc=hh == 3)
                    t2 = cp(OHG[:, blk, 4 * half:4 * half + 4, :],
                            PS[:, b, :].rearrange("p (h d) -> p h d", h=4), [t] + lev_done)
                    free[b] = [t2]
                    o_t.append(t2)
                    hg_end.append(t)
                yield
            yield from head_norm(U(4).rearrange("p (n d) -> p n d", d=P), 16, P, U(7), o_t, lev_done)
            o = OHG
            for i in range(4):
                b = 6 + i % 2
                for c in range(2):
                    for blk in range(2):
                        t = tr(PS[:, b, c * T + blk * P:c * T + blk * P + P], o[:, blk, 2 * i + c, :],
                               [norm_done[-1]] + free[b], inc=c == 1 and blk == 1)
                yield
                tmp = U(5)[:, 512 * i:512 * i + 512]
                t = stt(tmp, PS[:, b, :], gcol("hg_onorm_g"), GT[:, 512 * i:512 * i + 512], ALU.mult, ALU.mult,
                        [t] + tg + lev_done)
                free[b] = [t]
                hl = slice(8 + 2 * i, 10 + 2 * i)
                mix_ready.append(split(tmp.rearrange("p (c t) -> p c t", c=2), AH[:, hl, :], AL[:, hl, :], None,
                                       [t] + a_free_tok))

        side(da_out())
        side(hg_out())

        KT, VX = U(6)[:, 0:1024], U(6)[:, 1024:2048].rearrange("p (b n) -> p b n", b=2)
        bk = unit()
        t = run("ckv0", BH, BL, True, bk, mem_ready)
        for s in lev:
            drain(s)
        tkx = act(KT, flat(bk), after=[t] + lev_done)
        free[bk[0]] = free[bk[1]] = [tkx]
        bk = unit()
        t = run("ckv1", BH, BL, False, bk)
        tvx = act(VX, PS[:, bk[0]:bk[1] + 1, :], after=[t] + lev_done)
        free[bk[0]] = free[bk[1]] = [tvx]
        b_free_tok = [pe_done[-1]]
        drain()

        M23 = U(2, 2).rearrange("p (b d) -> p b d", b=2)
        d_gb = gain_rows("mix_post_g", [norm_done])
        SQ = [SP4[:, 0:512], SP4[:, 512:1024]]
        ssq, mt = token_groups([f"wo{c}" for c in range(4)], AH, AL, M23, mix_ready, hg_end + mix_ready, SQ)
        xt = post_norm(M23, mt, ssq, d_gb, xr)
        al = list(range(8))
        xr = finish(norm_t(X, XN45, [U(0), U(1)], BH, BL, GOFF["cross_pre_g"], al, xt + mix_ready, b_free_tok))

        QX, PX, PT = U(7)[:, 0:1024], U(0).rearrange("p (n k) -> p n k", k=T), U(1)
        bk = unit()
        t = run("cq", BH, BL, True, bk, xr)
        t = act(QX, flat(bk), scale=float(P) ** -0.5, after=[t] + norm_done)
        free[bk[0]] = free[bk[1]] = [t]
        sc = []
        for h in range(4):
            for blk in range(2):
                u = mm(PS[:, 4 + h, blk * T:blk * T + T], hv(QX)[:, h, blk * P:blk * P + P], hv(KT)[:, h, :],
                       blk == 0, True, [t, tkx] + free[4 + h], inc=blk == 1)
            sc.append(u)
        nm, l, rl = stat(8), stat(8), stat(8)
        ex = []
        for h in range(4):
            sv = PS[:, 4 + h, :].rearrange("p (b k) -> p b k", b=2)
            t = red(nm[:, 2 * h:2 * h + 2], sv, ALU.max, [sc[h]], negate=True)
            for blk in range(2):
                n = 2 * h + blk
                ex.append(act(PX[:, n, :], sv[:, blk, :], ACT.Exp, bias=nm[:, n:n + 1], accum=l[:, n:n + 1],
                              after=[t] + xr))
            free[4 + h] = [ex[-1]]
        t = Q.op("dve", lambda g: g.reciprocal(rl, l), ex)
        t = tt(PX, PX, rl.unsqueeze(2).broadcast_to([P, 8, T]), ALU.mult, [t])
        pts = []
        for h in range(4):
            for kb in range(2):
                for blk in range(2):
                    u = tr(PS[:, 4 + h, kb * T + blk * P:kb * T + blk * P + P], PX[:, 2 * h + blk, kb * P:kb * P + P],
                           [t] + free[4 + h], inc=kb == 1 and blk == 1)
            e = act(PT[:, 512 * h:512 * h + 512], PS[:, 4 + h, :], after=[u] + xr) if h % 2 else \
                cp(PT[:, 512 * h:512 * h + 512], PS[:, 4 + h, :], [u] + xr)
            free[4 + h] = [e]
            pts.append(e)
        oxr = []
        for i in range(2):
            for c in range(2):
                h = 2 * i + c
                for kb in range(2):
                    u = mm(PS[:, 4 + i, c * T:c * T + T], VX[:, kb, h * P:h * P + P],
                           PT[:, 512 * h + kb * T:512 * h + kb * T + T], c == 0 and kb == 0, kb == 1,
                           [pts[h], tvx] + free[4 + i], inc=c == 1 and kb == 1)
            e = split(PS[:, 4 + i, :].rearrange("p (c t) -> p c t", c=2), AH[:, 2 * i:2 * i + 2, :],
                      AL[:, 2 * i:2 * i + 2, :], None, [u, pe_done[groups["wo3"][-1]]])
            free[4 + i] = [e]
            oxr.append(e)
        b_free_tok = [pe_done[groups["cq"][-1]]]
        d_gb = gain_rows("cross_post_g", xt)
        ssq, mt = token_groups([f"co{c}" for c in range(4)], AH, AL, M23, oxr, xt, SQ)
        xt = post_norm(M23, mt, ssq, d_gb, xr)
        xr = finish(norm_t(X, XN45, [U(6), U(7)], BH, BL, GOFF["ffn_pre_g"], al, xt + oxr, b_free_tok))

        def ffn(tag, inH, inL, hidH, hidL, in_ready, post, x_toks, hid_free, tmp_free):
            SIL = [U(0)[:, 0:1024], U(0)[:, 1024:2048]]
            Fa = M23
            sil_free = [list(tmp_free), list(tmp_free)]
            d = gain_rows(post, x_toks)
            ftok = list(x_toks)
            ssq = stat(8).rearrange("p (b c) -> p b c", b=2)
            mt, n = [], 0
            for p, (a, b) in enumerate(PARTS):
                hid = []
                for j in range(a, b):
                    g = unit(4)
                    tg_ = run(f"{tag}g{j}", inH, inL, True, g, in_ready if j == 0 else ())
                    s = SIL[n % 2]
                    t = act(s, flat(g), ACT.Silu, after=[tg_] + sil_free[n % 2])
                    free[g[0]] = free[g[1]] = [t]
                    u = unit(4)
                    tu = run(f"{tag}u{j}", inH, inL, True, u)
                    t = tt(s, s, flat(u), ALU.mult, [t, tu])
                    free[u[0]] = free[u[1]] = [t]
                    hl = slice(4 * (j - a), 4 * (j - a) + 4)
                    t = split(s.rearrange("p (c t) -> p c t", c=4), hidH[:, hl, :], hidL[:, hl, :], None,
                              [t] + list(hid_free))
                    sil_free[n % 2] = [t]
                    hid.append(t)
                    n += 1
                for c in range(4):
                    bk = unit(4)
                    t = run(f"{tag}o{p}_{c}", hidH, hidL, False, bk, hid if c == 0 else ())
                    cs = slice(512 * c, 512 * c + 512)
                    src = PS[:, bk[0]:bk[1] + 1, :]
                    if p == 0:
                        t = act(Fa[:, :, cs], src, after=[t] + ftok)
                    else:
                        t = tt(Fa[:, :, cs], src, Fa[:, :, cs], ALU.add, [t] + mt)
                    free[bk[0]] = free[bk[1]] = [t]
                    mt.append(t)
                    if p == 2:
                        for k in range(2):
                            mt.append(act(SQ[k], Fa[:, k, cs], ACT.Square, accum=ssq[:, k, c:c + 1], after=[t]))
                hid_free = [pe_done[-1]]
            return post_norm(Fa, mt, ssq, d, x_toks)

        xt = ffn("F", BH, BL, AH, AL, xr, "ffn_post_g", xt + xr, [pe_done[groups["co3"][-1]]], xr)

        xr = finish(norm_t(X, XN45, [U(6), U(7)], BH, BL, GOFF["norm_mix_pre_2"], al, xt,
                           [pe_done[groups["Fu10"][-1]]]))
        old = xt + xr
        WP = U(8).rearrange("p (g k n) -> p g k n", g=4, k=2)
        d_wp = Q.dma("pool", "wp", WP, A["w_pool_2"][0].rearrange("g (k p) n -> p g k n", p=P), xt)
        GU = U(6)[0:16, 0:1024]
        d_gu = Q.dma("pool", "gu", GU, A["w_gate_up_2"][0], old)
        tk, tq = [], []
        for n, dst, lst, s in (("K", U(1), tk, 1.0), ("Q", U(0), tq, 0.0625)):
            for j in range(2):
                bk = unit()
                t = run(f"{n}{j}", BH, BL, True, bk, xr)
                t = act(dst[:, 1024 * j:1024 * j + 1024], flat(bk), scale=s, after=[t] + old)
                free[bk[0]] = free[bk[1]] = [t]
                lst.append(t)
        bk = unit()
        t = run("LR", BH, BL, False, bk)
        glr = GL[:, 0:32].rearrange("p (b n) -> p b n", b=2)
        t = cp(glr, PS[:, bk[0]:bk[1] + 1, 0:16], [t])
        free[bk[0]] = free[bk[1]] = [t]
        G2 = U(2)
        g_ready = [[], []]
        t_glr = t

        def gate_side():
            yield
            for blk in range(2):
                t = tr(PS[0:16, 4, blk * P:blk * P + P], glr[:, blk, :], [t_glr] + free[4], inc=blk == 1)
            yield
            t = cp(GL[0:16, 32:32 + T], PS[0:16, 4, 0:T], [t])
            free[4] = [t]
            yield
            zt = []
            for c in range(8):
                u = mm(PS[:, 4 + c // 2, (c % 2) * T:(c % 2) * T + T], GU[:, c * P:c * P + P], GL[0:16, 32:32 + T],
                       c % 2 == 0, True, [t, d_gu] + free[4 + c // 2], inc=c % 2 == 1)
                if c % 2:
                    zt.append(u)
            gu_free.append(u)
            yield
            for j in range(2):
                a, m = [], []
                for c in range(4 * j, 4 * j + 4):
                    z = PS[:, 4 + c // 2, (c % 2) * T:(c % 2) * T + T]
                    cs = slice(c * T, c * T + T)
                    m.append(ts(G2[:, cs], z, gcol("b_gate_2", c), 0.0, ALU.add, ALU.min, zt + old))
                for c in range(4 * j, 4 * j + 4):
                    z = PS[:, 4 + c // 2, (c % 2) * T:(c % 2) * T + T]
                    a.append(act(U(4)[:, c * T:c * T + T], z, ACT.Abs, bias=gcol("b_gate_2", c), after=m + old))
                    free[4 + c // 2] = [a[-1]]
                hs = slice(1024 * j, 1024 * j + 1024)
                t = act(U(4)[:, hs], U(4)[:, hs], ACT.Exp, scale=-1.0, after=a)
                t = act(U(4)[:, hs], U(4)[:, hs], ACT.Ln, bias=1.0, after=[t])
                yield
                t = tt(G2[:, hs], G2[:, hs], U(4)[:, hs], ALU.subtract, [t] + m)
                u4_free.append(t)
                for k in range(2):
                    ks = slice(1024 * j + 512 * k, 1024 * j + 512 * k + 512)
                    g_ready[j].append(Q.op("dve", lambda g, ks=ks: g.tensor_tensor_scan(
                        G2[:, ks], SM[:, :], G2[:, ks], 0.0, ALU.mult, ALU.add), [t]))
                yield

        u4_free, gu_free, lev_done = [], [], []
        gs = gate_side()
        side(gs)
        ATT2 = SP4
        AX2 = SM

        def gla_levels(j):
            while gs in sides:
                yield
            cs = slice(1024 * j, 1024 * j + 1024)
            yield from levels(U(0)[:, cs], U(1)[:, cs], G2[:, cs], U(3)[:, cs], ATT2[:, 512 * j:512 * j + 512],
                              AX2[:, 256 * j:256 * j + 256], 2, 2, [6 + j], 0.0625, tq + tk + g_ready[j],
                              old, old, g_ready, lev_done)

        PP, S0, S1 = U(4), U(5), U(7)
        tp = []
        for j in range(2):
            bk = unit()
            t = run(f"P{j}", BH, BL, True, bk)
            drain(gs)
            t = act(PP[:, 1024 * j:1024 * j + 1024], flat(bk), after=[t] + u4_free)
            free[bk[0]] = free[bk[1]] = [t]
            tp.append(t)
        lev = [gla_levels(0), gla_levels(1)]
        for s in lev:
            side(s)
        pool_ready, pool_end = [], []

        def pool_side():
            pv, s0, s1 = hv(PP), hv(S0), hv(S1)
            src, prev = pv, tp + old
            bufs = [s0, s1, s0, s1]
            res = []
            for g, w in enumerate((2, 4, 8, 16)):
                sh, c0, dst = w // 2, 2 * g, bufs[g]
                a = tt(dst[:, c0:8, sh:T], src[:, c0:8, sh:T], src[:, c0:8, 0:T - sh], ALU.add, prev)
                b = cp(dst[:, c0:8, 0:sh], src[:, c0:8, 0:sh], prev)
                src, prev = dst, [a, b]
                res.append([a, b])
                yield
            tmp = GL[:, 0:32].rearrange("p (c t) -> p c t", c=2)
            early = EYE[:, 256:320]
            wt = []
            end = [t_glr]
            for g, w in enumerate((2, 4, 8, 16)):
                s, cs = bufs[g], slice(2 * g, 2 * g + 2)
                cnt = early[:, 16 * g:16 * g + 16].unsqueeze(1).broadcast_to([P, 2, 16])
                a = tt(tmp, s[:, cs, 0:16], cnt, ALU.mult, res[g] + prev + end + gu_free)
                b = stt(s[:, cs, :], s[:, cs, :], 1.0 / w, pv[:, cs, :], ALU.mult, ALU.subtract, [a])
                b = tt(s[:, cs, 0:16], tmp, pv[:, cs, 0:16], ALU.subtract, [b])
                end = [b]
                wt.append(b)
                yield
            for g in range(4):
                b, s = 4 + g % 2, bufs[g]
                for c in range(2):
                    for kc in range(2):
                        t = mm(PS[:, b, c * T:c * T + T], WP[:, g, kc, c * P:c * P + P], s[:, 2 * g + kc, :],
                               c == 0 and kc == 0, kc == 1, [wt[g], d_wp] + free[b], inc=c == 1 and kc == 1)
                yield
                pool_end.append(t)
                t = splits([(PS[:, b, c * T:c * T + T], AH[:, 2 * g + c, :], AL[:, 2 * g + c, :],
                             gcol("pool_scale_2", 2 * g + c)) for c in range(2)], [t, pe_done[groups["Fo2_3"][-1]]])
                free[b] = [t]
                pool_ready.append(t)

        ps_ = pool_side()
        side(ps_)
        T0 = U(6, 2)
        tt0 = []
        for j in range(4):
            bk = unit()
            t = run(f"G0{j}", BH, BL, True, bk)
            if j == 2:
                drain(ps_)
            for c in range(4):
                e = act(T0[:, 1024 * j + T * c:1024 * j + T * c + T], PS[:, bk[c // 2], (c % 2) * T:(c % 2) * T + T],
                        ACT.Sigmoid, bias=gcol("b_branch_gates_2", 4 * j + c), after=[t] + gu_free + pool_end)
            free[bk[0]] = free[bk[1]] = [e]
            tt0.append(e)
        for j in range(4):
            bk = unit()
            t = run(f"ya{j}", AH, AL, True, bk, pool_ready)
            ts_ = slice(1024 * j, 1024 * j + 1024)
            tt0[j] = tt(T0[:, ts_], T0[:, ts_], flat(bk), ALU.mult, [t, tt0[j]])
            free[bk[0]] = free[bk[1]] = [tt0[j]]
        for s in lev:
            drain(s)
        V2 = U(0, 2).rearrange("p (b n) -> p b n", b=2)
        tv = []
        for j in range(4):
            bk = unit()
            t = run(f"V{j}", BH, BL, False, bk)
            t = act(V2[:, :, 512 * j:512 * j + 512], PS[:, bk[0]:bk[1] + 1, :], after=[t] + lev_done)
            free[bk[0]] = free[bk[1]] = [t]
            tv.append(t)
        O2 = U(4, 2).rearrange("p (b h d) -> p b h d", b=2, h=4)
        tr_, ox_ready, v_free = [], [], []

        def gla_out():
            ot = []
            for blk in range(2):
                for h in range(4):
                    vs = slice(512 * h, 512 * h + 512)
                    o = PS[:, 4 + h, :]
                    at = lambda hh, s: ATT2[:, (2 * hh + s) * P:(2 * hh + s) * P + P]
                    t = mm(o, at(h, blk), V2[:, blk, vs], True, blk == 0, lev_done + tv + free[4 + h], inc=blk == 0)
                    if blk:
                        t = mm(o, AX2[:, h * P:h * P + P], V2[:, 0, vs], False, True, inc=True)
                    v_free.append(t)
                    if h % 2:
                        e = act(O2[:, blk, h, :], o, after=[t] + pool_end + pool_ready)
                    else:
                        e = cp(O2[:, blk, h, :], o, [t] + pool_end + pool_ready)
                    free[4 + h] = [e]
                    ot.append(e)
                yield
            ss = stat(8)
            sq = []
            for n in range(8):
                sq.append(act(U(8)[:, 512 * (n % 2):512 * (n % 2) + 512], O2[:, n // 4, n % 4, :], ACT.Square,
                              accum=ss[:, n:n + 1], after=ot + pool_end + sq[-1:]))
                if n % 2:
                    yield
            r, t = rsqrt(ss, 512, 8, sq)
            yield
            of = U(4, 2).rearrange("p (n d) -> p n d", d=512)
            sc = []
            for n in range(2):
                sc.append(tt(of[:, 4 * n:4 * n + 4, :], of[:, 4 * n:4 * n + 4, :],
                             r[:, 4 * n:4 * n + 4].unsqueeze(2).broadcast_to([P, 4, 512]), ALU.mult, [t]))
                yield
            while len(tr_) < 4:
                yield
            buf_free = [sq, sq]
            for i in range(8):
                b = 4 + i % 4
                for c in range(2):
                    cc = 2 * i + c
                    for blk in range(2):
                        t = tr(PS[:, b, c * T + blk * P:c * T + blk * P + P],
                               O2[:, blk, cc // 4, (cc % 4) * P:(cc % 4) * P + P], sc + free[b], inc=c == 1 and blk == 1)
                yield
                tmp = U(8)[:, 512 * (i % 2):512 * (i % 2) + 512]
                e = []
                for c in range(2):
                    cc = 2 * i + c
                    e.append(stt(tmp[:, c * T:c * T + T], PS[:, b, c * T:c * T + T], gcol("gla_norm_2", cc % 4),
                                 RS[:, cc * T:cc * T + T], ALU.mult, ALU.mult, [t] + tr_ + buf_free[i % 2]))
                free[b] = e
                hl = slice(2 * i, 2 * i + 2)
                t = split(tmp.rearrange("p (c t) -> p c t", c=2), AH[:, hl, :], AL[:, hl, :], None,
                          e + [pe_done[groups["ya3"][-1]]])
                buf_free[i % 2] = [t]
                ox_ready.append(t)

        go = gla_out()
        side(go)
        RS = U(2, 2)
        for j in range(4):
            bk = unit()
            t = run(f"R{j}", BH, BL, True, bk)
            t = act(RS[:, 1024 * j:1024 * j + 1024], flat(bk), ACT.Silu, after=[t] + lev_done)
            free[bk[0]] = free[bk[1]] = [t]
            tr_.append(t)
        G1 = U(0, 2)
        tg1 = []
        for j in range(4):
            bk = unit()
            t = run(f"G1{j}", BH, BL, True, bk)
            for c in range(4):
                e = act(G1[:, 1024 * j + T * c:1024 * j + T * c + T], PS[:, bk[c // 2], (c % 2) * T:(c % 2) * T + T],
                        ACT.Sigmoid, bias=gcol("b_branch_gates_2", 16 + 4 * j + c), after=[t] + v_free)
            free[bk[0]] = free[bk[1]] = [e]
            tg1.append(e)
        drain()
        hb_free = [pe_done[-1]]
        mr = []
        for j in range(4):
            bk = unit()
            t = run(f"yb{j}", AH, AL, True, bk, ox_ready)
            ts_ = slice(1024 * j, 1024 * j + 1024)
            t = tt(G1[:, ts_], G1[:, ts_], flat(bk), ALU.mult, [t, tg1[j]])
            free[bk[0]] = free[bk[1]] = [t]
            t = tt(G1[:, ts_], G1[:, ts_], T0[:, ts_], ALU.add, [t, tt0[j]])
            mr.append(split(G1[:, ts_].rearrange("p (c t) -> p c t", c=4), BH[:, 4 * j:4 * j + 4, :],
                            BL[:, 4 * j:4 * j + 4, :], None, [t] + hb_free))
        d_gb = gain_rows("norm_mix_post_2", ox_ready)
        ssq, mt = token_groups([f"W{c}" for c in range(4)], BH, BL, M23, mr, ox_ready + mr, SQ)
        xt = post_norm(M23, mt, ssq, d_gb, old)
        xr = finish(norm_t(X, XN45, [U(6), U(7)], AH, AL, GOFF["norm_ffn_pre_2"], al, xt + mr,
                           [pe_done[groups["yb3"][-1]]]))
        xt = ffn("H", AH, AL, BH, BL, xr, "norm_ffn_post_2", xt + xr, [pe_done[groups["W3"][-1]]], xr)
        ov = out[0].rearrange("(b p) d -> p b d", p=P)
        for b in range(2):
            t = Q.dma("sp", f"out{b}", ov[:, b, :], X[:, b, :], [xt[b]])
            Q.wait("sp", [t])

        block = ctx.enter_context(nc.Block())

        @block.sync
        def _(g):
            Q.play("sp", g)

        @block.scalar
        def _(g):
            Q.play("act", g)

        @block.vector
        def _(g):
            Q.play("dve", g)

        @block.gpsimd
        def _(g):
            Q.play("pool", g)

        @block.tensor
        def _(g):
            Q.play("pe", g)


RAWS = ["x", "mem", "w_in", "w_out", "w_cq", "w_ckv", "w_co", "w_ffn_in", "w_ffn_out", "rel_bias", "w_in_2",
        "w_gate_up_2", "w_pool_2", "w_branch_a_2", "w_branch_b_2", "w_out_2", "w_ffn_gate_2", "w_ffn_up_2",
        "w_ffn_down_2", "mix_post_g", "cross_post_g", "ffn_post_g", "norm_mix_post_2", "norm_ffn_post_2"]


def kernel(**inputs):
    import concourse.bacc as bacc
    from concourse.bass_utils import run_bass_kernel_spmd

    f = {n: np.ascontiguousarray(a) for n, a in inputs.items()}
    arrays = {n: f[n] for n in RAWS}
    cols = []
    for n in GAINS:
        cols.append(f[n].reshape(-1, P).T)
    arrays["gains"] = np.ascontiguousarray(np.concatenate(cols, 1))
    arrays["lambdas"] = np.ascontiguousarray(np.concatenate(
        [f[n].reshape(1, 64) for n in ("lambda_q1", "lambda_k1", "lambda_q2", "lambda_k2")], 1))
    arrays.update(shape_constants())
    nc = bacc.Bacc("TRN2", target_bir_lowering=False, num_devices=1)
    A = {n: nc.dram_tensor("in_" + n, a.shape, mybir.dt.from_np(a.dtype), kind="ExternalInput").ap()
         for n, a in arrays.items()}
    out = nc.dram_tensor("out_x", (1, T, D), F32, kind="ExternalOutput").ap()
    scratch = nc.dram_tensor("scratch", (8, 384), F32, kind="Internal").ap()
    build(nc, A, out, scratch)
    r = run_bass_kernel_spmd(nc, [{"in_" + n: a for n, a in arrays.items()}], core_ids=[0])
    return r.results[0]["out_x"]
```

```python
from contextlib import ExitStack

import numpy as np

import concourse.bass as bass
from concourse import mybir

F32 = mybir.dt.float32
F32R = mybir.dt.float32r
U8 = mybir.dt.uint8
ACT = mybir.ActivationFunctionType
ALU = mybir.AluOpType
AXX = mybir.AxisListType.X
P = 128
D = 2048
T = 256
FF = 5632
EPS = 1e-6

GAINS = ["mix_pre_g", "cross_pre_g", "mem_norm_g", "ffn_pre_g", "norm_mix_pre_2", "norm_ffn_pre_2",
         "b_gate_2", "pool_scale_2", "b_branch_gates_2", "hg_lb_logits", "da_subln_g", "hg_onorm_g", "gla_norm_2"]
GCOLS = [16, 16, 16, 16, 16, 16, 8, 8, 32, 8, 1, 1, 4]
GOFF = {n: sum(GCOLS[:i]) for i, n in enumerate(GAINS)}
NGC = sum(GCOLS)
LEVELS = [1, 2, 4, 8, 16, 32, 64]


def shape_constants():
    i = np.arange(P)
    ident = np.eye(P, dtype=np.float32)
    flip = np.ascontiguousarray(ident[::-1])
    m = np.arange(384)
    dist = np.maximum(255 - m, 0)
    nf = np.maximum(dist, 1).astype(np.float32)
    large = 16 + (np.log(nf / np.float32(16)) / np.float32(np.log(8.0)) * np.float32(16)).astype(np.int32)
    bucket = np.where(dist < 16, dist, np.minimum(large, 31))
    onehot = ((bucket[None, :] == np.arange(32)[:, None]) & (m[None, :] <= 255)).astype(np.float32)
    dead = np.broadcast_to(np.where(m > 255, -1e30, 0.0).astype(np.float32), (8, 384))
    masks = [i[:, None] == i[None, :]]
    for L in LEVELS:
        s, t = i[:, None], i[None, :]
        masks.append((s // (2 * L) == t // (2 * L)) & (s % (2 * L) < L) & (t % (2 * L) >= L))
    masks = np.stack(masks, 1).astype(np.float32)
    counts = np.stack([1.0 / np.minimum(np.arange(16) + 1, w) for w in (2, 4, 8, 16)])
    counts = np.broadcast_to(counts.astype(np.float32).reshape(1, 64), (P, 64))
    return {"c_eye": np.concatenate([ident, flip, counts], 1).astype(np.float32),
            "c_hot": np.ascontiguousarray(onehot), "c_dead": np.ascontiguousarray(dead),
            "c_mask": np.ascontiguousarray(masks.reshape(P, 8 * P))}


class Queues:

    def __init__(self, nc, ctx):
        self.nc, self.ctx = nc, ctx
        self.q = {e: [] for e in ("pe", "act", "dve", "pool", "sp")}
        self.sem = {e: ctx.enter_context(nc.semaphore("s_" + e)) for e in ("pe", "act", "dve", "pool")}
        self.n = {e: 0 for e in self.sem}
        self.told = {e: {} for e in self.q}

    def wait(self, e, after):
        need = {}
        for t in after:
            if isinstance(t, list):
                for u in t:
                    need[u[0]] = max(need.get(u[0], 0), u[1])
            elif t is not None:
                need[t[0]] = max(need.get(t[0], 0), t[1])
        for k, v in need.items():
            if self.told[e].get(k, 0) < v:
                self.told[e][k] = v
                self.q[e].append(("wait", k, v))

    def op(self, e, fn, after=(), inc=True):
        self.wait(e, after)
        if inc:
            self.n[e] += 1
        self.q[e].append(("op", fn, inc))
        return (e, self.n[e]) if inc else None

    def dma(self, e, name, out, in_, after=()):
        if name not in self.sem:
            self.sem[name] = self.ctx.enter_context(self.nc.semaphore("d_" + name))
            self.n[name] = 0
        self.wait(e, after)
        self.n[name] += 16
        self.q[e].append(("dma", lambda g: g.dma_start(out, in_), name))
        return (name, self.n[name])

    def play(self, e, g):
        for it in self.q[e]:
            if it[0] == "wait":
                g.wait_ge(self.sem[it[1]], it[2])
            elif it[0] == "dma":
                it[1](g).then_inc(self.sem[it[2]], 16)
            else:
                i = it[1](g)
                if it[2]:
                    i.then_inc(self.sem[e], 1)


def build(nc, A, out, scratch):
    ctx = ExitStack()
    with ctx:
        Q = Queues(nc, ctx)

        def sb(name, shape, dt=F32):
            return ctx.enter_context(nc.sbuf_tensor(name, shape, dt))

        NR, NH = 3, 4
        LA = NH - 1
        RAW = sb("RAW", [P, NR, 1024])
        RH = sb("RH", [P, NH, 1024], F32R)
        RL = sb("RL", [P, NH, 1024], F32R)
        AH, AL = sb("AH", [P, 16, T], F32R), sb("AL", [P, 16, T], F32R)
        BH, BL = sb("BH", [P, 16, T], F32R), sb("BL", [P, 16, T], F32R)
        X = sb("X", [P, 2, D])
        AR = sb("AR", [P, 9 * 2048])
        SP4 = sb("SP4", [P, 1024])[:, :]
        EYE = sb("EYE", [P, 320])
        MASK = sb("MASK", [P, 8, P], U8)
        GC = sb("GC", [P, NGC])
        ST = sb("ST", [P, 448])
        SM = sb("SM", [P, 512])
        RR = sb("RR", [P, 1, T])
        PS = ctx.enter_context(nc.psum_tensor("PS", [P, 8, 512], F32))
        ident, flip = EYE[:, 0:P], EYE[:, P:2 * P]

        def U(k, n=1):
            return AR[:, k * 2048:(k + n) * 2048]

        def gcol(name, c=0):
            return GC[:, GOFF[name] + c:GOFF[name] + c + 1]

        used = [0]

        def stat(n):
            used[0] += n
            assert used[0] <= 448
            return ST[:, used[0] - n:used[0]]

        def act(o, i, f=ACT.Copy, scale=1.0, bias=0.0, accum=None, after=()):
            return Q.op("act", lambda g: g.activation(o, i, f, bias=bias, scale=scale, accum_out=accum), after)

        def tt(o, a, b, f, after=(), e="dve"):
            return Q.op(e, lambda g: g.tensor_tensor(o, a, b, f), after)

        def ts(o, a, s1, s2, f0, f1=None, after=(), e="dve"):
            if f1 is None:
                return Q.op(e, lambda g: g.tensor_scalar(o, a, s1, None, f0), after)
            return Q.op(e, lambda g: g.tensor_scalar(o, a, s1, s2, f0, f1), after)

        def stt(o, a, s, b, f0, f1, after=()):
            return Q.op("dve", lambda g: g.scalar_tensor_tensor(o, a, s, b, f0, f1), after)

        def red(o, i, f, after=(), negate=False):
            return Q.op("dve", lambda g: g.tensor_reduce(o, i, AXX, f, negate=negate), after)

        def cp(o, i, after=(), e="dve"):
            return Q.op(e, lambda g: g.tensor_copy(o, i), after)

        def mm(o, l, r, start, stop, after=(), inc=False):
            return Q.op("pe", lambda g: g.matmul(o, l, r, start=start, stop=stop, skip_group_check=True), after, inc)

        def tr(o, i, after=(), inc=False):
            return Q.op("pe", lambda g: g.transpose(o, i, ident), after, inc)

        def split(src, h, l, scale=None, after=()):
            if scale is None:
                t = act(h, src, after=after)
                return tt(l, src, h.bitcast(F32), ALU.subtract, [t])
            t = act(h, src, scale=scale, after=after)
            return stt(l, src, scale, h.bitcast(F32), ALU.mult, ALU.subtract, [t])

        def splits(parts, after=()):
            for src, h, l, scale in parts:
                t = act(h, src, scale=scale, after=after)
            for src, h, l, scale in parts:
                u = stt(l, src, scale, h.bitcast(F32), ALU.mult, ALU.subtract, [t])
            return u

        def rsqrt(ss, n, k, after):
            a, b = stat(k), stat(k)
            t = ts(a, ss, 1.0 / n, EPS, ALU.mult, ALU.add, after)
            return b, tt(b, a, NEG[:, 0:k], ALU.pow, [t], "pool")

        free = {b: [] for b in range(8)}

        slots, groups = [], {}

        def group(name, w, k0, nk, c0, nc_=512):
            per = min(nk, 1024 // nc_)
            ids = []
            for k in range(k0, k0 + nk, per):
                src = w[k * P:(k + per) * P, c0:c0 + nc_].rearrange("(k p) n -> p k n", p=P)
                ids.append(len(slots))
                slots.append((src, per, nc_))
            groups[name] = ids

        w_in, w_in2 = A["w_in"][0], A["w_in_2"][0]
        for n, c in (("q", 0), ("k", 1024), ("v", 2048), ("f", 3072), ("qh", 4096), ("i", 5120), ("g", 6144)):
            for j in range(2):
                group(f"{n}{j}", w_in, 0, 16, c + 512 * j)
        group("ckv0", A["w_ckv"][0], 0, 16, 0)
        for j in range(4):
            group(f"wo{j}", A["w_out"][0], 0, 16, 512 * j)
        group("cq", A["w_cq"][0], 0, 16, 0)
        group("ckv1", A["w_ckv"][0], 0, 16, 512)
        for j in range(4):
            group(f"co{j}", A["w_co"][0], 0, 4, 512 * j)
        PARTS = [(0, 4), (4, 8), (8, 11)]

        def ffn_groups(tag, wg, wu, wo):
            for p, (a, b) in enumerate(PARTS):
                for j in range(a, b):
                    group(f"{tag}g{j}", wg, 0, 16, 512 * j)
                    group(f"{tag}u{j}", wu, 0, 16, 512 * j)
                for c in range(4):
                    group(f"{tag}o{p}_{c}", wo, 4 * a, 4 * (b - a), 512 * c)

        ffn_groups("F", A["w_ffn_in"][0][:, 0:FF], A["w_ffn_in"][0][:, FF:2 * FF], A["w_ffn_out"][0])
        for j in range(2):
            group(f"K{j}", w_in2, 0, 16, 2048 + 512 * j)
        group("LR", w_in2, 0, 16, 5120, 16)
        for j in range(2):
            group(f"Q{j}", w_in2, 0, 16, 1024 + 512 * j)
        for j in range(2):
            group(f"P{j}", w_in2, 0, 16, 512 * j)
        for j in range(4):
            group(f"G0{j}", w_in2, 0, 16, 7184 + 512 * j)
        for j in range(4):
            group(f"ya{j}", A["w_branch_a_2"][0], 0, 8, 512 * j)
        for j in range(4):
            group(f"V{j}", w_in2, 0, 16, 3072 + 512 * j)
        for j in range(4):
            group(f"R{j}", w_in2, 0, 16, 5136 + 512 * j)
        for j in range(4):
            group(f"G1{j}", w_in2, 0, 16, 9232 + 512 * j)
        for j in range(4):
            group(f"yb{j}", A["w_branch_b_2"][0], 0, 16, 512 * j)
        for j in range(4):
            group(f"W{j}", A["w_out_2"][0], 0, 16, 512 * j)
        ffn_groups("H", A["w_ffn_gate_2"][0], A["w_ffn_up_2"][0], A["w_ffn_down_2"][0])

        raw_read, lo_done, pe_done = [], [], []
        busy = [n for n in groups if n[0] in "fiKQP" or n[:2] in ("qh", "g0", "g1")]
        on_pool = {i for n in busy for i in groups[n] if i % 3 == 0}
        on_pool |= {i for n in ("q0", "cq", "co0", "co1", "Fg0", "K0", "Hg0") for i in groups[n] if i % 2}

        def ensure(n):
            while len(lo_done) <= min(n, len(slots) - 1):
                i = len(lo_done)
                src, per, w = slots[i]
                r, h = i % NR, i % NH
                m = per * w
                t = Q.dma("sp", f"w{r}", RAW[:, r, 0:m].rearrange("p (k n) -> p k n", k=per), src,
                          [raw_read[i - NR]] if i >= NR else [])
                th = act(RH[:, h, 0:m], RAW[:, r, 0:m], after=[t] + ([pe_done[i - NH]] if i >= NH else []))
                tl = tt(RL[:, h, 0:m], RAW[:, r, 0:m], RH[:, h, 0:m].bitcast(F32), ALU.subtract, [th],
                        "pool" if i in on_pool else "dve")
                raw_read.append(tl)
                lo_done.append(tl)

        sides = []

        def pump():
            for s in list(sides):
                if next(s, "end") == "end":
                    sides.remove(s)

        def side(s):
            sides.append(s)

        def drain(s=None):
            while (s in sides) if s is not None else sides:
                pump()

        def run(name, H, L, feature, banks, after=(), ready=None):
            ids = groups[name]
            last = None
            first = list(after) + [free[b] for b in banks]
            k = 0
            for si in ids:
                ensure(si + LA)
                _, per, w = slots[si]
                h = si % NH
                hi = RH[:, h, 0:per * w].rearrange("p (k n) -> p k n", k=per)
                lo = RL[:, h, 0:per * w].rearrange("p (k n) -> p k n", k=per)
                need = first + [lo_done[si]]
                first = []
                for j in range(per):
                    s0 = k == 0
                    if ready:
                        while ready[k] is None:
                            pump()
                        need = need + [ready[k]]
                    fin = si == ids[-1] and j == per - 1
                    if feature:
                        for c in range(4):
                            o = PS[:, banks[c // 2], (c % 2) * T:(c % 2) * T + T]
                            cs = slice(c * P, c * P + P)
                            mm(o, lo[:, j, cs], H[:, k, :], s0 and c % 2 == 0, False, need)
                            need = []
                            mm(o, hi[:, j, cs], H[:, k, :], False, False)
                            last = mm(o, hi[:, j, cs], L[:, k, :], False, fin, inc=j == per - 1 and c == 3)
                    else:
                        for b in range(2):
                            o = PS[:, banks[b], 0:w]
                            bs = slice(b * P, b * P + P)
                            mm(o, L[:, k, bs], hi[:, j, :], s0, False, need)
                            need = []
                            mm(o, H[:, k, bs], lo[:, j, :], False, False)
                            last = mm(o, H[:, k, bs], hi[:, j, :], False, fin, inc=j == per - 1 and b == 1)
                    k += 1
                    if j == per - 1:
                        pe_done.append(last)
                    if per == 2 or j == per - 1:
                        pump()
            return last

        turn = [0]

        def unit(n=2):
            b = 2 * (turn[0] % n)
            turn[0] += 1
            return [b, b + 1]

        def flat(banks):
            return PS[:, banks[0]:banks[1] + 1, :].rearrange("p b n -> p (b n)")

        d_eye = Q.dma("act", "eye", EYE[:, :], A["c_eye"])
        d_gc = Q.dma("act", "gc", GC[:, :], A["gains"])
        xv = A["x"][0].rearrange("(b p) d -> p b d", p=P)
        d_x = [[Q.dma("sp", f"x{c}{b}", X[:, b, 512 * c:512 * c + 512], xv[:, b, 512 * c:512 * c + 512])
                for b in range(2)] for c in range(4)]
        MEM = U(4, 2).rearrange("p (b d) -> p b d", b=2)

        NEG = sb("NEG", [P, 16])
        Q.op("pool", lambda g: g.memset(NEG[:, :], -0.5))
        t = Q.op("pool", lambda g: g.memset(SM[:, :], 1.0))
        t_sm = Q.op("pool", lambda g: g.memset(SM[:, :].rearrange("p (a b) -> p a b", b=64)[:, :, 0:1], 0.0), after=[t])

        def norm_t(src, src_toks, H, L, gain, banks, dst_free=()):
            done = []
            for i in range(8):
                b = banks[i % len(banks)]
                for c in range(2):
                    cc = 2 * i + c
                    for blk in range(2):
                        t = tr(PS[:, b, c * T + blk * P:c * T + blk * P + P], src[:, blk, cc * P:cc * P + P],
                               src_toks[i // 2] + [d_eye] + free[b], inc=c == 1 and blk == 1)
                t = splits([(PS[:, b, c * T:c * T + T], H[:, 2 * i + c, :], L[:, 2 * i + c, :],
                             GC[:, gain + 2 * i + c:gain + 2 * i + c + 1]) for c in range(2)],
                           [t, d_gc] + list(dst_free))
                done += [t, t]
                free[b] = [t]
            return done

        row_ready, row_read, col = [], [], [None]

        def row_scale(src, src_toks, junk, bank):
            ss = stat(4).rearrange("p (b h) -> p b h", b=2)
            sq = []
            for half in range(2):
                for b in range(2):
                    hs = slice(1024 * half, 1024 * half + 1024)
                    sq.append(act(junk, src[:, b, hs], ACT.Square, accum=ss[:, b, half:half + 1],
                                  after=src_toks[2 * half] + src_toks[2 * half + 1] + sq[-1:]))
                yield
            s = stat(2)
            t = red(s, ss, ALU.add, sq)
            r, t = rsqrt(s, D, 2, [t])
            yield
            yield
            w = junk[:, 0:T].rearrange("p (b n) -> p b n", b=2)
            t = act(w, r.unsqueeze(2).broadcast_to([P, 2, P]), after=[t] + sq)
            yield
            yield
            for b in range(2):
                u = tr(PS[:, bank, b * P:b * P + P], w[:, b, :], [t, d_eye] + free[bank], inc=b == 1)
            yield
            u = act(RR[:, 0, :], PS[:, bank, 0:T], after=[u] + row_read)
            free[bank] = [u]
            col[0] = r
            row_ready[:] = [t, u]
            row_read.clear()

        def start_row(src, src_toks, junk, bank):
            row_ready.clear()
            g = row_scale(src, src_toks, junk, bank)
            side(g)
            return g

        def rowed(o, banks, after, k=None):
            src = flat(banks).rearrange("p (c t) -> p c t", t=T)
            o = o.rearrange("p (c t) -> p c t", t=T)
            r = RR[:, 0:1, :].broadcast_to([P, 4, T])
            if k is None:
                t = tt(o, src, r, ALU.mult, list(after) + row_ready)
            else:
                t = stt(o, src, k, r, ALU.mult, ALU.mult, list(after) + row_ready)
            free[banks[0]] = free[banks[1]] = [t]
            row_read.append(t)
            return t

        def coled(o, banks, after):
            for b in range(2):
                t = act(o[:, b, :], PS[:, banks[b], 0:o.shape[2]], scale=col[0][:, b:b + 1], after=list(after) + row_ready)
            free[banks[0]] = free[banks[1]] = [t]
            return t

        def gain_rows(name, after):
            return Q.dma("pool", "gb", U(8), A[name].broadcast_to([P, D]), after)

        GB = U(8).rearrange("p (a n) -> p a n", a=1)

        def post_norm(M, mtoks, ssq):
            s = stat(2)
            t = red(s, ssq, ALU.add, mtoks)
            r, t = rsqrt(s, D, 2, [t])
            res = []
            for c in range(4):
                hs = slice(512 * c, 512 * c + 512)
                res.append([stt(X[:, b, hs], M[:, b, hs], r[:, b:b + 1], X[:, b, hs], ALU.mult, ALU.add,
                                [t] + mtoks) for b in range(2)])
            return res

        def token_groups(names, H, L, M, ready, d_gb, m_free, junk):
            ssq = stat(8).rearrange("p (b c) -> p b c", b=2)
            toks, last = [], [[], []]
            for c, n in enumerate(names):
                bk = unit()
                t = run(n, H, L, False, bk, (), ready if c == 0 else None)
                cs = slice(c * 512, c * 512 + 512)
                w = [t] + m_free()
                sq = lambda b, after: act(junk[b], PS[:, bk[b], :], ACT.Square, accum=ssq[:, b, c:c + 1],
                                           after=after + last[b])
                mul = lambda b, after: tt(M[:, b, cs], PS[:, bk[b], :], GB[:, 0, cs], ALU.mult, after)
                t0, v1 = sq(0, w), mul(1, w + [d_gb])
                t1, v0 = sq(1, [v1]), mul(0, [t0])
                last = [[t0], [t1]]
                free[bk[0]], free[bk[1]] = [v0], [t1]
                toks += [t1, v0]
            return ssq, toks

        al = list(range(8))
        xr = norm_t(X, d_x, AH, AL, GOFF["mix_pre_g"], al)
        rg = start_row(X, d_x, SP4, 7)

        mem_ready = []

        def mem_side():
            ss = stat(2)
            for _ in range(4):
                yield
            sq = [act(U(6 + b), MEM[:, b, :], ACT.Square, accum=ss[:, b:b + 1], after=[d_mem]) for b in range(2)]
            yield
            r, t = rsqrt(ss, D, 2, sq)
            yield
            yield
            sc = []
            for b in range(2):
                sc.append(act(MEM[:, b, :], MEM[:, b, :], scale=r[:, b:b + 1], after=[t] + sq))
                yield
            for i in range(8):
                b = 4 + i % 2
                for c in range(2):
                    for blk in range(2):
                        cc = 2 * i + c
                        t = tr(PS[:, b, c * T + blk * P:c * T + blk * P + P], MEM[:, blk, cc * P:cc * P + P],
                               sc + [d_eye] + free[b], inc=c == 1 and blk == 1)
                yield
                gm = GOFF["mem_norm_g"] + 2 * i
                t = splits([(PS[:, b, c * T:c * T + T], BH[:, 2 * i + c, :], BL[:, 2 * i + c, :],
                             GC[:, gm + c:gm + c + 1]) for c in range(2)], [t, d_gc])
                free[b] = [t]
                mem_ready.append(t)

        BIAS = U(8).rearrange("p (h n) -> p h n", h=8)
        bias_ready, lam_ready, lb_ready = [], [], []
        neglam, lb, oml = stat(1), stat(8), stat(8)

        def bias_side():
            x = stat(8), stat(8)
            yield
            yield
            t = mm(PS[0:8, 6, 0:384], U(2)[0:32, 768:776], U(2)[0:32, 0:384], True, True,
                   [d_hot, d_rel] + free[6], inc=True)
            l2 = stat(2)
            lv = U(2)[:, 776:1032].rearrange("p (a m n) -> p a m n", a=2, m=2)
            t1 = tt(lv[:, :, 0, :], lv[:, :, 0, :], lv[:, :, 1, :], ALU.mult, [d_lam])
            t1 = red(l2, lv[:, :, 0, :], ALU.add, [t1])
            lg = GC[:, GOFF["hg_lb_logits"]:GOFF["hg_lb_logits"] + 8]
            t2 = tt(x[0], lg, lg, ALU.subtract, [d_gc])
            yield
            t = tt(U(2)[0:8, 384:768], PS[0:8, 6, 0:384], U(2)[0:8, 384:768], ALU.add, [t, d_dead])
            free[6] = [t]
            d = Q.dma("pool", "scr", scratch, U(2)[0:8, 384:768], [t])
            e = stat(2)
            t1 = act(e, l2, ACT.Exp, after=[t1])
            t2 = act(x[0], x[0], ACT.Exp, after=[t2])
            yield
            t1 = tt(neglam, e[:, 1:2], e[:, 0:1], ALU.subtract, [t1])
            lam_ready.append(ts(neglam, neglam, LAM0, None, ALU.subtract, after=[t1]))
            t3 = Q.op("dve", lambda g: g.reciprocal(x[1], x[0]), [t2])
            t3 = tt(x[0], x[0], x[1], ALU.mult, [t3])
            t3 = tt(lb, x[0], x[0], ALU.subtract, [t3])
            lb_ready.append(ts(oml, lb, -1.0, 1.0, ALU.mult, ALU.add, [t3]))
            lb_ready.append(t3)
            yield
            hank = bass.AP(scratch.tensor, 0, [[1, P], [384, 8], [1, 256]])
            d = Q.dma("pool", "hank", U(3).rearrange("p (h n) -> p h n", h=8), hank, [d])
            for _ in range(5):
                yield
            ts_ = []
            for c in range(2):
                for b in (6, 7):
                    j = 2 * c + b - 6
                    t = mm(PS[:, b, :], flip, U(3)[:, 512 * j:512 * j + 512], True, True, [d, d_eye] + free[b], inc=True)
                    t = act(U(8)[:, 512 * j:512 * j + 512], PS[:, b, :], after=[t, d_mask])
                    free[b] = [t]
                    ts_.append(t)
                yield
            bias_ready.extend(ts_)

        LAM0 = 0.8 - 0.6 * float(np.exp(0.0))
        bias_g = [bias_side()]


        hv = lambda ap: ap.rearrange("p (h t) -> p h t", t=T)
        tq, tk, tv = [], [], []
        V = U(2).rearrange("p (b n) -> p b n", b=2)
        for j in range(2):
            bk = unit()
            t = run(f"q{j}", AH, AL, True, bk, (), xr if j == 0 else None)
            drain(rg)
            if j == 0:
                d_hot = Q.dma("sp", "hot", U(2)[0:32, 0:384], A["c_hot"])
                d_dead = Q.dma("sp", "dead", U(2)[0:8, 384:768], A["c_dead"])
                d_rel = Q.dma("sp", "rel", U(2)[0:32, 768:776], A["rel_bias"])
                d_lam = Q.dma("sp", "lam", U(2)[:, 776:1032], A["lambdas"].broadcast_to([P, 256]))
                d_mem = Q.dma("sp", "mem", MEM, A["mem"][0].rearrange("(b p) d -> p b d", p=P))
                d_mask = Q.dma("sp", "mask", U(8)[:, 0:1024], A["c_mask"])
                d_mask = cp(MASK[:, :, :].rearrange("p a b -> p (a b)"), U(8)[:, 0:1024], [d_mask])
                side(bias_g[0])
                side(mem_side())
            tq.append(rowed(U(0)[:, 1024 * j:1024 * j + 1024], bk, [t], 0.125))
        for j in range(2):
            bk = unit()
            t = run(f"k{j}", AH, AL, True, bk)
            tk.append(rowed(U(1)[:, 1024 * j:1024 * j + 1024], bk, [t]))
        for j in range(2):
            bk = unit()
            t = run(f"v{j}", AH, AL, False, bk)
            for g_ in bias_g:
                drain(g_)
            tv.append(coled(V[:, :, 512 * j:512 * j + 512], bk, [t] + lam_ready + bias_ready))
        drain()

        ODA = U(3).rearrange("p (b h d) -> p b h d", b=2, h=8)
        s_free, a_free, oda = [list(mem_ready), list(mem_ready)], [list(row_ready), list(row_ready)], []

        def da_head(h):
            for _ in range(3 * h):
                yield
            S = U(7)[:, 1024 * (h % 2):1024 * (h % 2) + 768].rearrange("p (m n) -> p m n", m=2)
            aT = SP4[:, 512 * (h % 2):512 * (h % 2) + 384]
            qv, kv = hv(U(0)), hv(U(1))
            done = [None, None]
            for m in range(2):
                r = slice(64 * m, 64 * m + 64)
                mm(PS[:, 4 + m, 0:256], qv[r, h, P:T], kv[r, h, :], True, True, tq + tk + free[4 + m])
                done[m] = mm(PS[:, 4 + m, 256:384], qv[r, h, 0:P], kv[r, h, 0:P], False, True, inc=True)
            yield
            Bh = BIAS[:, h:h + 1, :]
            t0 = tt(S[:, :, 0:256], PS[:, 4:6, 0:256], Bh.broadcast_to([P, 2, 256]), ALU.add,
                    done + bias_ready + s_free[h % 2])
            t1 = tt(S[:, :, 256:384], PS[:, 4:6, 256:384], Bh[:, :, P:T].broadcast_to([P, 2, P]), ALU.add, done)
            free[4] = free[5] = [t0, t1]
            nm, l, rc = stat(4), stat(4), stat(4)
            t0 = red(nm[:, 0:2], S[:, :, 0:256], ALU.max, [t0], negate=True)
            t1 = red(nm[:, 2:4], S[:, :, 256:384], ALU.max, [t1], negate=True)
            e = []
            for m in range(2):
                for c, cs, t in ((m, slice(0, 256), t0), (2 + m, slice(256, 384), t1)):
                    e.append(act(S[:, m, cs], S[:, m, cs], ACT.Exp, bias=nm[:, c:c + 1], accum=l[:, c:c + 1], after=[t]))
            yield
            yield
            t = Q.op("dve", lambda g: g.reciprocal(rc, l), e)
            t = ts(rc.rearrange("p (a m) -> p a m", m=2)[:, :, 1], rc.rearrange("p (a m) -> p a m", m=2)[:, :, 1],
                   neglam, None, ALU.mult, after=[t] + lam_ready)
            a = []
            for c, cs in ((0, slice(0, 256)), (2, slice(256, 384))):
                t1 = ts(S[:, 1, cs], S[:, 1, cs], rc[:, c + 1:c + 2], None, ALU.mult, after=[t])
                a.append(stt(S[:, 0, cs], S[:, 0, cs], rc[:, c:c + 1], S[:, 1, cs], ALU.mult, ALU.add, [t1]))
            yield
            yield
            for c in range(3):
                t = tr(PS[:, 6, c * P:c * P + P], S[:, 0, c * P:c * P + P], a + free[6], inc=c == 2)
            s_free[h % 2] = [t]
            yield
            t = act(aT, PS[:, 6, 0:384], after=[t] + a_free[h % 2])
            free[6] = [t]
            yield
            vs = slice(h * P, h * P + P)
            mm(PS[:, 7, P:T], aT[:, 0:P], V[:, 0, vs], True, False, [t] + tv + free[7])
            mm(PS[:, 7, P:T], aT[:, P:T], V[:, 1, vs], False, True)
            t = mm(PS[:, 7, 0:P], aT[:, T:384], V[:, 0, vs], False, True, inc=True)
            a_free[h % 2] = [t]
            yield
            t = cp(ODA[:, :, h, :], PS[:, 7, 0:T].rearrange("p (b d) -> p b d", b=2), [t] + bias_ready)
            free[7] = [t]
            oda.append(t)

        heads = [da_head(h) for h in range(8)]
        for s in heads:
            side(s)

        def head_norm(O, n, d, junk, after, junk_free):
            Of = O.rearrange("p n d -> p (n d)")
            t = act(junk, Of, ACT.Square, after=list(after) + list(junk_free))
            yield
            ss = stat(n)
            t = red(ss, junk.rearrange("p (n d) -> p n d", n=n), ALU.add, [t])
            r, t = rsqrt(ss, d, n, [t])
            yield
            yield
            norm_done.append(tt(O, O, r.unsqueeze(2).broadcast_to([P, n, d]), ALU.mult, [t]))

        norm_done = []

        tf, tqh, ti, tg = [], [], [], []
        KK, BB, QH, EE = U(4), U(5), U(6), U(7)
        for j in range(2):
            bk = unit()
            t = run(f"f{j}", AH, AL, True, bk)
            cs = slice(1024 * j, 1024 * j + 1024)
            t = rowed(KK[:, cs], bk, [t] + mem_ready)
            t = act(KK[:, cs], KK[:, cs], ACT.Sigmoid, after=[t])
            fs = []
            for h in range(4):
                hs = slice(1024 * j + T * h, 1024 * j + T * h + T)
                c = 4 * j + h
                fs.append(ts(KK[:, hs], KK[:, hs], oml[:, c:c + 1], lb[:, c:c + 1], ALU.mult, ALU.add, [t] + lb_ready))
            t = ts(BB[:, cs], KK[:, cs], 2.0 ** -62, None, ALU.max, after=fs)
            t = act(BB[:, cs], BB[:, cs], ACT.Ln, after=[t])
            t2 = ts(KK[:, cs], KK[:, cs], -1.0, 1.0, ALU.mult, ALU.add, fs)
            sc = []
            for h in range(2):
                hs = slice(1024 * j + 512 * h, 1024 * j + 512 * h + 512)
                sc.append(Q.op("dve", lambda g, hs=hs: g.tensor_tensor_scan(BB[:, hs], SM[:, :], BB[:, hs], 0.0,
                                                                            ALU.mult, ALU.add), [t, t_sm]))
            tf.append([t2] + sc)
        for j in range(2):
            bk = unit()
            t = run(f"qh{j}", AH, AL, True, bk)
            tqh.append(rowed(QH[:, 1024 * j:1024 * j + 1024], bk, [t] + mem_ready))

        def levels(todo, q, k, b, E, dst, cross, nu, kc, banks, escale, after, e_free, cross_free, cdone):
            blk = lambda ap, u, c, s: ap[:, (u * kc + c) * T + s * P:(u * kc + c) * T + s * P + P]
            e_busy = list(e_free)

            def products(lhs, rhs, need):
                pos = 0
                toks = {}
                for u in range(nu):
                    for s in range(2):
                        bk, o = banks[pos // 4], (pos % 4) * P
                        for c in range(kc):
                            t = mm(PS[:, bk, o:o + P], blk(lhs, u, c, s), blk(rhs, u, c, s), pos % 4 == 0 and c == 0,
                                   c == kc - 1, need + free[bk], inc=pos % 4 == 3 and c == kc - 1)
                        if t:
                            toks[bk] = t
                        pos += 1
                return toks

            def pick(toks, mi):
                for n, bk in enumerate(banks):
                    d = dst[:, 512 * n:512 * n + 512].rearrange("p (r t) -> p r t", t=P)
                    m = MASK[:, mi:mi + 1, :].broadcast_to([P, 4, P])
                    src = PS[:, bk, :].rearrange("p (r t) -> p r t", t=P)
                    t = Q.op("dve", lambda g, d=d, m=m, src=src: g.copy_predicated(d, m, src),
                             [toks[bk], d_mask] + list(after))
                    free[bk] = [t]
                    cdone.append(t)

            for L in todo:
                if L == 0:
                    yield
                    yield
                    toks = products(k, q, list(after))
                    yield
                    pick(toks, 0)
                    yield
                    continue
                w = lambda ap: ap.rearrange("p (n t) -> p n t", t=2 * L)
                bv, ev, qv, kv = w(b), w(E), w(q), w(k)
                n = bv.shape[1]
                aft = list(after) + e_busy
                ref = bv[:, :, L - 1:L].broadcast_to([P, n, L])
                t1 = tt(ev[:, :, 0:L], ref, bv[:, :, 0:L], ALU.subtract, aft)
                if L < 64:
                    t0 = tt(ev[:, :, L:2 * L], bv[:, :, L:2 * L], ref, ALU.subtract, aft)
                elif L == 64:
                    t0 = cp(ev[:, :, L:2 * L], bv[:, :, L:2 * L], aft)
                else:
                    t2 = cp(ev[:, :, P:T], bv[:, :, P:T], aft)
                    t0 = tt(ev[:, :, P + 64:T], ev[:, :, P + 64:T], bv[:, :, P + 63:P + 64].broadcast_to([P, n, 64]),
                            ALU.add, [t2])
                    t1 = tt(ev[:, :, 0:64], ev[:, :, 0:64], bv[:, :, 63:64].broadcast_to([P, n, 64]), ALU.add, [t1])
                t = act(E, E, ACT.Exp, scale=escale, after=[t0, t1])
                yield
                t0 = tt(ev[:, :, L:2 * L], ev[:, :, L:2 * L], qv[:, :, L:2 * L], ALU.mult, [t], "pool")
                t1 = tt(ev[:, :, 0:L], ev[:, :, 0:L], kv[:, :, 0:L], ALU.mult, [t])
                yield
                if L < P:
                    toks = products(E, E, [t0, t1])
                    e_busy = list(toks.values())
                    yield
                    pick(toks, 1 + LEVELS.index(L))
                    yield
                    continue
                bk = banks[0]
                for u in range(nu):
                    for c in range(kc):
                        t = mm(PS[:, bk, u * P:u * P + P], blk(E, u, c, 0), blk(E, u, c, 1), u == 0 and c == 0,
                               c == kc - 1, [t0, t1] + free[bk], inc=u == nu - 1 and c == kc - 1)
                e_busy = [t]
                yield
                t = cp(cross, PS[:, bk, 0:nu * P], [t] + list(cross_free))
                free[bk] = [t]
                cdone.append(t)
                yield

        att, att_x = U(0), SP4
        lev_done = []

        att_zero = []

        def hg_levels(j, part):
            while len(oda) < 8 or not norm_done:
                yield
            if not att_zero:
                att_zero.append(Q.op("pool", lambda g: g.memset(att, 0.0), [oda, s_free[0], s_free[1]]))
            for _ in range(2 * part):
                yield
            cs = slice(1024 * j, 1024 * j + 1024)
            yield from levels(([128, 64, 32, 16], [0, 1, 2, 4, 8])[part], QH[:, cs], KK[:, cs], BB[:, cs],
                              (EE, U(8))[part][:, cs], att[:, cs], att_x[:, 512 * j:512 * j + 512],
                              4, 1, [4 + 2 * j, 5 + 2 * j], 1.0, tqh + tf[j] + att_zero,
                              [s_free[0], s_free[1]] + norm_done, [a_free[0], a_free[1]], lev_done)

        def da_norm():
            while len(oda) < 8:
                yield
            yield from head_norm(U(3).rearrange("p (n d) -> p n d", d=P), 16, P, U(8), oda, oda)

        lev = [hg_levels(j, part) for part in range(2) for j in range(2)]
        for s in lev:
            side(s)
        dn = da_norm()
        side(dn)

        VI = U(2).rearrange("p (b n) -> p b n", b=2)
        for j in range(2):
            bk = unit()
            t = run(f"i{j}", AH, AL, False, bk)
            for h in heads:
                drain(h)
            ti.append(coled(VI[:, :, 512 * j:512 * j + 512], bk, [t] + oda))
        GT = U(1)
        for j in range(2):
            bk = unit()
            t = run(f"g{j}", AH, AL, True, bk)
            gs_ = GT[:, 1024 * j:1024 * j + 1024]
            tg.append(act(gs_, gs_, ACT.Silu, after=[rowed(gs_, bk, [t] + oda)]))
        a_free_tok = [pe_done[-1]]
        drain(dn)
        da_normed = [norm_done[-1]]
        subg = stat(1)
        t_sub = ts(subg, gcol("da_subln_g"), 1.0 - LAM0, None, ALU.mult, after=[d_gc])
        mix_ready = [None] * 16

        def da_out():
            o = U(3).rearrange("p (b h d) -> p b h d", b=2, h=8)
            for i in range(4):
                b = 4 + i % 2
                for c in range(2):
                    for blk in range(2):
                        t = tr(PS[:, b, c * T + blk * P:c * T + blk * P + P], o[:, blk, 2 * i + c, :],
                               da_normed + free[b], inc=c == 1 and blk == 1)
                yield
                hl = slice(2 * i, 2 * i + 2)
                t = split(PS[:, b, :].rearrange("p (c t) -> p c t", c=2), AH[:, hl, :], AL[:, hl, :], subg,
                          [t, t_sub] + a_free_tok)
                free[b] = [t]
                mix_ready[2 * i] = mix_ready[2 * i + 1] = t

        OHG = U(4).rearrange("p (b h d) -> p b h d", b=2, h=8)
        hg_end = []

        def hg_out():
            while any(g in sides for g in lev):
                yield
            av = att.rearrange("p (h b t) -> p h b t", h=8, b=2)
            o_t = []
            for half in range(2):
                for blk in range(2):
                    b = 6 + blk
                    for hh in range(4):
                        h = 4 * half + hh
                        o = PS[:, b, hh * P:hh * P + P]
                        vs = slice(h * P, h * P + P)
                        t = mm(o, av[:, h, blk, :], VI[:, blk, vs], hh == 0, blk == 0, lev_done + ti + free[b],
                               inc=hh == 3 and blk == 0)
                        if blk:
                            t = mm(o, att_x[:, h * P:h * P + P], VI[:, 0, vs], False, True, inc=hh == 3)
                    t2 = cp(OHG[:, blk, 4 * half:4 * half + 4, :],
                            PS[:, b, :].rearrange("p (h d) -> p h d", h=4), [t] + lev_done)
                    free[b] = [t2]
                    o_t.append(t2)
                    hg_end.append(t)
                yield
            yield from head_norm(U(4).rearrange("p (n d) -> p n d", d=P), 16, P, U(7), o_t, lev_done)
            o = OHG
            yield
            for i in range(4):
                b = 6 + i % 2
                for c in range(2):
                    for blk in range(2):
                        t = tr(PS[:, b, c * T + blk * P:c * T + blk * P + P], o[:, blk, 2 * i + c, :],
                               [norm_done[-1]] + free[b], inc=c == 1 and blk == 1)
                yield
                tmp = U(5)[:, 512 * i:512 * i + 512]
                t = stt(tmp, PS[:, b, :], gcol("hg_onorm_g"), GT[:, 512 * i:512 * i + 512], ALU.mult, ALU.mult,
                        [t] + tg + lev_done)
                free[b] = [t]
                hl = slice(8 + 2 * i, 10 + 2 * i)
                mix_ready[8 + 2 * i] = mix_ready[9 + 2 * i] = split(
                    tmp.rearrange("p (c t) -> p c t", c=2), AH[:, hl, :], AL[:, hl, :], None, [t] + a_free_tok)

        side(da_out())
        side(hg_out())

        KT, VX = U(6)[:, 0:1024], U(6)[:, 1024:2048].rearrange("p (b n) -> p b n", b=2)
        bk = unit()
        t = run("ckv0", BH, BL, True, bk, mem_ready)
        for s in lev:
            drain(s)
        tkx = act(KT, flat(bk), after=[t] + lev_done)
        free[bk[0]] = free[bk[1]] = [tkx]

        M23 = U(2, 2).rearrange("p (b d) -> p b d", b=2)
        d_gb = gain_rows("mix_post_g", norm_done + lev_done)
        SQ = [SP4[:, 0:512], SP4[:, 512:1024]]
        ssq, mt = token_groups([f"wo{c}" for c in range(4)], AH, AL, M23, mix_ready, d_gb, lambda: hg_end + mix_ready, SQ)
        xt = post_norm(M23, mt, ssq)
        xr = norm_t(X, xt, AH, AL, GOFF["cross_pre_g"], al, [pe_done[groups["wo3"][-1]]])
        rg = start_row(X, xt, SP4, 7)

        QX, PX, PT = U(7)[:, 0:1024], U(0).rearrange("p (n k) -> p n k", k=T), U(1)
        bk = unit()
        t = run("cq", AH, AL, True, bk, (), xr)
        drain(rg)
        t = rowed(QX, bk, [t] + norm_done, float(P) ** -0.5)
        t_qx, pts = t, []

        def cross():
            yield
            sc, ex = [], []
            for h in range(4):
                for blk in range(2):
                    u = mm(PS[:, 4 + h, blk * T:blk * T + T], hv(QX)[:, h, blk * P:blk * P + P], hv(KT)[:, h, :],
                           blk == 0, True, [t_qx, tkx] + free[4 + h], inc=blk == 1)
                sc.append(u)
            yield
            nm, l, rl = stat(8), stat(8), stat(8)
            for h in range(4):
                sv = PS[:, 4 + h, :].rearrange("p (b k) -> p b k", b=2)
                t = red(nm[:, 2 * h:2 * h + 2], sv, ALU.max, [sc[h]], negate=True)
                for blk in range(2):
                    n = 2 * h + blk
                    ex.append(act(PX[:, n, :], sv[:, blk, :], ACT.Exp, bias=nm[:, n:n + 1], accum=l[:, n:n + 1],
                                  after=[t] + hg_end))
                free[4 + h] = [ex[-1]]
            yield
            yield
            t = Q.op("dve", lambda g: g.reciprocal(rl, l), ex)
            pn = [tt(PX[:, 2 * h:2 * h + 2, :], PX[:, 2 * h:2 * h + 2, :],
                     rl[:, 2 * h:2 * h + 2].unsqueeze(2).broadcast_to([P, 2, T]), ALU.mult, [t]) for h in range(4)]
            yield
            yield
            for h in range(4):
                for kb in range(2):
                    for blk in range(2):
                        u = tr(PS[:, 4 + h, kb * T + blk * P:kb * T + blk * P + P],
                               PX[:, 2 * h + blk, kb * P:kb * P + P], [pn[h]] + free[4 + h], inc=kb == 1 and blk == 1)
                e = act(PT[:, 512 * h:512 * h + 512], PS[:, 4 + h, :], after=[u] + mix_ready)
                free[4 + h] = [e]
                pts.append(e)

        side(cross())
        bk = unit()
        u = run("ckv1", BH, BL, False, bk)
        tvx = act(VX, PS[:, bk[0]:bk[1] + 1, :], after=[u] + lev_done)
        free[bk[0]] = free[bk[1]] = [tvx]
        drain()
        oxr = []
        for i in range(2):
            for c in range(2):
                h = 2 * i + c
                for kb in range(2):
                    u = mm(PS[:, 4 + i, c * T:c * T + T], VX[:, kb, h * P:h * P + P],
                           PT[:, 512 * h + kb * T:512 * h + kb * T + T], c == 0 and kb == 0, kb == 1,
                           [pts[h], tvx] + free[4 + i], inc=c == 1 and kb == 1)
            e = split(PS[:, 4 + i, :].rearrange("p (c t) -> p c t", c=2), BH[:, 2 * i:2 * i + 2, :],
                      BL[:, 2 * i:2 * i + 2, :], None, [u, pe_done[groups["ckv1"][-1]]])
            free[4 + i] = [e]
            oxr += [e, e]
        d_gb = gain_rows("cross_post_g", mt)
        ssq, mt = token_groups([f"co{c}" for c in range(4)], BH, BL, M23, oxr, d_gb, lambda: row_ready, SQ)
        xt = post_norm(M23, mt, ssq)
        AH, AL, BH, BL = BH, BL, AH, AL
        xr = norm_t(X, xt, BH, BL, GOFF["ffn_pre_g"], al, [pe_done[groups["cq"][-1]]])
        rg = start_row(X, xt, SP4, 7)

        def ffn(tag, inH, inL, hidH, hidL, in_ready, post, x_toks, hid_free, rg, old_mt):
            SG = [U(0)[:, 0:1024], U(0)[:, 1024:2048]]
            SU = [U(1)[:, 0:1024], U(1)[:, 1024:2048]]
            Fa = M23
            s_free = [list(x_toks), list(x_toks)]
            d = gain_rows(post, old_mt)
            ssq = stat(8).rearrange("p (b c) -> p b c", b=2)
            mt, acc, n = [], [None] * 4, 0
            for p, (a, b) in enumerate(PARTS):
                hid = []
                for j in range(a, b):
                    g = unit(4)
                    tg_ = run(f"{tag}g{j}", inH, inL, True, g, (), in_ready if j == 0 else None)
                    drain(rg)
                    s, v = SG[n % 2], SU[n % 2]
                    tg_ = rowed(s, g, [tg_] + s_free[n % 2])
                    tg_ = act(s, s, ACT.Silu, after=[tg_])
                    u = unit(4)
                    tu = run(f"{tag}u{j}", inH, inL, True, u)
                    tu = rowed(v, u, [tu] + s_free[n % 2])
                    t = tt(s, s, v, ALU.mult, [tg_, tu])
                    hl = slice(4 * (j - a), 4 * (j - a) + 4)
                    t = split(s.rearrange("p (c t) -> p c t", c=4), hidH[:, hl, :], hidL[:, hl, :], None,
                              [t] + list(hid_free))
                    s_free[n % 2] = [t]
                    hid += [t] * 4
                    n += 1
                for c in range(4):
                    bk = unit(4)
                    t = run(f"{tag}o{p}_{c}", hidH, hidL, False, bk, (), hid if c == 0 else None)
                    cs = slice(512 * c, 512 * c + 512)
                    src = PS[:, bk[0]:bk[1] + 1, :]
                    if p == 0:
                        t = act(Fa[:, :, cs], src, after=[t] + list(x_toks))
                    else:
                        t = tt(Fa[:, :, cs], src, Fa[:, :, cs], ALU.add, [t, acc[c]])
                    free[bk[0]] = free[bk[1]] = [t]
                    acc[c] = t
                    if p == 2:
                        for k in range(2):
                            t = act(SQ[k], Fa[:, k, cs], ACT.Square, accum=ssq[:, k, c:c + 1],
                                    after=[acc[c]] + row_ready + mt[-2:])
                        mt += [t, tt(Fa[:, :, cs], Fa[:, :, cs], GB[:, :, cs].broadcast_to([P, 2, 512]), ALU.mult,
                                     [t, d], "pool" if c < 3 else "dve")]
                hid_free = [pe_done[-1]]
            return post_norm(Fa, mt, ssq), mt

        xt, mt = ffn("F", BH, BL, AH, AL, xr, "ffn_post_g", sum(xt, []), [pe_done[groups["co3"][-1]]], rg, mt)

        xr = norm_t(X, xt, BH, BL, GOFF["norm_mix_pre_2"], al, [pe_done[groups["Fu10"][-1]]])
        rg = start_row(X, xt, SP4, 7)
        old = sum(xt, []) + mt
        WP = U(8).rearrange("p (g k n) -> p g k n", g=4, k=2)
        d_wp = Q.dma("pool", "wp", WP, A["w_pool_2"][0].rearrange("g (k p) n -> p g k n", p=P), mt)
        GU = U(6)[0:16, 0:1024]
        d_gu = Q.dma("pool", "gu", GU, A["w_gate_up_2"][0], old)
        tk, tq = [], []
        for j in range(2):
            bk = unit()
            t = run(f"K{j}", BH, BL, True, bk, (), xr if j == 0 else None)
            drain(rg)
            tk.append(rowed(U(1)[:, 1024 * j:1024 * j + 1024], bk, [t] + old))
        bk = unit()
        t = run("LR", BH, BL, False, bk)
        GL = U(5)[:, 0:32 + T]
        glr = GL[:, 0:32].rearrange("p (b n) -> p b n", b=2)
        t = coled(glr, bk, [t] + old)
        G2 = U(2)
        g_ready = [[], []]
        t_glr = t

        def gate_side():
            yield
            for blk in range(2):
                t = tr(PS[0:16, 4, blk * P:blk * P + P], glr[:, blk, :], [t_glr] + free[4], inc=blk == 1)
            yield
            t = cp(GL[0:16, 32:32 + T], PS[0:16, 4, 0:T], [t])
            free[4] = [t]
            yield
            zt = []
            for c in range(8):
                u = mm(PS[:, 4 + c // 2, (c % 2) * T:(c % 2) * T + T], GU[:, c * P:c * P + P], GL[0:16, 32:32 + T],
                       c % 2 == 0, True, [t, d_gu] + free[4 + c // 2], inc=c % 2 == 1)
                if c % 2:
                    zt.append(u)
            gu_free.append(u)
            yield
            for j in range(2):
                a, m = [], []
                for c in range(4 * j, 4 * j + 4):
                    z = PS[:, 4 + c // 2, (c % 2) * T:(c % 2) * T + T]
                    cs = slice(c * T, c * T + T)
                    m.append(ts(G2[:, cs], z, gcol("b_gate_2", c), 0.0, ALU.add, ALU.min, zt + old))
                for c in range(4 * j, 4 * j + 4):
                    z = PS[:, 4 + c // 2, (c % 2) * T:(c % 2) * T + T]
                    a.append(act(U(4)[:, c * T:c * T + T], z, ACT.Abs, bias=gcol("b_gate_2", c), after=m + old))
                    free[4 + c // 2] = [a[-1]]
                hs = slice(1024 * j, 1024 * j + 1024)
                t = act(U(4)[:, hs], U(4)[:, hs], ACT.Exp, scale=-1.0, after=a)
                t = act(U(4)[:, hs], U(4)[:, hs], ACT.Ln, bias=1.0, after=[t])
                yield
                t = tt(G2[:, hs], G2[:, hs], U(4)[:, hs], ALU.subtract, [t] + m)
                u4_free.append(t)
                for k in range(2):
                    ks = slice(1024 * j + 512 * k, 1024 * j + 512 * k + 512)
                    g_ready[j].append(Q.op("dve", lambda g, ks=ks: g.tensor_tensor_scan(
                        G2[:, ks], SM[:, :], G2[:, ks], 0.0, ALU.mult, ALU.add), [t]))
                yield

        u4_free, gu_free, lev_done = [], [], []
        gs = gate_side()
        side(gs)
        for j in range(2):
            bk = unit()
            t = run(f"Q{j}", BH, BL, True, bk)
            tq.append(rowed(U(0)[:, 1024 * j:1024 * j + 1024], bk, [t] + old, 0.0625))
        ATT2 = SP4
        AX2 = SM
        att_zero = []

        def gla_levels(j):
            while gs in sides:
                yield
            if not att_zero:
                att_zero.append(Q.op("pool", lambda g: g.memset(ATT2, 0.0), old + row_ready))
            for _ in range(2 * j):
                yield
            cs = slice(1024 * j, 1024 * j + 1024)
            yield from levels([0, 1, 2, 4, 8, 16, 32, 64, 128], U(0)[:, cs], U(1)[:, cs], G2[:, cs], U(3)[:, cs],
                              ATT2[:, 512 * j:512 * j + 512], AX2[:, 256 * j:256 * j + 256], 2, 2, [6 + j], 0.0625,
                              tq + tk + g_ready[j] + att_zero, old, g_ready, lev_done)

        PP, S0, S1 = U(4), U(5), U(7)
        tp = []
        for j in range(2):
            bk = unit()
            t = run(f"P{j}", BH, BL, True, bk)
            drain(gs)
            tp.append(rowed(PP[:, 1024 * j:1024 * j + 1024], bk, [t] + u4_free))
        lev = [gla_levels(0), gla_levels(1)]
        for s in lev:
            side(s)
        pool_ready, pool_end = [], []

        def pool_side():
            pv, s0, s1 = hv(PP), hv(S0), hv(S1)
            src, prev = pv, tp + old + gu_free
            bufs = [s0, s1, s0, s1]
            res = []
            for g, w in enumerate((2, 4, 8, 16)):
                sh, c0, dst = w // 2, 2 * g, bufs[g]
                a = tt(dst[:, c0:8, sh:T], src[:, c0:8, sh:T], src[:, c0:8, 0:T - sh], ALU.add, prev)
                b = cp(dst[:, c0:8, 0:sh], src[:, c0:8, 0:sh], prev)
                src, prev = dst, [a, b]
                res.append([a, b])
                yield
            tmp = stat(32).rearrange("p (c t) -> p c t", c=2)
            early = EYE[:, 256:320]
            wt = []
            end = []
            for g, w in enumerate((2, 4, 8, 16)):
                s, cs = bufs[g], slice(2 * g, 2 * g + 2)
                cnt = early[:, 16 * g:16 * g + 16].unsqueeze(1).broadcast_to([P, 2, 16])
                a = tt(tmp, s[:, cs, 0:16], cnt, ALU.mult, res[g] + prev + end)
                b = stt(s[:, cs, :], s[:, cs, :], 1.0 / w, pv[:, cs, :], ALU.mult, ALU.subtract, [a])
                b = tt(s[:, cs, 0:16], tmp, pv[:, cs, 0:16], ALU.subtract, [b])
                end = [b]
                wt.append(b)
                yield
            for g in range(4):
                b, s = 4 + g % 2, bufs[g]
                for c in range(2):
                    for kc in range(2):
                        t = mm(PS[:, b, c * T:c * T + T], WP[:, g, kc, c * P:c * P + P], s[:, 2 * g + kc, :],
                               c == 0 and kc == 0, kc == 1, [wt[g], d_wp] + free[b], inc=c == 1 and kc == 1)
                yield
                pool_end.append(t)
                t = splits([(PS[:, b, c * T:c * T + T], AH[:, 2 * g + c, :], AL[:, 2 * g + c, :],
                             gcol("pool_scale_2", 2 * g + c)) for c in range(2)], [t, pe_done[groups["Fo2_3"][-1]]])
                free[b] = [t]
                pool_ready.append(t)

        ps_ = pool_side()
        side(ps_)
        T0 = U(6, 2)
        tt0 = []
        for j in range(4):
            bk = unit()
            t = run(f"G0{j}", BH, BL, True, bk)
            if j == 2:
                drain(ps_)
            t = rowed(T0[:, 1024 * j:1024 * j + 1024], bk, [t] + gu_free + pool_end)
            for c in range(4):
                z = T0[:, 1024 * j + T * c:1024 * j + T * c + T]
                e = act(z, z, ACT.Sigmoid, bias=gcol("b_branch_gates_2", 4 * j + c), after=[t])
            tt0.append(e)
        for j in range(4):
            bk = unit()
            t = run(f"ya{j}", AH, AL, True, bk, (), [pool_ready[k // 2] for k in range(8)] if j == 0 else None)
            ts_ = slice(1024 * j, 1024 * j + 1024)
            tt0[j] = tt(T0[:, ts_], T0[:, ts_], flat(bk), ALU.mult, [t, tt0[j]])
            free[bk[0]] = free[bk[1]] = [tt0[j]]
        for s in lev:
            drain(s)
        V2 = U(0, 2).rearrange("p (b n) -> p b n", b=2)
        tv = []
        for j in range(4):
            bk = unit()
            t = run(f"V{j}", BH, BL, False, bk)
            tv.append(coled(V2[:, :, 512 * j:512 * j + 512], bk, [t] + lev_done))
        O2 = U(4, 2).rearrange("p (b h d) -> p b h d", b=2, h=4)
        tr_, ox_ready, v_free = [], [], []

        def gla_out():
            ot = []
            for blk in range(2):
                for h in range(4):
                    vs = slice(512 * h, 512 * h + 512)
                    o = PS[:, 4 + h, :]
                    at = lambda hh, s: ATT2[:, (2 * hh + s) * P:(2 * hh + s) * P + P]
                    t = mm(o, at(h, blk), V2[:, blk, vs], True, blk == 0, lev_done + tv + free[4 + h], inc=blk == 0)
                    if blk:
                        t = mm(o, AX2[:, h * P:h * P + P], V2[:, 0, vs], False, True, inc=True)
                    v_free.append(t)
                    if h % 2:
                        e = act(O2[:, blk, h, :], o, after=[t] + pool_end + pool_ready)
                    else:
                        e = cp(O2[:, blk, h, :], o, [t] + pool_end + pool_ready)
                    free[4 + h] = [e]
                    ot.append(e)
                yield
            ss = stat(8)
            sq = []
            for n in range(8):
                sq.append(act(U(8)[:, 512 * (n % 2):512 * (n % 2) + 512], O2[:, n // 4, n % 4, :], ACT.Square,
                              accum=ss[:, n:n + 1], after=ot + pool_end + sq[-1:]))
                if n % 2:
                    yield
            r, t = rsqrt(ss, 512, 8, sq)
            yield
            yield
            of = U(4, 2).rearrange("p (n d) -> p n d", d=512)
            sc = []
            for n in range(2):
                sc.append(tt(of[:, 4 * n:4 * n + 4, :], of[:, 4 * n:4 * n + 4, :],
                             r[:, 4 * n:4 * n + 4].unsqueeze(2).broadcast_to([P, 4, 512]), ALU.mult, [t]))
                yield
            yield
            while len(tr_) < 4:
                yield
            buf_free = [sq, sq]
            for i in range(8):
                b = 4 + i % 4
                for c in range(2):
                    cc = 2 * i + c
                    for blk in range(2):
                        t = tr(PS[:, b, c * T + blk * P:c * T + blk * P + P],
                               O2[:, blk, cc // 4, (cc % 4) * P:(cc % 4) * P + P], sc + free[b], inc=c == 1 and blk == 1)
                yield
                tmp = U(8)[:, 512 * (i % 2):512 * (i % 2) + 512]
                e = []
                for c in range(2):
                    cc = 2 * i + c
                    e.append(stt(tmp[:, c * T:c * T + T], PS[:, b, c * T:c * T + T], gcol("gla_norm_2", cc % 4),
                                 RS[:, cc * T:cc * T + T], ALU.mult, ALU.mult, [t] + tr_ + buf_free[i % 2]))
                free[b] = e
                hl = slice(2 * i, 2 * i + 2)
                t = split(tmp.rearrange("p (c t) -> p c t", c=2), AH[:, hl, :], AL[:, hl, :], None,
                          e + [pe_done[groups["ya3"][-1]]])
                buf_free[i % 2] = [t]
                ox_ready.append(t)

        go = gla_out()
        side(go)
        RS = U(2, 2)
        for j in range(4):
            bk = unit()
            t = run(f"R{j}", BH, BL, True, bk)
            rs = RS[:, 1024 * j:1024 * j + 1024]
            tr_.append(act(rs, rs, ACT.Silu, after=[rowed(rs, bk, [t] + lev_done)]))
        G1 = U(0, 2)
        tg1 = []
        for j in range(4):
            bk = unit()
            t = run(f"G1{j}", BH, BL, True, bk)
            t = rowed(G1[:, 1024 * j:1024 * j + 1024], bk, [t] + v_free)
            for c in range(4):
                z = G1[:, 1024 * j + T * c:1024 * j + T * c + T]
                e = act(z, z, ACT.Sigmoid, bias=gcol("b_branch_gates_2", 16 + 4 * j + c), after=[t])
            tg1.append(e)
        drain()
        hb_free = [pe_done[-1]]
        mr = []
        for j in range(4):
            bk = unit()
            t = run(f"yb{j}", AH, AL, True, bk, (), [ox_ready[k // 2] for k in range(16)] if j == 0 else None)
            ts_ = slice(1024 * j, 1024 * j + 1024)
            t = tt(G1[:, ts_], G1[:, ts_], flat(bk), ALU.mult, [t, tg1[j]])
            free[bk[0]] = free[bk[1]] = [t]
            t = tt(G1[:, ts_], G1[:, ts_], T0[:, ts_], ALU.add, [t, tt0[j]])
            mr.append(split(G1[:, ts_].rearrange("p (c t) -> p c t", c=4), BH[:, 4 * j:4 * j + 4, :],
                            BL[:, 4 * j:4 * j + 4, :], None, [t] + hb_free))
        d_gb = gain_rows("norm_mix_post_2", ox_ready)
        ssq, mt = token_groups([f"W{c}" for c in range(4)], BH, BL, M23, [mr[k // 4] for k in range(16)], d_gb,
                               lambda: ox_ready + v_free, SQ)
        xt = post_norm(M23, mt, ssq)
        xr = norm_t(X, xt, AH, AL, GOFF["norm_ffn_pre_2"], al, [pe_done[groups["yb3"][-1]]])
        rg = start_row(X, xt, SP4, 7)
        xt, mt = ffn("H", AH, AL, BH, BL, xr, "norm_ffn_post_2", sum(xt, []), [pe_done[groups["W3"][-1]]], rg, mt)
        ov = out[0].rearrange("(b p) d -> p b d", p=P)
        ends = []
        for c in range(4):
            for b in range(2):
                hs = slice(512 * c, 512 * c + 512)
                ends.append(Q.dma("sp" if b else "act", f"out{c}{b}", ov[:, b, hs], X[:, b, hs], [xt[c][b]]))
        Q.wait("sp", ends)

        block = ctx.enter_context(nc.Block())

        @block.sync
        def _(g):
            Q.play("sp", g)

        @block.scalar
        def _(g):
            Q.play("act", g)

        @block.vector
        def _(g):
            Q.play("dve", g)

        @block.gpsimd
        def _(g):
            Q.play("pool", g)

        @block.tensor
        def _(g):
            Q.play("pe", g)


RAWS = ["x", "mem", "w_in", "w_out", "w_cq", "w_ckv", "w_co", "w_ffn_in", "w_ffn_out", "rel_bias", "w_in_2",
        "w_gate_up_2", "w_pool_2", "w_branch_a_2", "w_branch_b_2", "w_out_2", "w_ffn_gate_2", "w_ffn_up_2",
        "w_ffn_down_2", "mix_post_g", "cross_post_g", "ffn_post_g", "norm_mix_post_2", "norm_ffn_post_2"]


def kernel(**inputs):
    import concourse.bacc as bacc
    from concourse.bass_utils import run_bass_kernel_spmd

    f = {n: np.ascontiguousarray(a) for n, a in inputs.items()}
    arrays = {n: f[n] for n in RAWS}
    cols = []
    for n in GAINS:
        cols.append(f[n].reshape(-1, P).T)
    arrays["gains"] = np.ascontiguousarray(np.concatenate(cols, 1))
    arrays["lambdas"] = np.ascontiguousarray(np.concatenate(
        [f[n].reshape(1, 64) for n in ("lambda_q1", "lambda_k1", "lambda_q2", "lambda_k2")], 1))
    arrays.update(shape_constants())
    nc = bacc.Bacc("TRN2", target_bir_lowering=False, num_devices=1)
    A = {n: nc.dram_tensor("in_" + n, a.shape, mybir.dt.from_np(a.dtype), kind="ExternalInput").ap()
         for n, a in arrays.items()}
    out = nc.dram_tensor("out_x", (1, T, D), F32, kind="ExternalOutput").ap()
    scratch = nc.dram_tensor("scratch", (8, 384), F32, kind="Internal").ap()
    build(nc, A, out, scratch)
    r = run_bass_kernel_spmd(nc, [{"in_" + n: a for n, a in arrays.items()}], core_ids=[0])
    return r.results[0]["out_x"]
```

```python
from contextlib import ExitStack

import numpy as np

import concourse.bass as bass
from concourse import mybir

F32 = mybir.dt.float32
F32R = mybir.dt.float32r
U8 = mybir.dt.uint8
ACT = mybir.ActivationFunctionType
ALU = mybir.AluOpType
AXX = mybir.AxisListType.X
P = 128
D = 2048
T = 256
FF = 5632
EPS = 1e-6

GAINS = ["mix_pre_g", "cross_pre_g", "mem_norm_g", "ffn_pre_g", "norm_mix_pre_2", "norm_ffn_pre_2",
         "b_gate_2", "pool_scale_2", "b_branch_gates_2", "hg_lb_logits", "da_subln_g", "hg_onorm_g", "gla_norm_2"]
GCOLS = [16, 16, 16, 16, 16, 16, 8, 8, 32, 8, 1, 1, 4]
GOFF = {n: sum(GCOLS[:i]) for i, n in enumerate(GAINS)}
NGC = sum(GCOLS)
LEVELS = [1, 2, 4, 8, 16, 32, 64]


def shape_constants():
    i = np.arange(P)
    ident = np.eye(P, dtype=np.float32)
    flip = np.ascontiguousarray(ident[::-1])
    m = np.arange(384)
    dist = np.maximum(255 - m, 0)
    nf = np.maximum(dist, 1).astype(np.float32)
    large = 16 + (np.log(nf / np.float32(16)) / np.float32(np.log(8.0)) * np.float32(16)).astype(np.int32)
    bucket = np.where(dist < 16, dist, np.minimum(large, 31))
    onehot = ((bucket[None, :] == np.arange(32)[:, None]) & (m[None, :] <= 255)).astype(np.float32)
    dead = np.broadcast_to(np.where(m > 255, -1e30, 0.0).astype(np.float32), (8, 384))
    masks = [i[:, None] == i[None, :]]
    for L in LEVELS:
        s, t = i[:, None], i[None, :]
        masks.append((s // (2 * L) == t // (2 * L)) & (s % (2 * L) < L) & (t % (2 * L) >= L))
    masks = np.stack(masks, 1).astype(np.float32)
    counts = np.stack([1.0 / np.minimum(np.arange(16) + 1, w) for w in (2, 4, 8, 16)])
    counts = np.broadcast_to(counts.astype(np.float32).reshape(1, 64), (P, 64))
    return {"c_eye": np.concatenate([ident, flip, counts], 1).astype(np.float32),
            "c_hot": np.ascontiguousarray(onehot), "c_dead": np.ascontiguousarray(dead),
            "c_mask": np.ascontiguousarray(masks.reshape(P, 8 * P))}


class Queues:

    def __init__(self, nc, ctx):
        self.nc, self.ctx = nc, ctx
        self.q = {e: [] for e in ("pe", "act", "dve", "pool", "sp")}
        self.sem = {e: ctx.enter_context(nc.semaphore("s_" + e)) for e in ("pe", "act", "dve", "pool")}
        self.n = {e: 0 for e in self.sem}
        self.told = {e: {} for e in self.q}

    def wait(self, e, after):
        need = {}
        for t in after:
            if isinstance(t, list):
                for u in t:
                    need[u[0]] = max(need.get(u[0], 0), u[1])
            elif t is not None:
                need[t[0]] = max(need.get(t[0], 0), t[1])
        for k, v in need.items():
            if self.told[e].get(k, 0) < v:
                self.told[e][k] = v
                self.q[e].append(("wait", k, v))

    def op(self, e, fn, after=(), inc=True):
        self.wait(e, after)
        if inc:
            self.n[e] += 1
        self.q[e].append(("op", fn, inc))
        return (e, self.n[e]) if inc else None

    def dma(self, e, name, out, in_, after=()):
        if name not in self.sem:
            self.sem[name] = self.ctx.enter_context(self.nc.semaphore("d_" + name))
            self.n[name] = 0
        self.wait(e, after)
        self.n[name] += 16
        self.q[e].append(("dma", lambda g: g.dma_start(out, in_), name))
        return (name, self.n[name])

    def play(self, e, g):
        for it in self.q[e]:
            if it[0] == "wait":
                g.wait_ge(self.sem[it[1]], it[2])
            elif it[0] == "dma":
                it[1](g).then_inc(self.sem[it[2]], 16)
            else:
                i = it[1](g)
                if it[2]:
                    i.then_inc(self.sem[e], 1)


def build(nc, A, out, scratch):
    ctx = ExitStack()
    with ctx:
        Q = Queues(nc, ctx)

        def sb(name, shape, dt=F32):
            return ctx.enter_context(nc.sbuf_tensor(name, shape, dt))

        NR, NH = 3, 4
        LA = NH - 1
        RAW = sb("RAW", [P, NR, 1024])
        RH = sb("RH", [P, NH, 1024], F32R)
        RL = sb("RL", [P, NH, 1024], F32R)
        AH, AL = sb("AH", [P, 16, T], F32R), sb("AL", [P, 16, T], F32R)
        BH, BL = sb("BH", [P, 16, T], F32R), sb("BL", [P, 16, T], F32R)
        X = sb("X", [P, 2, D])
        AR = sb("AR", [P, 9 * 2048])
        SP4 = sb("SP4", [P, 1024])[:, :]
        EYE = sb("EYE", [P, 320])
        MASK = sb("MASK", [P, 8, P], U8)
        GC = sb("GC", [P, NGC])
        ST = sb("ST", [P, 448])
        SM = sb("SM", [P, 512])
        RR = sb("RR", [P, 1, T])
        PS = ctx.enter_context(nc.psum_tensor("PS", [P, 8, 512], F32))
        ident, flip = EYE[:, 0:P], EYE[:, P:2 * P]

        def U(k, n=1):
            return AR[:, k * 2048:(k + n) * 2048]

        def gcol(name, c=0):
            return GC[:, GOFF[name] + c:GOFF[name] + c + 1]

        used = [0]

        def stat(n):
            used[0] += n
            assert used[0] <= 448
            return ST[:, used[0] - n:used[0]]

        def act(o, i, f=ACT.Copy, scale=1.0, bias=0.0, accum=None, after=()):
            return Q.op("act", lambda g: g.activation(o, i, f, bias=bias, scale=scale, accum_out=accum), after)

        def tt(o, a, b, f, after=(), e="dve"):
            return Q.op(e, lambda g: g.tensor_tensor(o, a, b, f), after)

        def ts(o, a, s1, s2, f0, f1=None, after=(), e="dve"):
            if f1 is None:
                return Q.op(e, lambda g: g.tensor_scalar(o, a, s1, None, f0), after)
            return Q.op(e, lambda g: g.tensor_scalar(o, a, s1, s2, f0, f1), after)

        def stt(o, a, s, b, f0, f1, after=()):
            return Q.op("dve", lambda g: g.scalar_tensor_tensor(o, a, s, b, f0, f1), after)

        def red(o, i, f, after=(), negate=False):
            return Q.op("dve", lambda g: g.tensor_reduce(o, i, AXX, f, negate=negate), after)

        def cp(o, i, after=(), e="dve"):
            return Q.op(e, lambda g: g.tensor_copy(o, i), after)

        def mm(o, l, r, start, stop, after=(), inc=False):
            return Q.op("pe", lambda g: g.matmul(o, l, r, start=start, stop=stop, skip_group_check=True), after, inc)

        def tr(o, i, after=(), inc=False):
            return Q.op("pe", lambda g: g.transpose(o, i, ident), after, inc)

        def split(src, h, l, scale=None, after=()):
            if scale is None:
                t = act(h, src, after=after)
                return tt(l, src, h.bitcast(F32), ALU.subtract, [t])
            t = act(h, src, scale=scale, after=after)
            return stt(l, src, scale, h.bitcast(F32), ALU.mult, ALU.subtract, [t])

        def splits(parts, after=()):
            for src, h, l, scale in parts:
                t = act(h, src, scale=scale, after=after)
            for src, h, l, scale in parts:
                u = stt(l, src, scale, h.bitcast(F32), ALU.mult, ALU.subtract, [t])
            return u

        def rsqrt(ss, n, k, after):
            a, b = stat(k), stat(k)
            t = ts(a, ss, 1.0 / n, EPS, ALU.mult, ALU.add, after)
            return b, tt(b, a, NEG[:, 0:k], ALU.pow, [t], "pool")

        free = {b: [] for b in range(8)}

        slots, groups = [], {}

        def group(name, w, k0, nk, c0, nc_=512):
            per = min(nk, 1024 // nc_)
            ids = []
            for k in range(k0, k0 + nk, per):
                src = w[k * P:(k + per) * P, c0:c0 + nc_].rearrange("(k p) n -> p k n", p=P)
                ids.append(len(slots))
                slots.append((src, per, nc_))
            groups[name] = ids

        w_in, w_in2 = A["w_in"][0], A["w_in_2"][0]
        IN = {"q": 0, "k": 1024, "v": 2048, "f": 3072, "qh": 4096, "i": 5120, "g": 6144}
        for n in ("q0", "k0", "v0", "q1", "k1", "v1", "f0", "qh0", "f1", "qh1", "i0", "i1", "g0", "g1"):
            group(n, w_in, 0, 16, IN[n[:-1]] + 512 * int(n[-1]))
        group("ckv0", A["w_ckv"][0], 0, 16, 0)
        for j in range(4):
            group(f"wo{j}", A["w_out"][0], 0, 16, 512 * j)
        group("cq", A["w_cq"][0], 0, 16, 0)
        group("ckv1", A["w_ckv"][0], 0, 16, 512)
        for j in range(4):
            group(f"co{j}", A["w_co"][0], 0, 4, 512 * j)
        PARTS = [(0, 4), (4, 8), (8, 11)]

        def ffn_groups(tag, wg, wu, wo):
            for p, (a, b) in enumerate(PARTS):
                for j in range(a, b):
                    group(f"{tag}g{j}", wg, 0, 16, 512 * j)
                    group(f"{tag}u{j}", wu, 0, 16, 512 * j)
                for c in range(4):
                    group(f"{tag}o{p}_{c}", wo, 4 * a, 4 * (b - a), 512 * c)

        ffn_groups("F", A["w_ffn_in"][0][:, 0:FF], A["w_ffn_in"][0][:, FF:2 * FF], A["w_ffn_out"][0])
        group("K0", w_in2, 0, 16, 2048)
        group("LR", w_in2, 0, 16, 5120, 16)
        group("K1", w_in2, 0, 16, 2048 + 512)
        for j in range(2):
            group(f"Q{j}", w_in2, 0, 16, 1024 + 512 * j)
        for j in range(2):
            group(f"P{j}", w_in2, 0, 16, 512 * j)
        for j in range(4):
            group(f"G0{j}", w_in2, 0, 16, 7184 + 512 * j)
        for j in range(4):
            group(f"ya{j}", A["w_branch_a_2"][0], 0, 8, 512 * j)
        for j in range(4):
            group(f"V{j}", w_in2, 0, 16, 3072 + 512 * j)
        for j in range(4):
            group(f"R{j}", w_in2, 0, 16, 5136 + 512 * j)
        for j in range(4):
            group(f"G1{j}", w_in2, 0, 16, 9232 + 512 * j)
        for j in range(4):
            group(f"yb{j}", A["w_branch_b_2"][0], 0, 16, 512 * j)
        for j in range(4):
            group(f"W{j}", A["w_out_2"][0], 0, 16, 512 * j)
        ffn_groups("H", A["w_ffn_gate_2"][0], A["w_ffn_up_2"][0], A["w_ffn_down_2"][0])

        raw_read, lo_done, pe_done = [], [], []
        busy = [n for n in groups if n[0] in "fiKQP" or n[:2] in ("qh", "g0", "g1")]
        on_pool = {i for n in busy for i in groups[n] if i % 3 == 0}
        on_pool |= {i for n in ("q0", "cq", "co0", "co1", "Fg0", "K0", "Hg0") for i in groups[n][1:2]}

        def ensure(n):
            while len(lo_done) <= min(n, len(slots) - 1):
                i = len(lo_done)
                src, per, w = slots[i]
                r, h = i % NR, i % NH
                m = per * w
                t = Q.dma("sp", f"w{r}", RAW[:, r, 0:m].rearrange("p (k n) -> p k n", k=per), src,
                          [raw_read[i - NR]] if i >= NR else [])
                th = act(RH[:, h, 0:m], RAW[:, r, 0:m], after=[t] + ([pe_done[i - NH]] if i >= NH else []))
                tl = tt(RL[:, h, 0:m], RAW[:, r, 0:m], RH[:, h, 0:m].bitcast(F32), ALU.subtract, [th],
                        "pool" if i in on_pool else "dve")
                raw_read.append(tl)
                lo_done.append(tl)

        sides = []

        def rest(n):
            for _ in range(n):
                yield

        def pump():
            for s in list(sides):
                if next(s, "end") == "end":
                    sides.remove(s)

        def side(s):
            sides.append(s)

        def drain(s=None):
            while (s in sides) if s is not None else sides:
                pump()

        def run(name, H, L, feature, banks, after=(), ready=None):
            ids = groups[name]
            last = None
            first = list(after) + [free[b] for b in banks]
            k = 0
            for si in ids:
                ensure(si + LA)
                _, per, w = slots[si]
                h = si % NH
                hi = RH[:, h, 0:per * w].rearrange("p (k n) -> p k n", k=per)
                lo = RL[:, h, 0:per * w].rearrange("p (k n) -> p k n", k=per)
                need = first + [lo_done[si]]
                first = []
                for j in range(per):
                    s0 = k == 0
                    if ready:
                        while ready[k] is None:
                            pump()
                        need = need + [ready[k]]
                    fin = si == ids[-1] and j == per - 1
                    if feature and w < P:
                        o = PS[0:w, banks[0], 0:T]
                        mm(o, lo[:, j, :], H[:, k, :], s0, False, need)
                        need = []
                        mm(o, hi[:, j, :], H[:, k, :], False, False)
                        last = mm(o, hi[:, j, :], L[:, k, :], False, fin, inc=j == per - 1)
                    elif feature:
                        for c in range(4):
                            o = PS[:, banks[c // 2], (c % 2) * T:(c % 2) * T + T]
                            cs = slice(c * P, c * P + P)
                            mm(o, lo[:, j, cs], H[:, k, :], s0 and c % 2 == 0, False, need)
                            need = []
                            mm(o, hi[:, j, cs], H[:, k, :], False, False)
                            last = mm(o, hi[:, j, cs], L[:, k, :], False, fin, inc=j == per - 1 and c == 3)
                    else:
                        for b in range(2):
                            o = PS[:, banks[b], 0:w]
                            bs = slice(b * P, b * P + P)
                            mm(o, L[:, k, bs], hi[:, j, :], s0, False, need)
                            need = []
                            mm(o, H[:, k, bs], lo[:, j, :], False, False)
                            last = mm(o, H[:, k, bs], hi[:, j, :], False, fin, inc=j == per - 1 and b == 1)
                    k += 1
                    if j == per - 1:
                        pe_done.append(last)
                    if per == 2 or j == per - 1:
                        pump()
            return last

        turn = [0]

        def unit(n=2):
            b = 2 * (turn[0] % n)
            turn[0] += 1
            return [b, b + 1]

        def flat(banks):
            return PS[:, banks[0]:banks[1] + 1, :].rearrange("p b n -> p (b n)")

        d_eye = Q.dma("act", "eye", EYE[:, :], A["c_eye"])
        d_gc = Q.dma("act", "gc", GC[:, :], A["gains"])
        xv = A["x"][0].rearrange("(b p) d -> p b d", p=P)
        d_x = [[Q.dma("sp", f"x{c}{b}", X[:, b, 512 * c:512 * c + 512], xv[:, b, 512 * c:512 * c + 512])
                for b in range(2)] for c in range(4)]
        MEM = U(4, 2).rearrange("p (b d) -> p b d", b=2)

        NEG = sb("NEG", [P, 16])
        Q.op("pool", lambda g: g.memset(NEG[:, :], -0.5))
        t = Q.op("pool", lambda g: g.memset(SM[:, :], 1.0))
        t_sm = Q.op("pool", lambda g: g.memset(SM[:, :].rearrange("p (a b) -> p a b", b=64)[:, :, 0:1], 0.0), after=[t])

        def norm_t(src, src_toks, H, L, gain, banks, dst_free=()):
            done = []
            for i in range(8):
                b = banks[i % len(banks)]
                if i == 2:
                    ensure(len(pe_done) + 1)
                for blk in range(2):
                    for c in range(2):
                        cc = 2 * i + c
                        t = tr(PS[:, b, c * T + blk * P:c * T + blk * P + P], src[:, blk, cc * P:cc * P + P],
                               [src_toks[i // 2][blk], d_eye] + free[b], inc=c == 1 and blk == 1)
                t = splits([(PS[:, b, c * T:c * T + T], H[:, 2 * i + c, :], L[:, 2 * i + c, :],
                             GC[:, gain + 2 * i + c:gain + 2 * i + c + 1]) for c in range(2)],
                           [t, d_gc] + list(dst_free))
                done += [t, t]
                free[b] = [t]
            return done

        row_ready, row_read, col = [], [], [None]

        def row_scale(src, src_toks, junk, bank):
            ss = stat(4).rearrange("p (b h) -> p b h", b=2)
            sq = []
            for half in range(2):
                for b in range(2):
                    hs = slice(1024 * half, 1024 * half + 1024)
                    sq.append(act(junk, src[:, b, hs], ACT.Square, accum=ss[:, b, half:half + 1],
                                  after=src_toks[2 * half] + src_toks[2 * half + 1] + sq[-1:]))
                yield
            yield
            s = stat(2)
            t = red(s, ss, ALU.add, sq)
            r, t = rsqrt(s, D, 2, [t])
            yield from rest(3)
            w = junk[:, 0:T].rearrange("p (b n) -> p b n", b=2)
            t = act(w, r.unsqueeze(2).broadcast_to([P, 2, P]), after=[t] + sq)
            yield from rest(4)
            for b in range(2):
                u = tr(PS[:, bank, b * P:b * P + P], w[:, b, :], [t, d_eye] + free[bank], inc=b == 1)
            yield
            u = act(RR[:, 0, :], PS[:, bank, 0:T], after=[u] + row_read)
            free[bank] = [u]
            col[0] = r
            row_ready[:] = [t, u]
            row_read.clear()

        def start_row(src, src_toks, junk, bank):
            row_ready.clear()
            g = row_scale(src, src_toks, junk, bank)
            side(g)
            return g

        def rowed(o, banks, after, k=None):
            src = flat(banks).rearrange("p (c t) -> p c t", t=T)
            o = o.rearrange("p (c t) -> p c t", t=T)
            r = RR[:, 0:1, :].broadcast_to([P, 4, T])
            if k is None:
                t = tt(o, src, r, ALU.mult, list(after) + row_ready)
            else:
                t = stt(o, src, k, r, ALU.mult, ALU.mult, list(after) + row_ready)
            free[banks[0]] = free[banks[1]] = [t]
            row_read.append(t)
            return t

        def coled(o, banks, after):
            for b in range(2):
                t = act(o[:, b, :], PS[:, banks[b], 0:o.shape[2]], scale=col[0][:, b:b + 1], after=list(after) + row_ready)
            free[banks[0]] = free[banks[1]] = [t]
            return t

        def gain_rows(name, after):
            return Q.dma("pool", "gb", U(8), A[name].broadcast_to([P, D]), after)

        GB = U(8).rearrange("p (a n) -> p a n", a=1)

        def post_norm(M, mtoks, ssq, last=None):
            s = stat(2)
            t = red(s, ssq, ALU.add, mtoks)
            r, t = rsqrt(s, D, 2, [t])
            res = []
            for c in range(4):
                if c == 3 and last:
                    mtoks.append(last())
                hs = slice(512 * c, 512 * c + 512)
                res.append([])
                for b in range(2):
                    x, m = X[:, b, hs], M[:, b, hs]
                    if c < 2:
                        res[c].append(stt(x, m, r[:, b:b + 1], x, ALU.mult, ALU.add, [t] + mtoks))
                    else:
                        u = act(m, m, scale=r[:, b:b + 1], after=[t] + mtoks)
                        res[c].append(tt(x, m, x, ALU.add, [u], "pool"))
            return res

        def token_groups(names, H, L, M, ready, d_gb, m_free, junk):
            ssq = stat(8).rearrange("p (b c) -> p b c", b=2)
            toks, last = [], [[], []]
            for c, n in enumerate(names):
                bk = unit()
                t = run(n, H, L, False, bk, (), ready if c == 0 else None)
                cs = slice(c * 512, c * 512 + 512)
                w = [t] + m_free()
                sq = lambda b, after: act(junk[b], PS[:, bk[b], :], ACT.Square, accum=ssq[:, b, c:c + 1],
                                           after=after + last[b])
                mul = lambda b, after: tt(M[:, b, cs], PS[:, bk[b], :], GB[:, 0, cs], ALU.mult, after)
                t0, v1 = sq(0, w), mul(1, w + [d_gb])
                t1, v0 = sq(1, [v1]), mul(0, [t0])
                last = [[t0], [t1]]
                free[bk[0]], free[bk[1]] = [v0], [t1]
                toks += [t1, v0]
            return ssq, toks

        al = list(range(8))
        xr = norm_t(X, d_x, AH, AL, GOFF["mix_pre_g"], al)
        rg = start_row(X, d_x, SP4, 7)

        mem_ready = []

        def mem_side():
            ss = stat(2)
            mv = A["mem"][0].rearrange("(b p) d -> p b d", p=P)
            d_mem = [[], []]
            for b in range(2):
                for c in range(2):
                    hs = slice(1024 * c, 1024 * c + 1024)
                    d_mem[b].append(Q.dma("sp", f"mem{b}{c}", MEM[:, b, hs], mv[:, b, hs]))
                    yield from rest(2)
            yield from rest(2)
            sq = []
            for b in range(2):
                sq.append(act(U(6 + b), MEM[:, b, :], ACT.Square, accum=ss[:, b:b + 1], after=d_mem[b]))
                yield from rest(2)
            r, t = rsqrt(ss, D, 2, sq)
            yield
            yield
            sc = []
            for b in range(2):
                sc.append(act(MEM[:, b, :], MEM[:, b, :], scale=r[:, b:b + 1], after=[t] + sq))
                yield
                yield
            for i in range(8):
                b = 4 + i % 2
                for c in range(2):
                    for blk in range(2):
                        cc = 2 * i + c
                        t = tr(PS[:, b, c * T + blk * P:c * T + blk * P + P], MEM[:, blk, cc * P:cc * P + P],
                               sc + [d_eye] + free[b], inc=c == 1 and blk == 1)
                yield
                gm = GOFF["mem_norm_g"] + 2 * i
                t = splits([(PS[:, b, c * T:c * T + T], BH[:, 2 * i + c, :], BL[:, 2 * i + c, :],
                             GC[:, gm + c:gm + c + 1]) for c in range(2)], [t, d_gc])
                free[b] = [t]
                mem_ready.append(t)

        BIAS = U(8).rearrange("p (h n) -> p h n", h=8)
        bias_ready, lam_ready, lb_ready = [], [], []
        neglam, lb, oml = stat(1), stat(8), stat(8)

        def bias_side():
            x = stat(8), stat(8)
            yield
            yield
            t = mm(PS[0:8, 6, 0:384], U(2)[0:32, 768:776], U(2)[0:32, 0:384], True, True,
                   [d_hot, d_rel] + free[6], inc=True)
            l2 = stat(2)
            lv = U(2)[:, 776:1032].rearrange("p (a m n) -> p a m n", a=2, m=2)
            t1 = tt(lv[:, :, 0, :], lv[:, :, 0, :], lv[:, :, 1, :], ALU.mult, [d_lam])
            t1 = red(l2, lv[:, :, 0, :], ALU.add, [t1])
            lg = GC[:, GOFF["hg_lb_logits"]:GOFF["hg_lb_logits"] + 8]
            t2 = tt(x[0], lg, lg, ALU.subtract, [d_gc])
            yield
            t = tt(U(2)[0:8, 384:768], PS[0:8, 6, 0:384], U(2)[0:8, 384:768], ALU.add, [t, d_dead])
            free[6] = [t]
            d = Q.dma("pool", "scr", scratch, U(2)[0:8, 384:768], [t])
            e = stat(2)
            t1 = act(e, l2, ACT.Exp, after=[t1])
            t2 = act(x[0], x[0], ACT.Exp, after=[t2])
            yield
            t1 = tt(neglam, e[:, 1:2], e[:, 0:1], ALU.subtract, [t1])
            lam_ready.append(ts(neglam, neglam, LAM0, None, ALU.subtract, after=[t1]))
            t3 = Q.op("dve", lambda g: g.reciprocal(x[1], x[0]), [t2])
            t3 = tt(x[0], x[0], x[1], ALU.mult, [t3])
            t3 = tt(lb, x[0], x[0], ALU.subtract, [t3])
            lb_ready.append(ts(oml, lb, -1.0, 1.0, ALU.mult, ALU.add, [t3]))
            lb_ready.append(t3)
            yield
            hank = bass.AP(scratch.tensor, 0, [[1, P], [384, 8], [1, 256]])
            d = Q.dma("pool", "hank", U(3).rearrange("p (h n) -> p h n", h=8), hank, [d])
            yield from rest(13)
            ts_ = []
            for c in range(2):
                for b in (6, 7):
                    j = 2 * c + b - 6
                    t = mm(PS[:, b, :], flip, U(3)[:, 512 * j:512 * j + 512], True, True, [d, d_eye] + free[b], inc=True)
                    t = act(U(8)[:, 512 * j:512 * j + 512], PS[:, b, :], after=[t, d_mask])
                    free[b] = [t]
                    ts_.append(t)
                yield
            bias_ready.extend(ts_)

        LAM0 = 0.8 - 0.6 * float(np.exp(0.0))
        bias_g = [bias_side()]


        hv = lambda ap: ap.rearrange("p (h t) -> p h t", t=T)
        tq, tk, tv = [], [], []
        V = U(2).rearrange("p (b n) -> p b n", b=2)

        ODA = U(3).rearrange("p (b h d) -> p b h d", b=2, h=8)
        s_free, a_free, oda = [mem_ready, mem_ready], [row_ready, row_ready], []

        def da_head(h):
            yield from rest((8, 7)[h // 4] * (h % 4))
            S = U(7)[:, 1024 * (h % 2):1024 * (h % 2) + 768].rearrange("p (m n) -> p m n", m=2)
            aT = SP4[:, 512 * (h % 2):512 * (h % 2) + 384]
            qv, kv = hv(U(0)), hv(U(1))
            done = [None, None]
            for m in range(2):
                r = slice(64 * m, 64 * m + 64)
                mm(PS[:, 4 + m, 0:256], qv[r, h, P:T], kv[r, h, :], True, True, [tq[h // 4], tk[h // 4]] + free[4 + m])
                done[m] = mm(PS[:, 4 + m, 256:384], qv[r, h, 0:P], kv[r, h, 0:P], False, True, inc=True)
            yield
            Bh = BIAS[:, h:h + 1, :]
            t0 = tt(S[:, :, 0:256], PS[:, 4:6, 0:256], Bh.broadcast_to([P, 2, 256]), ALU.add,
                    done + bias_ready + s_free[h % 2])
            t1 = tt(S[:, :, 256:384], PS[:, 4:6, 256:384], Bh[:, :, P:T].broadcast_to([P, 2, P]), ALU.add, done)
            free[4] = free[5] = [t0, t1]
            nm, l, rc = stat(4), stat(4), stat(4)
            t0 = red(nm[:, 0:2], S[:, :, 0:256], ALU.max, [t0], negate=True)
            t1 = red(nm[:, 2:4], S[:, :, 256:384], ALU.max, [t1], negate=True)
            yield from rest(2)
            e = []
            for m in range(2):
                for c, cs, t in ((m, slice(0, 256), t0), (2 + m, slice(256, 384), t1)):
                    e.append(act(S[:, m, cs], S[:, m, cs], ACT.Exp, bias=nm[:, c:c + 1], accum=l[:, c:c + 1], after=[t]))
            yield from rest(3)
            t = Q.op("dve", lambda g: g.reciprocal(rc, l), e)
            t = ts(rc.rearrange("p (a m) -> p a m", m=2)[:, :, 1], rc.rearrange("p (a m) -> p a m", m=2)[:, :, 1],
                   neglam, None, ALU.mult, after=[t] + lam_ready)
            a = []
            for c, cs in ((0, slice(0, 256)), (2, slice(256, 384))):
                t1 = ts(S[:, 1, cs], S[:, 1, cs], rc[:, c + 1:c + 2], None, ALU.mult, after=[t])
                a.append(stt(S[:, 0, cs], S[:, 0, cs], rc[:, c:c + 1], S[:, 1, cs], ALU.mult, ALU.add, [t1]))
            yield from rest(5)
            for c in range(3):
                t = tr(PS[:, 6, c * P:c * P + P], S[:, 0, c * P:c * P + P], a + free[6], inc=c == 2)
            s_free[h % 2] = [t]
            yield
            t = act(aT, PS[:, 6, 0:384], after=[t] + a_free[h % 2])
            free[6] = [t]
            yield
            vs = slice(h * P, h * P + P)
            mm(PS[:, 7, P:T], aT[:, 0:P], V[:, 0, vs], True, False, [t, tv[h // 4]] + free[7])
            mm(PS[:, 7, P:T], aT[:, P:T], V[:, 1, vs], False, True)
            t = mm(PS[:, 7, 0:P], aT[:, T:384], V[:, 0, vs], False, True, inc=True)
            a_free[h % 2] = [t]
            yield
            t = cp(ODA[:, :, h, :], PS[:, 7, 0:T].rearrange("p (b d) -> p b d", b=2), [t] + bias_ready)
            free[7] = [t]
            oda.append(t)

        heads = [da_head(h) for h in range(8)]

        def heads_go(half):
            for h in range(4 * half, 4 * half + 4):
                side(heads[h])

        for j in range(2):
            bk = unit()
            t = run(f"q{j}", AH, AL, True, bk, (), xr if j == 0 else None)
            if j == 0:
                drain(rg)
                d_hot = Q.dma("sp", "hot", U(2)[0:32, 0:384], A["c_hot"])
                d_dead = Q.dma("sp", "dead", U(2)[0:8, 384:768], A["c_dead"])
                d_rel = Q.dma("sp", "rel", U(2)[0:32, 768:776], A["rel_bias"])
                d_lam = Q.dma("sp", "lam", U(2)[:, 776:1032], A["lambdas"].broadcast_to([P, 256]))
                d_mask = Q.dma("sp", "mask", U(8)[:, 0:1024], A["c_mask"])
                d_mask = cp(MASK[:, :, :].rearrange("p a b -> p (a b)"), U(8)[:, 0:1024], [d_mask])
                side(bias_g[0])
                mg = mem_side()
                side(mg)
            tq.append(rowed(U(0)[:, 1024 * j:1024 * j + 1024], bk, [t], 0.125))
            bk = unit()
            t = run(f"k{j}", AH, AL, True, bk)
            tk.append(rowed(U(1)[:, 1024 * j:1024 * j + 1024], bk, [t]))
            bk = unit()
            t = run(f"v{j}", AH, AL, False, bk)
            drain(bias_g[0])
            tv.append(coled(V[:, :, 512 * j:512 * j + 512], bk, [t] + lam_ready + bias_ready))
            if j == 0:
                while mg in sides:
                    pump()
                heads_go(0)

        heads_go(1)

        def head_norm(O, junk, after):
            n, d = O.shape[1], O.shape[2]
            t = act(junk, O.rearrange("p n d -> p (n d)"), ACT.Square, after=after)
            yield from rest(2)
            ss = stat(n)
            t = red(ss, junk.rearrange("p (n d) -> p n d", n=n), ALU.add, [t])
            r, t = rsqrt(ss, d, n, [t])
            yield from rest(4)
            h = n // 2
            res = [tt(O[:, c, :], O[:, c, :], r[:, c].unsqueeze(2).broadcast_to([P, h, d]), ALU.mult, [t])
                   for c in (slice(0, h), slice(h, n))]
            norm_done.extend(res)
            return res

        norm_done = []

        tf, tqh, ti, tg = [None, None], [], [], []
        KK, BB, QH, EE = U(4), U(5), U(6), U(7)

        def f_side(j, t):
            cs = slice(1024 * j, 1024 * j + 1024)
            yield
            t = act(KK[:, cs], KK[:, cs], ACT.Sigmoid, after=[t])
            yield
            fs = []
            for h in range(4):
                hs = slice(1024 * j + T * h, 1024 * j + T * h + T)
                c = 4 * j + h
                fs.append(ts(KK[:, hs], KK[:, hs], oml[:, c:c + 1], lb[:, c:c + 1], ALU.mult, ALU.add, [t] + lb_ready))
            t = ts(BB[:, cs], KK[:, cs], 2.0 ** -62, None, ALU.max, after=fs)
            yield
            t = act(BB[:, cs], BB[:, cs], ACT.Ln, after=[t])
            t2 = ts(KK[:, cs], KK[:, cs], -1.0, 1.0, ALU.mult, ALU.add, fs)
            yield
            yield
            sc = []
            for h in range(2):
                hs = slice(1024 * j + 512 * h, 1024 * j + 512 * h + 512)
                sc.append(Q.op("dve", lambda g, hs=hs: g.tensor_tensor_scan(BB[:, hs], SM[:, :], BB[:, hs], 0.0,
                                                                            ALU.mult, ALU.add), [t, t_sm]))
            tf[j] = [t2] + sc

        held = set()

        def levels(todo, q, k, b, E, dst, cross, nu, kc, banks, escale, after, e_free, cross_free, cdone, pace):
            blk = lambda ap, u, c, s: ap[:, (u * kc + c) * T + s * P:(u * kc + c) * T + s * P + P]
            e_busy = list(e_free)

            def products(lhs, rhs, need):
                pos = 0
                toks = {}
                for u in range(nu):
                    for s in range(2):
                        bk, o = banks[pos // 4], (pos % 4) * P
                        for c in range(kc):
                            t = mm(PS[:, bk, o:o + P], blk(lhs, u, c, s), blk(rhs, u, c, s), pos % 4 == 0 and c == 0,
                                   c == kc - 1, need + free[bk], inc=pos % 4 == 3 and c == kc - 1)
                        if t:
                            toks[bk] = t
                        pos += 1
                return toks

            def pick(toks, mi):
                for n, bk in enumerate(banks):
                    d = dst[:, 512 * n:512 * n + 512].rearrange("p (r t) -> p r t", t=P)
                    m = MASK[:, mi:mi + 1, :].broadcast_to([P, 4, P])
                    src = PS[:, bk, :].rearrange("p (r t) -> p r t", t=P)
                    t = Q.op("dve", lambda g, d=d, m=m, src=src: g.copy_predicated(d, m, src),
                             [toks[bk], d_mask] + list(after))
                    free[bk] = [t]
                    cdone.append(t)

            for L in todo:
                if L == 0:
                    while held & set(banks):
                        yield
                    held.update(banks)
                    toks = products(k, q, list(after))
                    yield from rest(pace)
                    pick(toks, 0)
                    held.difference_update(banks)
                    continue
                w = lambda ap: ap.rearrange("p (n t) -> p n t", t=2 * L)
                bv, ev, qv, kv = w(b), w(E), w(q), w(k)
                n = bv.shape[1]
                aft = list(after) + e_busy
                ref = bv[:, :, L - 1:L].broadcast_to([P, n, L])
                t1 = tt(ev[:, :, 0:L], ref, bv[:, :, 0:L], ALU.subtract, aft)
                if L < 64:
                    t0 = tt(ev[:, :, L:2 * L], bv[:, :, L:2 * L], ref, ALU.subtract, aft)
                elif L == 64:
                    t0 = cp(ev[:, :, L:2 * L], bv[:, :, L:2 * L], aft)
                else:
                    t2 = cp(ev[:, :, P:T], bv[:, :, P:T], aft)
                    t0 = tt(ev[:, :, P + 64:T], ev[:, :, P + 64:T], bv[:, :, P + 63:P + 64].broadcast_to([P, n, 64]),
                            ALU.add, [t2])
                    t1 = tt(ev[:, :, 0:64], ev[:, :, 0:64], bv[:, :, 63:64].broadcast_to([P, n, 64]), ALU.add, [t1])
                yield from rest(pace)
                t = act(E, E, ACT.Exp, scale=escale, after=[t0, t1])
                yield from rest(pace)
                t0 = tt(ev[:, :, L:2 * L], ev[:, :, L:2 * L], qv[:, :, L:2 * L], ALU.mult, [t])
                t1 = tt(ev[:, :, 0:L], ev[:, :, 0:L], kv[:, :, 0:L], ALU.mult, [t])
                yield from rest(pace + 1)
                while held & set(banks):
                    yield
                held.update(banks)
                if L < P:
                    toks = products(E, E, [t0, t1])
                    e_busy = list(toks.values())
                    yield from rest(pace)
                    pick(toks, 1 + LEVELS.index(L))
                    held.difference_update(banks)
                    continue
                bk = banks[0]
                for u in range(nu):
                    for c in range(kc):
                        t = mm(PS[:, bk, u * P:u * P + P], blk(E, u, c, 0), blk(E, u, c, 1), u == 0 and c == 0,
                               c == kc - 1, [t0, t1] + free[bk], inc=u == nu - 1 and c == kc - 1)
                e_busy = [t]
                yield
                t = cp(cross, PS[:, bk, 0:nu * P], [t] + list(cross_free))
                free[bk] = [t]
                cdone.append(t)
                held.difference_update(banks)

        att, att_x = U(0), SP4
        lev_done, lev_half, att_zero = [], [[], []], []

        def hg_levels(j, part):
            while len(oda) < 8 or tf[j] is None:
                yield
            if not att_zero:
                att_zero.append(Q.op("pool", lambda g: g.memset(att, 0.0), [oda, s_free[0], s_free[1]]))
            yield from rest(6 * part + 1)
            cs = slice(1024 * j, 1024 * j + 1024)
            done = lev_half[j]
            yield from levels(([128, 64, 32, 16], [0, 1, 2, 4, 8])[part], QH[:, cs], KK[:, cs], BB[:, cs],
                              (EE, U(8))[part][:, cs], att[:, cs], att_x[:, 512 * j:512 * j + 512],
                              4, 1, [4 + 2 * j, 5 + 2 * j], 1.0, [tqh[j], tf[j]] + att_zero,
                              [oda, s_free[0], s_free[1]], [a_free[0], a_free[1]], done, 2)
            lev_done.extend(done)

        da_normed = []

        def da_norm():
            while len(oda) < 8:
                yield
            for c in range(2):
                da_normed.extend((yield from head_norm(
                    U(3)[:, 1024 * c:1024 * c + 1024].rearrange("p (n d) -> p n d", d=P),
                    U(1)[:, 1024 * c:1024 * c + 1024], oda)))

        lev = [[hg_levels(j, part) for part in range(2)] for j in range(2)]
        for j in range(2):
            bk = unit()
            t = run(f"f{j}", AH, AL, True, bk)
            t = rowed(KK[:, 1024 * j:1024 * j + 1024], bk, [t] + mem_ready)
            side(f_side(j, t))
            bk = unit()
            t = run(f"qh{j}", AH, AL, True, bk)
            tqh.append(rowed(QH[:, 1024 * j:1024 * j + 1024], bk, [t] + mem_ready))
            for s in lev[j]:
                side(s)
        dn = da_norm()

        VI = U(2).rearrange("p (b n) -> p b n", b=2)
        for j in range(2):
            bk = unit()
            t = run(f"i{j}", AH, AL, False, bk)
            for h in heads:
                drain(h)
            ti.append(coled(VI[:, :, 512 * j:512 * j + 512], bk, [t] + oda))
            if j == 0:
                side(dn)
        GT = U(1)
        mix_ready, a_free_tok = [None] * 16, []
        hg_end, hg_normed = [], []

        def hg_out(half):
            while any(g in sides for g in lev[half]):
                yield
            av = att.rearrange("p (h b t) -> p h b t", h=8, b=2)
            OHG = U(4)[:, 1024 * half:1024 * half + 1024].rearrange("p (b h d) -> p b h d", b=2, h=4)
            o_t = []
            for blk in range(2):
                b = 4 + 2 * half + blk
                for hh in range(4):
                    h = 4 * half + hh
                    o = PS[:, b, hh * P:hh * P + P]
                    vs = slice(h * P, h * P + P)
                    t = mm(o, av[:, h, blk, :], VI[:, blk, vs], hh == 0, blk == 0, lev_half[half] + ti + free[b],
                           inc=hh == 3 and blk == 0)
                    if blk:
                        t = mm(o, att_x[:, h * P:h * P + P], VI[:, 0, vs], False, True, inc=hh == 3)
                hg_end.append(t)
                yield
                t2 = cp(OHG[:, blk, :, :], PS[:, b, :].rearrange("p (h d) -> p h d", h=4), [t] + lev_half[half])
                free[b] = [t2]
                o_t.append(t2)
            yield
            normed = yield from head_norm(
                U(4)[:, 1024 * half:1024 * half + 1024].rearrange("p (n d) -> p n d", d=P),
                U(6)[:, 1024 * half:1024 * half + 1024], o_t + lev_half[half])
            hg_normed.extend(normed)
            yield
            while len(tg) < 2 or not a_free_tok:
                yield
            if half == 0:
                yield from da_out()
            for i in range(2 * half, 2 * half + 2):
                b = 4 + 2 * half + i % 2
                for c in range(2):
                    for blk in range(2):
                        t = tr(PS[:, b, c * T + blk * P:c * T + blk * P + P], OHG[:, blk, 2 * (i % 2) + c, :],
                               normed + free[b], inc=c == 1 and blk == 1)
                yield
                tmp = U(5)[:, 512 * i:512 * i + 512]
                t = stt(tmp, PS[:, b, :], gcol("hg_onorm_g"), GT[:, 512 * i:512 * i + 512], ALU.mult, ALU.mult,
                        [t] + tg + lev_half[half])
                free[b] = [t]
                yield
                hl = slice(8 + 2 * i, 10 + 2 * i)
                mix_ready[8 + 2 * i] = mix_ready[9 + 2 * i] = split(
                    tmp.rearrange("p (c t) -> p c t", c=2), AH[:, hl, :], AL[:, hl, :], None, [t] + a_free_tok)

        for half in range(2):
            side(hg_out(half))
        for j in range(2):
            bk = unit()
            t = run(f"g{j}", AH, AL, True, bk)
            gs_ = GT[:, 1024 * j:1024 * j + 1024]
            if j == 0:
                drain(dn)
            tg.append(act(gs_, gs_, ACT.Silu, after=[rowed(gs_, bk, [t] + oda + norm_done)]))
        a_free_tok.append(pe_done[-1])
        subg = stat(1)
        t_sub = ts(subg, gcol("da_subln_g"), 1.0 - LAM0, None, ALU.mult, after=[d_gc])

        def da_out():
            o = U(3).rearrange("p (b h d) -> p b h d", b=2, h=8)
            for i in range(4):
                b = 4 + i % 2
                for c in range(2):
                    for blk in range(2):
                        t = tr(PS[:, b, c * T + blk * P:c * T + blk * P + P], o[:, blk, 2 * i + c, :],
                               da_normed + free[b], inc=c == 1 and blk == 1)
                yield
                hl = slice(2 * i, 2 * i + 2)
                t = split(PS[:, b, :].rearrange("p (c t) -> p c t", c=2), AH[:, hl, :], AL[:, hl, :], subg,
                          [t, t_sub] + a_free_tok)
                free[b] = [t]
                mix_ready[2 * i] = mix_ready[2 * i + 1] = t

        KT, VX = U(6)[:, 0:1024], U(6)[:, 1024:2048].rearrange("p (b n) -> p b n", b=2)
        bk = unit()
        t = run("ckv0", BH, BL, True, bk, mem_ready)
        for s in lev[0] + lev[1]:
            drain(s)
        while not hg_normed:
            pump()
        tkx = act(KT, flat(bk), after=[t] + lev_done + hg_normed)
        free[bk[0]] = free[bk[1]] = [tkx]

        M23 = U(2, 2).rearrange("p (b d) -> p b d", b=2)
        d_gb = gain_rows("mix_post_g", lev_done)
        SQ = [SP4[:, 0:512], SP4[:, 512:1024]]
        ssq, mt = token_groups([f"wo{c}" for c in range(4)], AH, AL, M23, mix_ready, d_gb, lambda: hg_end + mix_ready, SQ)
        xt = post_norm(M23, mt, ssq)
        xr = norm_t(X, xt, AH, AL, GOFF["cross_pre_g"], al, [pe_done[groups["wo3"][-1]]])
        rg = start_row(X, xt, SP4, 7)

        QX, PX, PT = U(7)[:, 0:1024], U(0).rearrange("p (n k) -> p n k", k=T), U(1)
        bk = unit()
        t = run("cq", AH, AL, True, bk, (), xr)
        drain(rg)
        t = rowed(QX, bk, [t] + norm_done, float(P) ** -0.5)
        t_qx, pts = t, []

        def cross():
            yield
            sc, ex = [], []
            for h in range(4):
                for blk in range(2):
                    u = mm(PS[:, 4 + h, blk * T:blk * T + T], hv(QX)[:, h, blk * P:blk * P + P], hv(KT)[:, h, :],
                           blk == 0, True, [t_qx, tkx] + free[4 + h], inc=blk == 1)
                sc.append(u)
            yield
            nm, l, rl = stat(8), stat(8), stat(8)
            svs = [PS[:, 4 + h, :].rearrange("p (b k) -> p b k", b=2) for h in range(4)]
            mx = [red(nm[:, 2 * h:2 * h + 2], svs[h], ALU.max, [sc[h]], negate=True) for h in range(4)]
            yield
            for h in range(4):
                for blk in range(2):
                    n = 2 * h + blk
                    ex.append(act(PX[:, n, :], svs[h][:, blk, :], ACT.Exp, bias=nm[:, n:n + 1], accum=l[:, n:n + 1],
                                  after=[mx[h]] + hg_end))
                free[4 + h] = [ex[-1]]
            yield
            yield
            t = Q.op("dve", lambda g: g.reciprocal(rl, l), ex)
            pn = [tt(PX[:, 2 * h:2 * h + 2, :], PX[:, 2 * h:2 * h + 2, :],
                     rl[:, 2 * h:2 * h + 2].unsqueeze(2).broadcast_to([P, 2, T]), ALU.mult, [t]) for h in range(4)]
            yield
            yield
            for h in range(4):
                for kb in range(2):
                    for blk in range(2):
                        u = tr(PS[:, 4 + h, kb * T + blk * P:kb * T + blk * P + P],
                               PX[:, 2 * h + blk, kb * P:kb * P + P], [pn[h]] + free[4 + h], inc=kb == 1 and blk == 1)
                e = act(PT[:, 512 * h:512 * h + 512], PS[:, 4 + h, :], after=[u] + mix_ready)
                free[4 + h] = [e]
                pts.append(e)

        side(cross())
        bk = unit()
        u = run("ckv1", BH, BL, False, bk)
        tvx = act(VX, PS[:, bk[0]:bk[1] + 1, :], after=[u] + lev_done)
        free[bk[0]] = free[bk[1]] = [tvx]
        drain()
        oxr = []
        for i in range(2):
            for c in range(2):
                h = 2 * i + c
                for kb in range(2):
                    u = mm(PS[:, 4 + i, c * T:c * T + T], VX[:, kb, h * P:h * P + P],
                           PT[:, 512 * h + kb * T:512 * h + kb * T + T], c == 0 and kb == 0, kb == 1,
                           [pts[h], tvx] + free[4 + i], inc=c == 1 and kb == 1)
            e = split(PS[:, 4 + i, :].rearrange("p (c t) -> p c t", c=2), BH[:, 2 * i:2 * i + 2, :],
                      BL[:, 2 * i:2 * i + 2, :], None, [u, pe_done[groups["ckv1"][-1]]])
            free[4 + i] = [e]
            oxr += [e, e]
        d_gb = gain_rows("cross_post_g", mt)
        ssq, mt = token_groups([f"co{c}" for c in range(4)], BH, BL, M23, oxr, d_gb, lambda: row_ready, SQ)
        xt = post_norm(M23, mt, ssq)
        AH, AL, BH, BL = BH, BL, AH, AL
        xr = norm_t(X, xt, BH, BL, GOFF["ffn_pre_g"], al, [pe_done[groups["cq"][-1]]])
        rg = start_row(X, xt, SP4, 7)

        def ffn(tag, inH, inL, hidH, hidL, in_ready, post, x_toks, hid_free, rg, old_mt):
            SG = [U(0)[:, 0:1024], U(0)[:, 1024:2048]]
            SU = [U(1)[:, 0:1024], U(1)[:, 1024:2048]]
            Fa = M23
            s_free = [list(x_toks), list(x_toks)]
            d = gain_rows(post, old_mt)
            ssq = stat(8).rearrange("p (b c) -> p b c", b=2)
            mt, acc, n = [], [None] * 4, 0
            for p, (a, b) in enumerate(PARTS):
                hid = []
                for j in range(a, b):
                    g = unit(4)
                    tg_ = run(f"{tag}g{j}", inH, inL, True, g, (), in_ready if j == 0 else None)
                    drain(rg)
                    s, v = SG[n % 2], SU[n % 2]
                    tg_ = rowed(s, g, [tg_] + s_free[n % 2])
                    tg_ = act(s, s, ACT.Silu, after=[tg_])
                    u = unit(4)
                    tu = run(f"{tag}u{j}", inH, inL, True, u)
                    tu = rowed(v, u, [tu] + s_free[n % 2])
                    t = tt(s, s, v, ALU.mult, [tg_, tu])
                    hl = slice(4 * (j - a), 4 * (j - a) + 4)
                    t = split(s.rearrange("p (c t) -> p c t", c=4), hidH[:, hl, :], hidL[:, hl, :], None,
                              [t] + list(hid_free))
                    s_free[n % 2] = [t]
                    hid += [t] * 4
                    n += 1
                for c in range(4):
                    bk = unit(4)
                    t = run(f"{tag}o{p}_{c}", hidH, hidL, False, bk, (), hid if c == 0 else None)
                    cs = slice(512 * c, 512 * c + 512)
                    src = PS[:, bk[0]:bk[1] + 1, :]
                    if p == 0:
                        t = act(Fa[:, :, cs], src, after=[t] + list(x_toks))
                    elif p == 1:
                        t = tt(Fa[:, :, cs], src, Fa[:, :, cs], ALU.add, [t, acc[c]])
                    else:
                        for k in range(2):
                            u = tt(Fa[:, k, cs], PS[:, bk[k], :], Fa[:, k, cs], ALU.add, [t, acc[c]])
                            mt.append(act(SQ[k], Fa[:, k, cs], ACT.Square, accum=ssq[:, k, c:c + 1],
                                          after=[u] + row_ready + mt[-2:]))
                        t = u
                        gain = lambda c=c, cs=cs, u=mt[-1]: tt(
                            Fa[:, :, cs], Fa[:, :, cs], GB[:, :, cs].broadcast_to([P, 2, 512]), ALU.mult,
                            [u, d], "pool" if c < 3 else "dve")
                        if c < 3:
                            mt.append(gain())
                    free[bk[0]] = free[bk[1]] = [t]
                    acc[c] = t
                hid_free = [pe_done[-1]]
            return post_norm(Fa, mt, ssq, gain), mt

        xt, mt = ffn("F", BH, BL, AH, AL, xr, "ffn_post_g", sum(xt, []), [pe_done[groups["co3"][-1]]], rg, mt)

        xr = norm_t(X, xt, BH, BL, GOFF["norm_mix_pre_2"], al, [pe_done[groups["Fu10"][-1]]])
        rg = start_row(X, xt, SP4, 7)
        old = sum(xt, []) + mt
        WP = U(8).rearrange("p (g k n) -> p g k n", g=4, k=2)
        d_wp = Q.dma("pool", "wp", WP, A["w_pool_2"][0].rearrange("g (k p) n -> p g k n", p=P), mt)
        GU = U(6)[0:16, 0:1024]
        d_gu = Q.dma("pool", "gu", GU, A["w_gate_up_2"][0], old)
        tk, tq = [], []

        def k_group(j, ready):
            bk = unit()
            t = run(f"K{j}", BH, BL, True, bk, (), ready)
            drain(rg)
            tk.append(rowed(U(1)[:, 1024 * j:1024 * j + 1024], bk, [t] + old))

        k_group(0, xr)
        bk = unit()
        t = run("LR", BH, BL, True, bk)
        GL = U(5)[0:16, 0:T]
        t_glr = tt(GL, PS[0:16, bk[0], 0:T], RR[0:16, 0, :], ALU.mult, [t] + old + row_ready)
        free[bk[0]] = [t_glr]
        row_read.append(t_glr)
        G2 = U(2)
        g_ready = [[], []]

        def gate_side():
            yield
            zt = []
            for c in range(8):
                u = mm(PS[:, 4 + c // 2, (c % 2) * T:(c % 2) * T + T], GU[:, c * P:c * P + P], GL,
                       c % 2 == 0, True, [t_glr, d_gu] + free[4 + c // 2], inc=c % 2 == 1)
                if c % 2:
                    zt.append(u)
            gu_free.append(u)
            yield from rest(2)
            for j in range(2):
                a, m = [], []
                for c in range(4 * j, 4 * j + 4):
                    z = PS[:, 4 + c // 2, (c % 2) * T:(c % 2) * T + T]
                    cs = slice(c * T, c * T + T)
                    m.append(ts(G2[:, cs], z, gcol("b_gate_2", c), 0.0, ALU.add, ALU.min, zt + old))
                yield from rest(3)
                for c in range(4 * j, 4 * j + 4):
                    z = PS[:, 4 + c // 2, (c % 2) * T:(c % 2) * T + T]
                    a.append(act(U(4)[:, c * T:c * T + T], z, ACT.Abs, bias=gcol("b_gate_2", c), after=m + old))
                    free[4 + c // 2] = [a[-1]]
                yield from rest(3)
                hs = slice(1024 * j, 1024 * j + 1024)
                t = act(U(4)[:, hs], U(4)[:, hs], ACT.Exp, scale=-1.0, after=a)
                yield from rest(3)
                t = act(U(4)[:, hs], U(4)[:, hs], ACT.Ln, bias=1.0, after=[t])
                yield from rest(4)
                t = tt(G2[:, hs], G2[:, hs], U(4)[:, hs], ALU.subtract, [t] + m)
                u4_free.append(t)
                for k in range(2):
                    ks = slice(1024 * j + 512 * k, 1024 * j + 512 * k + 512)
                    g_ready[j].append(Q.op("dve", lambda g, ks=ks: g.tensor_tensor_scan(
                        G2[:, ks], SM[:, :], G2[:, ks], 0.0, ALU.mult, ALU.add), [t]))
                yield

        u4_free, gu_free, lev_done = [], [], []
        gs = gate_side()
        side(gs)
        k_group(1, None)
        for j in range(2):
            bk = unit()
            t = run(f"Q{j}", BH, BL, True, bk)
            tq.append(rowed(U(0)[:, 1024 * j:1024 * j + 1024], bk, [t] + old, 0.0625))
        ATT2 = SP4
        AX2 = SM
        att_zero = []

        def gla_levels(j):
            while gs in sides:
                yield
            if not att_zero:
                att_zero.append(Q.op("pool", lambda g: g.memset(ATT2, 0.0), old + row_ready))
            yield from rest(5 * j)
            cs = slice(1024 * j, 1024 * j + 1024)
            yield from levels([0, 1, 2, 4, 8, 16, 32, 64, 128], U(0)[:, cs], U(1)[:, cs], G2[:, cs], U(3)[:, cs],
                              ATT2[:, 512 * j:512 * j + 512], AX2[:, 256 * j:256 * j + 256], 2, 2, [6 + j], 0.0625,
                              tq + tk + g_ready[j] + att_zero, old, g_ready, lev_done, 2)

        PP, S0, S1 = U(4), U(5), U(7)
        tp = []
        lev = [gla_levels(0), gla_levels(1)]
        for s in lev:
            side(s)
        for j in range(2):
            bk = unit()
            t = run(f"P{j}", BH, BL, True, bk)
            drain(gs)
            tp.append(rowed(PP[:, 1024 * j:1024 * j + 1024], bk, [t] + u4_free))
        pool_ready, pool_end = [], []

        def pool_side():
            pv, s0, s1 = hv(PP), hv(S0), hv(S1)
            src, prev = pv, tp + old + gu_free
            bufs = [s0, s1, s0, s1]
            res = []
            for g, w in enumerate((2, 4, 8, 16)):
                sh, c0, dst = w // 2, 2 * g, bufs[g]
                done = []
                for c in range(c0, 8, 2):
                    cs = slice(c, c + 2)
                    done.append(tt(dst[:, cs, sh:T], src[:, cs, sh:T], src[:, cs, 0:T - sh], ALU.add, prev, "pool"))
                    done.append(cp(dst[:, cs, 0:sh], src[:, cs, 0:sh], prev))
                    yield
                src, prev = dst, done
                res.append(done)
            tmp = stat(32).rearrange("p (c t) -> p c t", c=2)
            early = EYE[:, 256:320]
            wt = []
            end = []
            for g, w in enumerate((2, 4, 8, 16)):
                s, cs = bufs[g], slice(2 * g, 2 * g + 2)
                cnt = early[:, 16 * g:16 * g + 16].unsqueeze(1).broadcast_to([P, 2, 16])
                a = tt(tmp, s[:, cs, 0:16], cnt, ALU.mult, res[g] + prev + end)
                b = stt(s[:, cs, :], s[:, cs, :], 1.0 / w, pv[:, cs, :], ALU.mult, ALU.subtract, [a])
                b = tt(s[:, cs, 0:16], tmp, pv[:, cs, 0:16], ALU.subtract, [b])
                end = [b]
                wt.append(b)
                yield
            yield from rest(3)
            for g in range(4):
                b, s = 4 + g % 2, bufs[g]
                for c in range(2):
                    for kc in range(2):
                        t = mm(PS[:, b, c * T:c * T + T], WP[:, g, kc, c * P:c * P + P], s[:, 2 * g + kc, :],
                               c == 0 and kc == 0, kc == 1, [wt[g], d_wp] + free[b], inc=c == 1 and kc == 1)
                yield
                pool_end.append(t)
                t = splits([(PS[:, b, c * T:c * T + T], AH[:, 2 * g + c, :], AL[:, 2 * g + c, :],
                             gcol("pool_scale_2", 2 * g + c)) for c in range(2)], [t, pe_done[groups["Fo2_3"][-1]]])
                free[b] = [t]
                pool_ready.append(t)

        ps_ = pool_side()
        side(ps_)
        T0 = U(6, 2)
        tt0 = []
        for j in range(4):
            bk = unit()
            t = run(f"G0{j}", BH, BL, True, bk)
            if j == 2:
                drain(ps_)
            t = rowed(T0[:, 1024 * j:1024 * j + 1024], bk, [t] + gu_free + pool_end)
            for c in range(4):
                z = T0[:, 1024 * j + T * c:1024 * j + T * c + T]
                e = act(z, z, ACT.Sigmoid, bias=gcol("b_branch_gates_2", 4 * j + c), after=[t])
            tt0.append(e)
        for j in range(4):
            bk = unit()
            t = run(f"ya{j}", AH, AL, True, bk, (), [pool_ready[k // 2] for k in range(8)] if j == 0 else None)
            ts_ = slice(1024 * j, 1024 * j + 1024)
            tt0[j] = tt(T0[:, ts_], T0[:, ts_], flat(bk), ALU.mult, [t, tt0[j]])
            free[bk[0]] = free[bk[1]] = [tt0[j]]
        for s in lev:
            drain(s)
        V2 = U(0, 2).rearrange("p (b n) -> p b n", b=2)
        tv = []
        for j in range(4):
            bk = unit()
            t = run(f"V{j}", BH, BL, False, bk)
            tv.append(coled(V2[:, :, 512 * j:512 * j + 512], bk, [t] + lev_done))
        O2 = U(4, 2).rearrange("p (b h d) -> p b h d", b=2, h=4)
        tr_, ox_ready, v_free = [], [], []

        def gla_out():
            ot = []
            for blk in range(2):
                for h in range(4):
                    vs = slice(512 * h, 512 * h + 512)
                    o = PS[:, 4 + h, :]
                    at = lambda hh, s: ATT2[:, (2 * hh + s) * P:(2 * hh + s) * P + P]
                    t = mm(o, at(h, blk), V2[:, blk, vs], True, blk == 0, lev_done + tv + free[4 + h], inc=blk == 0)
                    if blk:
                        t = mm(o, AX2[:, h * P:h * P + P], V2[:, 0, vs], False, True, inc=True)
                    v_free.append(t)
                    if h % 2:
                        e = act(O2[:, blk, h, :], o, after=[t] + pool_end + pool_ready)
                    else:
                        e = cp(O2[:, blk, h, :], o, [t] + pool_end + pool_ready)
                    free[4 + h] = [e]
                    ot.append(e)
                yield
            ss = stat(8)
            sq = []
            for n in range(8):
                sq.append(act(U(8)[:, 512 * (n % 2):512 * (n % 2) + 512], O2[:, n // 4, n % 4, :], ACT.Square,
                              accum=ss[:, n:n + 1], after=ot + pool_end + sq[-1:]))
                if n % 2:
                    yield
            r, t = rsqrt(ss, 512, 8, sq)
            yield
            yield
            of = U(4, 2).rearrange("p (n d) -> p n d", d=512)
            sc = []
            for n in range(2):
                sc.append(tt(of[:, 4 * n:4 * n + 4, :], of[:, 4 * n:4 * n + 4, :],
                             r[:, 4 * n:4 * n + 4].unsqueeze(2).broadcast_to([P, 4, 512]), ALU.mult, [t]))
                yield
            yield
            while len(tr_) < 4:
                yield
            buf_free = [sq, sq]
            for i in range(8):
                b = 4 + i % 4
                for c in range(2):
                    cc = 2 * i + c
                    for blk in range(2):
                        t = tr(PS[:, b, c * T + blk * P:c * T + blk * P + P],
                               O2[:, blk, cc // 4, (cc % 4) * P:(cc % 4) * P + P], sc + free[b], inc=c == 1 and blk == 1)
                yield
                tmp = U(8)[:, 512 * (i % 2):512 * (i % 2) + 512]
                e = []
                for c in range(2):
                    cc = 2 * i + c
                    e.append(stt(tmp[:, c * T:c * T + T], PS[:, b, c * T:c * T + T], gcol("gla_norm_2", cc % 4),
                                 RS[:, cc * T:cc * T + T], ALU.mult, ALU.mult, [t] + tr_ + buf_free[i % 2]))
                free[b] = e
                yield
                hl = slice(2 * i, 2 * i + 2)
                t = split(tmp.rearrange("p (c t) -> p c t", c=2), AH[:, hl, :], AL[:, hl, :], None,
                          e + [pe_done[groups["ya3"][-1]]])
                buf_free[i % 2] = [t]
                ox_ready.append(t)

        go = gla_out()
        side(go)
        RS = U(2, 2)
        for j in range(4):
            bk = unit()
            t = run(f"R{j}", BH, BL, True, bk)
            rs = RS[:, 1024 * j:1024 * j + 1024]
            tr_.append(act(rs, rs, ACT.Silu, after=[rowed(rs, bk, [t] + lev_done)]))
        G1 = U(0, 2)
        tg1 = []
        for j in range(4):
            bk = unit()
            t = run(f"G1{j}", BH, BL, True, bk)
            t = rowed(G1[:, 1024 * j:1024 * j + 1024], bk, [t] + v_free)
            for c in range(4):
                z = G1[:, 1024 * j + T * c:1024 * j + T * c + T]
                e = act(z, z, ACT.Sigmoid, bias=gcol("b_branch_gates_2", 16 + 4 * j + c), after=[t])
            tg1.append(e)
        drain()
        hb_free = [pe_done[-1]]
        mr = []
        for j in range(4):
            bk = unit()
            t = run(f"yb{j}", AH, AL, True, bk, (), [ox_ready[k // 2] for k in range(16)] if j == 0 else None)
            ts_ = slice(1024 * j, 1024 * j + 1024)
            t = tt(G1[:, ts_], G1[:, ts_], flat(bk), ALU.mult, [t, tg1[j]])
            free[bk[0]] = free[bk[1]] = [t]
            t = tt(G1[:, ts_], G1[:, ts_], T0[:, ts_], ALU.add, [t, tt0[j]])
            mr.append(split(G1[:, ts_].rearrange("p (c t) -> p c t", c=4), BH[:, 4 * j:4 * j + 4, :],
                            BL[:, 4 * j:4 * j + 4, :], None, [t] + hb_free))
        d_gb = gain_rows("norm_mix_post_2", ox_ready)
        ssq, mt = token_groups([f"W{c}" for c in range(4)], BH, BL, M23, [mr[k // 4] for k in range(16)], d_gb,
                               lambda: ox_ready + v_free, SQ)
        xt = post_norm(M23, mt, ssq)
        xr = norm_t(X, xt, AH, AL, GOFF["norm_ffn_pre_2"], al, [pe_done[groups["yb3"][-1]]])
        rg = start_row(X, xt, SP4, 7)
        xt, mt = ffn("H", AH, AL, BH, BL, xr, "norm_ffn_post_2", sum(xt, []), [pe_done[groups["W3"][-1]]], rg, mt)
        ov = out[0].rearrange("(b p) d -> p b d", p=P)
        ends = []
        for c in range(4):
            for b in range(2):
                hs = slice(512 * c, 512 * c + 512)
                ends.append(Q.dma("sp" if b else "act", f"out{c}{b}", ov[:, b, hs], X[:, b, hs], [xt[c][b]]))
        Q.wait("sp", ends)

        block = ctx.enter_context(nc.Block())

        @block.sync
        def _(g):
            Q.play("sp", g)

        @block.scalar
        def _(g):
            Q.play("act", g)

        @block.vector
        def _(g):
            Q.play("dve", g)

        @block.gpsimd
        def _(g):
            Q.play("pool", g)

        @block.tensor
        def _(g):
            Q.play("pe", g)


RAWS = ["x", "mem", "w_in", "w_out", "w_cq", "w_ckv", "w_co", "w_ffn_in", "w_ffn_out", "rel_bias", "w_in_2",
        "w_gate_up_2", "w_pool_2", "w_branch_a_2", "w_branch_b_2", "w_out_2", "w_ffn_gate_2", "w_ffn_up_2",
        "w_ffn_down_2", "mix_post_g", "cross_post_g", "ffn_post_g", "norm_mix_post_2", "norm_ffn_post_2"]


def kernel(**inputs):
    import concourse.bacc as bacc
    from concourse.bass_utils import run_bass_kernel_spmd

    f = {n: np.ascontiguousarray(a) for n, a in inputs.items()}
    arrays = {n: f[n] for n in RAWS}
    cols = []
    for n in GAINS:
        cols.append(f[n].reshape(-1, P).T)
    arrays["gains"] = np.ascontiguousarray(np.concatenate(cols, 1))
    arrays["lambdas"] = np.ascontiguousarray(np.concatenate(
        [f[n].reshape(1, 64) for n in ("lambda_q1", "lambda_k1", "lambda_q2", "lambda_k2")], 1))
    arrays.update(shape_constants())
    nc = bacc.Bacc("TRN2", target_bir_lowering=False, num_devices=1)
    A = {n: nc.dram_tensor("in_" + n, a.shape, mybir.dt.from_np(a.dtype), kind="ExternalInput").ap()
         for n, a in arrays.items()}
    out = nc.dram_tensor("out_x", (1, T, D), F32, kind="ExternalOutput").ap()
    scratch = nc.dram_tensor("scratch", (8, 384), F32, kind="Internal").ap()
    build(nc, A, out, scratch)
    r = run_bass_kernel_spmd(nc, [{"in_" + n: a for n, a in arrays.items()}], core_ids=[0])
    return r.results[0]["out_x"]
```
